# Optimizing a Trainium2 kernel written in Bass

```python
import jax
import jax.numpy as jnp
from jax import lax
import numpy as np
import math
import jax, jax.numpy as jnp

D_MODEL = 1024
BATCH = 1
SEQ = 512
DEPTH = 2

GRID_W = 64
CTX_LEN = 256
N_MIXERS = 2
N_CONV_LAYERS = (DEPTH + 1) // 2
N_ATTN_LAYERS = DEPTH // 2
CONV_WIDTH = 31
HEAD_DIM = 64
N_HEADS = D_MODEL // HEAD_DIM
N_KV_HEADS = N_HEADS // 4
GQA_GROUP = N_HEADS // N_KV_HEADS
QKV_DIM = (N_HEADS + 2 * N_KV_HEADS) * HEAD_DIM
WINDOW = 128
BLOCK = 128
ROPE_BASE = 10000.0
D_FF = 2816
FFN_CONV_WIDTH = 3
EPS = 1e-6
NEG = -1e30


def rmsnorm(x, g):
    xf = x.astype(jnp.float32)
    y = xf * lax.rsqrt(jnp.mean(xf * xf, axis=-1, keepdims=True) + EPS)
    return (y * g.astype(jnp.float32)).astype(x.dtype)

def layernorm(x, g, b):
    xf = x.astype(jnp.float32)
    mu = jnp.mean(xf, axis=-1, keepdims=True)
    var = jnp.mean(jnp.square(xf - mu), axis=-1, keepdims=True)
    y = (xf - mu) * lax.rsqrt(var + EPS)
    return (y * g.astype(jnp.float32) + b.astype(jnp.float32)).astype(x.dtype)

def modulate(x, shift, scale):
    return x * (1.0 + scale) + shift

def dwconv(x, w, b):
    k = w.shape[0]
    pad = (k - 1) // 2
    y = lax.conv_general_dilated(x, w[:, None, :], window_strides=(1,), padding=[(pad, pad)],
                                 dimension_numbers=('NWC', 'WIO', 'NWC'),
                                 feature_group_count=x.shape[-1])
    return y + b

def axial_rope_tables(seq_len):
    rows = seq_len // GRID_W
    row = jnp.broadcast_to(jnp.arange(rows)[:, None], (rows, GRID_W)).reshape(-1).astype(jnp.float32)
    col = jnp.broadcast_to(jnp.arange(GRID_W)[None, :], (rows, GRID_W)).reshape(-1).astype(jnp.float32)
    n_freq = HEAD_DIM // 4
    inv = ROPE_BASE ** (-jnp.arange(n_freq, dtype=jnp.float32) / n_freq)
    ang = jnp.concatenate([row[:, None] * inv, col[:, None] * inv], axis=-1)
    return jnp.cos(ang), jnp.sin(ang)

def apply_rope(x, cos, sin):
    xf = x.astype(jnp.float32)
    half = HEAD_DIM // 2
    x1, x2 = xf[..., :half], xf[..., half:]
    c = cos[None, :, None, :]
    s = sin[None, :, None, :]
    return jnp.concatenate([x1 * c - x2 * s, x2 * c + x1 * s], axis=-1).astype(x.dtype)

def conformer_conv(h, w_pw1, b_pw1, w_dw, b_dw, ln_g, ln_b, w_pw2, b_pw2):
    u = h @ w_pw1 + b_pw1
    a, g = jnp.split(u, 2, axis=-1)
    v = a * jax.nn.sigmoid(g)
    v = dwconv(v, w_dw, b_dw)
    v = jax.nn.silu(layernorm(v, ln_g, ln_b))
    return v @ w_pw2 + b_pw2

def conv_ffn(h, w_up, w_dw, b_dw, w_down):
    u = dwconv(h @ w_up, w_dw, b_dw)
    a, b = jnp.split(u, 2, axis=-1)
    return (jax.nn.silu(a) * b) @ w_down

def split_qkv(h, w_qkv):
    bsz, length, _ = h.shape
    qkv = h @ w_qkv
    q = qkv[..., :N_HEADS * HEAD_DIM].reshape(bsz, length, N_HEADS, HEAD_DIM)
    k = qkv[..., N_HEADS * HEAD_DIM:(N_HEADS + N_KV_HEADS) * HEAD_DIM].reshape(bsz, length, N_KV_HEADS, HEAD_DIM)
    v = qkv[..., (N_HEADS + N_KV_HEADS) * HEAD_DIM:].reshape(bsz, length, N_KV_HEADS, HEAD_DIM)
    return q, k, v

def sink_logits(sink, bsz, nq):
    s = sink.astype(jnp.float32).reshape(N_KV_HEADS, GQA_GROUP)[None, :, :, None, None]
    return jnp.broadcast_to(s, (bsz, N_KV_HEADS, GQA_GROUP, nq, 1))

def window_attention(h_lat, h_ctx, w_qkv, w_o, sink, cos, sin, with_ctx_out):
    bsz, seq, _ = h_lat.shape
    scale = HEAD_DIM ** -0.5
    qc, kc, vc = split_qkv(h_ctx, w_qkv)
    q, k, v = split_qkv(h_lat, w_qkv)
    q = apply_rope(q, cos, sin) * scale
    k = apply_rope(k, cos, sin)
    q = q.reshape(bsz, seq, N_KV_HEADS, GQA_GROUP, HEAD_DIM)
    nb = seq // BLOCK
    k_pad = jnp.pad(k, ((0, 0), (BLOCK, BLOCK), (0, 0), (0, 0)))
    v_pad = jnp.pad(v, ((0, 0), (BLOCK, BLOCK), (0, 0), (0, 0)))
    q_blocks = jnp.moveaxis(q.reshape(bsz, nb, BLOCK, N_KV_HEADS, GQA_GROUP, HEAD_DIM), 1, 0)
    s_sink_lat = sink_logits(sink, bsz, BLOCK)

    def block_fn(args):
        i, qb = args
        kb = lax.dynamic_slice_in_dim(k_pad, i * BLOCK, 3 * BLOCK, axis=1)
        vb = lax.dynamic_slice_in_dim(v_pad, i * BLOCK, 3 * BLOCK, axis=1)
        qpos = i * BLOCK + jnp.arange(BLOCK)
        kpos = i * BLOCK - BLOCK + jnp.arange(3 * BLOCK)
        valid = (jnp.abs(qpos[:, None] - kpos[None, :]) <= WINDOW) & (kpos[None, :] >= 0) & (kpos[None, :] < seq)
        s_band = jnp.einsum('bqhgd,bkhd->bhgqk', qb, kb).astype(jnp.float32)
        s_band = jnp.where(valid[None, None, None], s_band, NEG)
        s_ctx = jnp.einsum('bqhgd,bkhd->bhgqk', qb, kc).astype(jnp.float32)
        p = jax.nn.softmax(jnp.concatenate([s_band, s_ctx, s_sink_lat], axis=-1), axis=-1)
        p_band = p[..., :3 * BLOCK].astype(vb.dtype)
        p_ctx = p[..., 3 * BLOCK:3 * BLOCK + CTX_LEN].astype(vc.dtype)
        o = jnp.einsum('bhgqk,bkhd->bqhgd', p_band, vb) + jnp.einsum('bhgqk,bkhd->bqhgd', p_ctx, vc)
        return o

    o_blocks = lax.map(block_fn, (jnp.arange(nb), q_blocks))
    o_lat = jnp.moveaxis(o_blocks, 0, 1).reshape(bsz, seq, N_HEADS * HEAD_DIM) @ w_o

    o_ctx = None
    if with_ctx_out:
        qcs = (qc * scale).reshape(bsz, CTX_LEN, N_KV_HEADS, GQA_GROUP, HEAD_DIM)
        s_c = jnp.einsum('bqhgd,bkhd->bhgqk', qcs, kc).astype(jnp.float32)
        p_c = jax.nn.softmax(jnp.concatenate([s_c, sink_logits(sink, bsz, CTX_LEN)], axis=-1), axis=-1)
        oc = jnp.einsum('bhgqk,bkhd->bqhgd', p_c[..., :CTX_LEN].astype(vc.dtype), vc)
        o_ctx = oc.reshape(bsz, CTX_LEN, N_HEADS * HEAD_DIM) @ w_o
    return o_lat, o_ctx

def first_inputs(seed: int = 0) -> dict:
    key = jax.random.key(seed)
    ks = jax.random.split(key, 32)
    D = D_MODEL

    def nrm(k, shape, scale):
        return jax.random.normal(k, shape, jnp.float32) * scale

    return {
        'x': nrm(ks[0], (BATCH, SEQ, D), 1.0),
        'c': nrm(ks[1], (BATCH, D), 1.0),
        'ctx': nrm(ks[2], (BATCH, CTX_LEN, D), 1.0),
        'c_ctx': nrm(ks[3], (D,), 1.0),
        'ada_w': nrm(ks[4], (DEPTH, D, 6 * D), 0.02),
        'ada_b': nrm(ks[5], (DEPTH, 6 * D), 0.02),
        'norm1_g': 1.0 + nrm(ks[6], (DEPTH, D), 0.05),
        'norm2_g': 1.0 + nrm(ks[7], (DEPTH, D), 0.05),
        'final_g': 1.0 + nrm(ks[8], (D,), 0.05),
        'conv_w_pw1': nrm(ks[9], (N_CONV_LAYERS, D, 2 * D), D ** -0.5),
        'conv_b_pw1': nrm(ks[10], (N_CONV_LAYERS, 2 * D), 0.02),
        'conv_w_dw': nrm(ks[11], (N_CONV_LAYERS, CONV_WIDTH, D), CONV_WIDTH ** -0.5),
        'conv_b_dw': nrm(ks[12], (N_CONV_LAYERS, D), 0.02),
        'conv_ln_g': 1.0 + nrm(ks[13], (N_CONV_LAYERS, D), 0.05),
        'conv_ln_b': nrm(ks[14], (N_CONV_LAYERS, D), 0.02),
        'conv_w_pw2': nrm(ks[15], (N_CONV_LAYERS, D, D), D ** -0.5),
        'conv_b_pw2': nrm(ks[16], (N_CONV_LAYERS, D), 0.02),
        'attn_w_qkv': nrm(ks[17], (N_ATTN_LAYERS, D, QKV_DIM), D ** -0.5),
        'attn_w_o': nrm(ks[18], (N_ATTN_LAYERS, N_HEADS * HEAD_DIM, D), (N_HEADS * HEAD_DIM) ** -0.5),
        'attn_sink': nrm(ks[19], (N_ATTN_LAYERS, N_HEADS), 1.0),
        'ffn_w_up': nrm(ks[20], (DEPTH, D, 2 * D_FF), D ** -0.5),
        'ffn_w_dw': nrm(ks[21], (DEPTH, FFN_CONV_WIDTH, 2 * D_FF), FFN_CONV_WIDTH ** -0.5),
        'ffn_b_dw': nrm(ks[22], (DEPTH, 2 * D_FF), 0.02),
        'ffn_w_down': nrm(ks[23], (DEPTH, D_FF, D), D_FF ** -0.5),
    }

def first_block(x, c, ctx, c_ctx, ada_w, ada_b, norm1_g, norm2_g, final_g,
              conv_w_pw1, conv_b_pw1, conv_w_dw, conv_b_dw, conv_ln_g, conv_ln_b, conv_w_pw2, conv_b_pw2,
              attn_w_qkv, attn_w_o, attn_sink,
              ffn_w_up, ffn_w_dw, ffn_b_dw, ffn_w_down):
    cos, sin = axial_rope_tables(x.shape[1])
    sc = jax.nn.silu(c)
    scc = jax.nn.silu(c_ctx)
    h_lat = x
    h_ctx = ctx
    for i in range(DEPTH):
        last = i == DEPTH - 1
        mod_lat = (sc @ ada_w[i] + ada_b[i])[:, None, :]
        mod_ctx = scc @ ada_w[i] + ada_b[i]
        sh1, sc1, g1, sh2, sc2, g2 = jnp.split(mod_lat, 6, axis=-1)
        csh1, csc1, cg1, csh2, csc2, cg2 = jnp.split(mod_ctx, 6, axis=-1)
        a_lat = modulate(rmsnorm(h_lat, norm1_g[i]), sh1, sc1)
        j = i // N_MIXERS
        if i % N_MIXERS == 0:
            y_lat = conformer_conv(a_lat, conv_w_pw1[j], conv_b_pw1[j], conv_w_dw[j], conv_b_dw[j],
                                   conv_ln_g[j], conv_ln_b[j], conv_w_pw2[j], conv_b_pw2[j])
            if not last:
                a_ctx = modulate(rmsnorm(h_ctx, norm1_g[i]), csh1, csc1)
                y_ctx = conformer_conv(a_ctx, conv_w_pw1[j], conv_b_pw1[j], conv_w_dw[j], conv_b_dw[j],
                                       conv_ln_g[j], conv_ln_b[j], conv_w_pw2[j], conv_b_pw2[j])
        else:
            a_ctx = modulate(rmsnorm(h_ctx, norm1_g[i]), csh1, csc1)
            y_lat, y_ctx = window_attention(a_lat, a_ctx, attn_w_qkv[j], attn_w_o[j], attn_sink[j],
                                            cos, sin, not last)
        h_lat = h_lat + g1 * y_lat
        b_lat = modulate(rmsnorm(h_lat, norm2_g[i]), sh2, sc2)
        h_lat = h_lat + g2 * conv_ffn(b_lat, ffn_w_up[i], ffn_w_dw[i], ffn_b_dw[i], ffn_w_down[i])
        if not last:
            h_ctx = h_ctx + cg1 * y_ctx
            b_ctx = modulate(rmsnorm(h_ctx, norm2_g[i]), csh2, csc2)
            h_ctx = h_ctx + cg2 * conv_ffn(b_ctx, ffn_w_up[i], ffn_w_dw[i], ffn_b_dw[i], ffn_w_down[i])
    return rmsnorm(h_lat, final_g)


DEPTH_2 = 1

MIX_WIDTH = D_MODEL
ATTN_HEADS = 6
ATTN_KV_HEADS = 2
ATTN_GROUP = ATTN_HEADS // ATTN_KV_HEADS
ATTN_WIDTH = ATTN_HEADS * HEAD_DIM
ATTN_KV_WIDTH = ATTN_KV_HEADS * HEAD_DIM
BLOCK_Q = 128
N_BUCKETS = 32
MAX_EXACT = N_BUCKETS // 2
MAX_DISTANCE = WINDOW
RWKV_HEADS = 6
RWKV_HEAD_DIM = 64
RWKV_WIDTH = RWKV_HEADS * RWKV_HEAD_DIM
D_DECAY_LORA = 32
D_AAA_LORA = 32
D_MV_LORA = 16
D_GATE_LORA = 64
RWKV_SHIFT_COLS = 3 * RWKV_WIDTH + D_DECAY_LORA + D_AAA_LORA + D_GATE_LORA
MEM_TOKENS = 256
MEM_HEADS = 4
MEM_WIDTH = MIX_WIDTH - ATTN_WIDTH - RWKV_WIDTH
IN_BASE = ATTN_WIDTH + 2 * ATTN_KV_WIDTH + RWKV_SHIFT_COLS + MEM_WIDTH
CONV_WIDTH_2 = 3
GN_EPS = 64e-5
L2_EPS = 1e-12


def split_cols(t, sizes):
    return jnp.split(t, [int(c) for c in np.cumsum(sizes)[:-1]], axis=-1)

def rms_norm(x, g):
    xf = x.astype(jnp.float32)
    y = xf * lax.rsqrt(jnp.mean(xf * xf, axis=-1, keepdims=True) + EPS)
    return (y * g.astype(jnp.float32)).astype(x.dtype)

def token_shift(p, mu):
    prev = jnp.pad(p, ((0, 0), (1, 0), (0, 0)))[:, :-1]
    return p + mu * (prev - p)

def t5_causal_bucket(dist):
    is_small = dist < MAX_EXACT
    d = jnp.maximum(dist, 1).astype(jnp.float32)
    large = MAX_EXACT + (jnp.log(d / MAX_EXACT) / math.log(MAX_DISTANCE / MAX_EXACT)
                         * (N_BUCKETS - MAX_EXACT)).astype(jnp.int32)
    large = jnp.minimum(large, N_BUCKETS - 1)
    return jnp.where(is_small, dist, large)

def sliding_window_attention(q, k, v, sinks, rel_bias):
    b, s = q.shape[0], q.shape[1]
    nb = s // BLOCK_Q
    qb = q.reshape(b, nb, BLOCK_Q, ATTN_KV_HEADS, ATTN_GROUP, HEAD_DIM)

    def band(t):
        tb = t.reshape(b, nb, BLOCK_Q, ATTN_KV_HEADS, HEAD_DIM)
        prev = jnp.concatenate([jnp.zeros_like(tb[:, :1]), tb[:, :-1]], axis=1)
        return jnp.concatenate([prev, tb], axis=2)

    kw, vw = band(k), band(v)
    logits = jnp.einsum('bnqhgd,bnkhd->bnhgqk', qb, kw,
                        preferred_element_type=jnp.float32) * (HEAD_DIM ** -0.5)
    qi = jnp.arange(BLOCK_Q)[:, None]
    kj = jnp.arange(2 * BLOCK_Q)[None, :]
    dist = qi + BLOCK_Q - kj
    in_band = (dist >= 0) & (dist < WINDOW)
    key_pos = jnp.arange(nb)[:, None, None] * BLOCK_Q - BLOCK_Q + kj[None]
    valid = in_band[None] & (key_pos >= 0)
    bucket = t5_causal_bucket(jnp.maximum(dist, 0))
    bias = rel_bias.astype(jnp.float32)[bucket]
    bias = bias.transpose(2, 0, 1).reshape(ATTN_KV_HEADS, ATTN_GROUP, BLOCK_Q, 2 * BLOCK_Q)
    logits = jnp.where(valid[None, :, None, None], logits + bias, -jnp.inf)
    sink = sinks.astype(jnp.float32).reshape(ATTN_KV_HEADS, ATTN_GROUP)[None, None, :, :, None, None]
    m = jnp.maximum(jnp.max(logits, axis=-1, keepdims=True), sink)
    e = jnp.exp(logits - m)
    p = e / (jnp.sum(e, axis=-1, keepdims=True) + jnp.exp(sink - m))
    out = jnp.einsum('bnhgqk,bnkhd->bnqhgd', p.astype(v.dtype), vw)
    return out.reshape(b, s, ATTN_WIDTH)

def rwkv7_scan(r, w, k, v, a, bvec):
    bsz = r.shape[0]
    decay = jnp.exp(-jnp.exp(w))

    def step(state, inp):
        r_t, d_t, k_t, v_t, a_t, b_t = inp
        sa = jnp.einsum('bhvk,bhk->bhv', state, a_t)
        state = (state * d_t[:, :, None, :] + sa[..., None] * b_t[:, :, None, :]
                 + v_t[..., None] * k_t[:, :, None, :])
        return state, jnp.einsum('bhvk,bhk->bhv', state, r_t)

    xs = tuple(jnp.moveaxis(t, 1, 0) for t in (r, decay, k, v, a, bvec))
    s0 = jnp.zeros((bsz, RWKV_HEADS, RWKV_HEAD_DIM, RWKV_HEAD_DIM), jnp.float32)
    _, y = lax.scan(step, s0, xs)
    return jnp.moveaxis(y, 0, 1)

def rwkv7_mixer(pb, value_residual, w0, w2, a0, a2, g2, k_k, k_a, r_k, ln_w, ln_b):
    out_dtype = pb.dtype
    f32 = lambda t: t.astype(jnp.float32)
    r, k, v, wd, ad, gd = split_cols(f32(pb), [RWKV_WIDTH, RWKV_WIDTH, RWKV_WIDTH,
                                               D_DECAY_LORA, D_AAA_LORA, D_GATE_LORA])
    w = -jax.nn.softplus(-(f32(w0) + jnp.tanh(wd) @ f32(w2))) - 0.5
    a = jax.nn.sigmoid(f32(a0) + ad @ f32(a2))
    g = jax.nn.sigmoid(gd) @ f32(g2)
    if value_residual is not None:
        v_first, v_down, v0, v2 = value_residual
        v = v + (f32(v_first) - v) * jax.nn.sigmoid(f32(v0) + f32(v_down) @ f32(v2))
    v_out = v
    b, s = pb.shape[0], pb.shape[1]
    heads = lambda t: t.reshape(b, s, RWKV_HEADS, RWKV_HEAD_DIM)
    kk = heads(k * f32(k_k))
    kk = kk / jnp.maximum(jnp.sqrt(jnp.sum(kk * kk, axis=-1, keepdims=True)), L2_EPS)
    k = k * (1.0 + (a - 1.0) * f32(k_a))
    rh, kh, vh, ah = heads(r), heads(k), heads(v), heads(a)
    y = rwkv7_scan(rh, heads(w), kh, vh, -kk, kk * ah)
    mu = jnp.mean(y, axis=-1, keepdims=True)
    var = jnp.mean(jnp.square(y - mu), axis=-1, keepdims=True)
    y = ((y - mu) * lax.rsqrt(var + GN_EPS)).reshape(b, s, RWKV_WIDTH) * f32(ln_w) + f32(ln_b)
    bonus = jnp.sum(rh * kh * f32(r_k), axis=-1, keepdims=True) * vh
    y = (y + bonus.reshape(b, s, RWKV_WIDTH)) * g
    return y.astype(out_dtype), v_out

def memory_attention(q, mk, mv):
    logits = jnp.einsum('bshd,bmhd->bhsm', q, mk,
                        preferred_element_type=jnp.float32) * (HEAD_DIM ** -0.5)
    p = jax.nn.softmax(logits, axis=-1)
    out = jnp.einsum('bhsm,bmhd->bshd', p.astype(mv.dtype), mv)
    return out.reshape(q.shape[0], q.shape[1], MEM_WIDTH)

def conv_ffn_2(h, w_up, conv_w, conv_b, w_down):
    u = h @ w_up
    s = u.shape[1]
    up_pad = jnp.pad(u, ((0, 0), (CONV_WIDTH_2 - 1, 0), (0, 0)))
    uc = conv_b + sum(conv_w[i] * up_pad[:, i:i + s] for i in range(CONV_WIDTH_2))
    gate, val = jnp.split(uc, 2, axis=-1)
    return (jax.nn.silu(gate) * val) @ w_down

def second_inputs(seed: int = 0) -> dict:
    key = jax.random.key(seed)
    ks = iter(jax.random.split(key, 40))
    n = lambda shape: jax.random.normal(next(ks), shape, jnp.float32)
    L, Lv = DEPTH_2, DEPTH_2 - 1
    C = RWKV_WIDTH
    return {
        "x": n((BATCH, SEQ, D_MODEL)),
        "mem": n((BATCH, MEM_TOKENS, D_MODEL)),
        "rel_bias": 0.5 * n((N_BUCKETS, ATTN_HEADS)),
        "mix_norm_g": 1.0 + 0.1 * n((L, D_MODEL)),
        "w_in": n((L, D_MODEL, IN_BASE)) * D_MODEL ** -0.5,
        "w_in_vres": n((Lv, D_MODEL, D_MV_LORA)) * D_MODEL ** -0.5,
        "attn_q_norm": 1.0 + 0.1 * n((L, HEAD_DIM)),
        "attn_k_norm": 1.0 + 0.1 * n((L, HEAD_DIM)),
        "attn_sinks": n((L, ATTN_HEADS)),
        "rwkv_mu": jax.random.uniform(next(ks), (L, RWKV_SHIFT_COLS), jnp.float32),
        "rwkv_mu_vres": jax.random.uniform(next(ks), (Lv, D_MV_LORA), jnp.float32),
        "rwkv_w0": -2.0 + 0.5 * n((L, C)),
        "rwkv_w2": 0.5 * n((L, D_DECAY_LORA, C)) * D_DECAY_LORA ** -0.5,
        "rwkv_a0": 0.5 * n((L, C)),
        "rwkv_a2": 0.5 * n((L, D_AAA_LORA, C)) * D_AAA_LORA ** -0.5,
        "rwkv_v0": 0.5 * n((Lv, C)),
        "rwkv_v2": 0.5 * n((Lv, D_MV_LORA, C)) * D_MV_LORA ** -0.5,
        "rwkv_g2": n((L, D_GATE_LORA, C)) * D_GATE_LORA ** -0.5,
        "rwkv_k_k": 0.85 + 0.1 * n((L, C)),
        "rwkv_k_a": 1.0 + 0.1 * n((L, C)),
        "rwkv_r_k": 0.1 * n((L, RWKV_HEADS, RWKV_HEAD_DIM)),
        "rwkv_ln_w": 1.0 + 0.1 * n((L, C)),
        "rwkv_ln_b": 0.02 * n((L, C)),
        "mem_norm_g": 1.0 + 0.1 * n((L, D_MODEL)),
        "w_mem_kv": n((L, D_MODEL, 2 * MEM_WIDTH)) * D_MODEL ** -0.5,
        "mem_q_norm": 1.0 + 0.1 * n((L, HEAD_DIM)),
        "mem_k_norm": 1.0 + 0.1 * n((L, HEAD_DIM)),
        "w_out": n((L, MIX_WIDTH, D_MODEL)) * MIX_WIDTH ** -0.5,
        "ffn_norm_g": 1.0 + 0.1 * n((L, D_MODEL)),
        "w_up": n((L, D_MODEL, 2 * D_FF)) * D_MODEL ** -0.5,
        "conv_w": n((L, CONV_WIDTH_2, 2 * D_FF)) * CONV_WIDTH_2 ** -0.5,
        "conv_b": 0.02 * n((L, 2 * D_FF)),
        "w_down": n((L, D_FF, D_MODEL)) * D_FF ** -0.5,
    }

def second_block(x, mem, rel_bias, mix_norm_g, w_in, w_in_vres, attn_q_norm, attn_k_norm, attn_sinks,
              rwkv_mu, rwkv_mu_vres, rwkv_w0, rwkv_w2, rwkv_a0, rwkv_a2, rwkv_v0, rwkv_v2, rwkv_g2,
              rwkv_k_k, rwkv_k_a, rwkv_r_k, rwkv_ln_w, rwkv_ln_b, mem_norm_g, w_mem_kv,
              mem_q_norm, mem_k_norm, w_out, ffn_norm_g, w_up, conv_w, conv_b, w_down):
    b, s = x.shape[0], x.shape[1]
    m_tok = mem.shape[1]
    v_first = None
    for l in range(DEPTH_2):
        h = rms_norm(x, mix_norm_g[l])
        w_l = w_in[l] if l == 0 else jnp.concatenate([w_in[l], w_in_vres[l - 1]], axis=1)
        proj = h @ w_l
        sizes = [ATTN_WIDTH, ATTN_KV_WIDTH, ATTN_KV_WIDTH, RWKV_SHIFT_COLS, MEM_WIDTH]
        if l > 0:
            sizes = sizes + [D_MV_LORA]
        parts = split_cols(proj, sizes)
        qa, ka, va, pb, qm = parts[:5]

        qa = rms_norm(qa.reshape(b, s, ATTN_HEADS, HEAD_DIM), attn_q_norm[l])
        ka = rms_norm(ka.reshape(b, s, ATTN_KV_HEADS, HEAD_DIM), attn_k_norm[l])
        va = va.reshape(b, s, ATTN_KV_HEADS, HEAD_DIM)
        out_a = sliding_window_attention(qa, ka, va, attn_sinks[l], rel_bias)

        pb = token_shift(pb, rwkv_mu[l])
        if l == 0:
            vres = None
        else:
            v_down = token_shift(parts[5], rwkv_mu_vres[l - 1])
            vres = (v_first, v_down, rwkv_v0[l - 1], rwkv_v2[l - 1])
        out_b, v_l = rwkv7_mixer(pb, vres, rwkv_w0[l], rwkv_w2[l], rwkv_a0[l], rwkv_a2[l],
                                 rwkv_g2[l], rwkv_k_k[l], rwkv_k_a[l], rwkv_r_k[l],
                                 rwkv_ln_w[l], rwkv_ln_b[l])
        if l == 0:
            v_first = v_l

        mkv = rms_norm(mem, mem_norm_g[l]) @ w_mem_kv[l]
        mk, mv = jnp.split(mkv, 2, axis=-1)
        mk = rms_norm(mk.reshape(b, m_tok, MEM_HEADS, HEAD_DIM), mem_k_norm[l])
        mv = mv.reshape(b, m_tok, MEM_HEADS, HEAD_DIM)
        qm = rms_norm(qm.reshape(b, s, MEM_HEADS, HEAD_DIM), mem_q_norm[l])
        out_m = memory_attention(qm, mk, mv)

        x = x + jnp.concatenate([out_a, out_b, out_m], axis=-1) @ w_out[l]

        x = x + conv_ffn_2(rms_norm(x, ffn_norm_g[l]), w_up[l], conv_w[l], conv_b[l], w_down[l])
    return x


def setup_inputs(seed=0):
    out = dict(first_inputs(seed))
    for name, value in second_inputs(seed + 1).items():
        if name != "x":
            out[name + "_2"] = value
    return out


def reference(
    x, c, ctx, c_ctx, ada_w, ada_b, norm1_g, norm2_g, final_g, conv_w_pw1, conv_b_pw1,
    conv_w_dw, conv_b_dw, conv_ln_g, conv_ln_b, conv_w_pw2, conv_b_pw2, attn_w_qkv, attn_w_o,
    attn_sink, ffn_w_up, ffn_w_dw, ffn_b_dw, ffn_w_down, mem_2, rel_bias_2, mix_norm_g_2,
    w_in_2, w_in_vres_2, attn_q_norm_2, attn_k_norm_2, attn_sinks_2, rwkv_mu_2, rwkv_mu_vres_2,
    rwkv_w0_2, rwkv_w2_2, rwkv_a0_2, rwkv_a2_2, rwkv_v0_2, rwkv_v2_2, rwkv_g2_2, rwkv_k_k_2,
    rwkv_k_a_2, rwkv_r_k_2, rwkv_ln_w_2, rwkv_ln_b_2, mem_norm_g_2, w_mem_kv_2, mem_q_norm_2,
    mem_k_norm_2, w_out_2, ffn_norm_g_2, w_up_2, conv_w_2, conv_b_2, w_down_2,
):
    x = first_block(
        x, c, ctx, c_ctx, ada_w, ada_b, norm1_g, norm2_g, final_g, conv_w_pw1, conv_b_pw1,
        conv_w_dw, conv_b_dw, conv_ln_g, conv_ln_b, conv_w_pw2, conv_b_pw2, attn_w_qkv,
        attn_w_o, attn_sink, ffn_w_up, ffn_w_dw, ffn_b_dw, ffn_w_down,
    )
    return second_block(
        x, mem_2, rel_bias_2, mix_norm_g_2, w_in_2, w_in_vres_2, attn_q_norm_2, attn_k_norm_2,
        attn_sinks_2, rwkv_mu_2, rwkv_mu_vres_2, rwkv_w0_2, rwkv_w2_2, rwkv_a0_2, rwkv_a2_2,
        rwkv_v0_2, rwkv_v2_2, rwkv_g2_2, rwkv_k_k_2, rwkv_k_a_2, rwkv_r_k_2, rwkv_ln_w_2,
        rwkv_ln_b_2, mem_norm_g_2, w_mem_kv_2, mem_q_norm_2, mem_k_norm_2, w_out_2,
        ffn_norm_g_2, w_up_2, conv_w_2, conv_b_2, w_down_2,
    )


_drawn_inputs = setup_inputs


def setup_inputs(seed=0):
    import zlib

    import numpy as np

    out = dict(_drawn_inputs(seed))
    spreads = {}
    factors = {'norm1_g': 3.09,
     'conv_b_pw1': 8.0,
     'conv_b_dw': 4.605,
     'conv_ln_g': 2.749,
     'conv_ln_b': 7.936,
     'conv_b_pw2': 4.519,
     'attn_sink': 64.0,
     'ffn_b_dw': 4.151,
     'attn_q_norm_2': 5.678,
     'attn_k_norm_2': 5.225,
     'attn_sinks_2': 41.488,
     'rwkv_w2_2': 8.394,
     'rwkv_k_k_2': 26.946,
     'rwkv_ln_b_2': 33.91,
     'mem_norm_g_2': 6.989,
     'mem_q_norm_2': 8.0,
     'mem_k_norm_2': 8.0,
     'conv_b_2': 11.91,
     'rel_bias_2': 4.381,
     'rwkv_a2_2': 3.026,
     'rwkv_k_a_2': 4.545,
     'rwkv_ln_w_2': 6.387,
     'ffn_norm_g_2': 2.743}
    for name, (base, spread) in spreads.items():
        noise = np.random.default_rng([zlib.crc32(name.encode()), seed]).standard_normal(out[name].shape)
        drawn = base * np.exp(spread * noise) if base else spread * noise
        out[name] = jnp.asarray(drawn.astype(out[name].dtype))
    for name, factor in factors.items():
        out[name] = (out[name] * factor).astype(out[name].dtype)
    return out
```

```python
from contextlib import ExitStack

import concourse.bass as bass
from concourse import mybir
import numpy as np

P = 128
D = 1024
KD = D // P
SEQ = 512
CTX = 256
TOK = SEQ + CTX
DFF = 2816
FT = DFF // P
HALF = FT // 2
HD = 64
TAPS = 31
PAD = TAPS // 2
EPS = 1e-6
GN_EPS = 64e-5
L2_EPS = 1e-12
KAPPA = float(np.exp(-0.5))
NEG = -1e30

F32 = mybir.dt.float32
F32R = mybir.dt.float32r
U32 = mybir.dt.uint32
ALU = mybir.AluOpType
ACT = mybir.ActivationFunctionType
AX = mybir.AxisListType

LEAD = 8


def done(n):
    return n + LEAD


PARAM_ROWS = [
    ("c", 8), ("c_ctx", 8), ("ada_b", 96), ("norm1_g", 16), ("norm2_g", 16), ("final_g", 8),
    ("conv_b_pw1", 16), ("conv_w_dw", 8 * TAPS), ("conv_b_dw", 8), ("conv_ln_g", 8), ("conv_ln_b", 8),
    ("conv_b_pw2", 8), ("ffn_w_dw", 2 * 3 * 2 * FT), ("ffn_b_dw", 2 * 2 * FT),
    ("mix_norm_g_2", 8), ("mem_norm_g_2", 8), ("ffn_norm_g_2", 8), ("conv_w_2", 3 * 2 * FT),
    ("conv_b_2", 2 * FT), ("rwkv_mu_2", 10), ("rwkv_a0_2", 3), ("rwkv_k_k_2", 3), ("rwkv_k_a_2", 3),
    ("rwkv_r_k_2", 3), ("rwkv_ln_w_2", 3), ("rwkv_ln_b_2", 3),
    ("attn_q_norm_2", 1), ("attn_k_norm_2", 1), ("mem_q_norm_2", 1), ("mem_k_norm_2", 1),
]
COL, _n = {}, 0
for _name, _rows in PARAM_ROWS:
    COL[_name] = _n
    _n += _rows
N_ROWS = _n
PT = -(-N_ROWS // P)

STREAMS = [("pw1", 16, 8), ("pw2", 8, 8)]
for _h in (0, 1):
    STREAMS += [(f"up0{_h}", 2 * HALF, 8), (f"down0{_h}", 8, HALF)]
STREAMS += [("qkv", 12, 8), ("wo", 8, 8)]
for _h in (0, 1):
    STREAMS += [(f"up1{_h}", 2 * HALF, 8), (f"down1{_h}", 8, HALF)]
STREAMS += [("w_in", 17, 8), ("mem_kv", 4, 8), ("w_out", 8, 8)]
for _h in (0, 1):
    STREAMS += [(f"up2{_h}", 2 * HALF, 8), (f"down2{_h}", 8, HALF)]
Q0, ROWS_OF, _q = {}, {}, 0
ROWS_AT = []
for _name, _chunks, _rows in STREAMS:
    Q0[_name], ROWS_OF[_name] = _q, _rows
    ROWS_AT += [_rows] * _chunks
    _q += _chunks
N_CHUNKS = dict((s[0], s[1]) for s in STREAMS)
Q_ALL = _q

NORMS = ["n10", "ln", "n20", "n11", "n21", "final", "mix", "ffn2_norm"]
NN = {s: i for i, s in enumerate(NORMS)}


def constants():
    eye = np.eye(P, dtype=np.float32)
    ones = np.ones((P, P), np.float32)
    head = np.kron(np.eye(2, dtype=np.float32), np.ones((HD, HD), np.float32))
    base = np.concatenate([eye, ones, head], 1)

    rot = np.zeros((P, P), np.float32)
    for h in (0, HD):
        for d in range(HD // 2):
            rot[h + d + HD // 2, h + d] = -1.0
            rot[h + d, h + d + HD // 2] = 1.0
    low = np.zeros((P, P), np.float32)
    high = np.zeros((P, P), np.float32)
    for d in range(HD):
        low[d, d] = low[d, d + HD] = 1.0
        high[d + HD, d] = high[d + HD, d + HD] = 1.0
    n_freq = HD // 4
    inv = np.float32(10000.0) ** (-np.arange(n_freq, dtype=np.float32) / np.float32(n_freq))
    pos = np.arange(SEQ)
    row, col = (pos // 64).astype(np.float32), (pos % 64).astype(np.float32)
    ang = np.concatenate([row[None] * inv[:, None], col[None] * inv[:, None]], 0).astype(np.float32)
    cos, sin = np.tile(np.cos(ang), (4, 1)), np.tile(np.sin(ang), (4, 1))
    q, k = np.arange(P)[:, None], np.arange(P)[None]
    before = np.where(k >= q, 0.0, NEG).astype(np.float32)
    after = np.where(k <= q, 0.0, NEG).astype(np.float32)
    first = np.concatenate([rot, low, high, cos, sin, before, np.zeros_like(before), after], 1)

    anti = eye[:, ::-1].copy()
    s, t = q, k
    strict, upto = (s < t).astype(np.float32), (s <= t).astype(np.float32)
    tri = np.concatenate([upto, strict], 1)
    mask = np.concatenate([strict, upto, strict, upto], 1)
    levels = []
    for e in range(7):
        b = 1 << e
        levels.append(((s // (2 * b) == t // (2 * b)) & (s // b % 2 == 0) & (t // b % 2 == 1)).astype(np.float32))
    second = np.concatenate([low, high, anti, tri, mask] + levels, 1)

    j = np.arange(384)
    dist = 255 - j
    inside = (dist >= 0) & (dist < 128)
    dd = np.clip(dist, 0, 127)
    large = 16 + (np.log(np.maximum(dd, 1).astype(np.float32) / np.float32(16)) / np.float32(np.log(128 / 16))
                  * np.float32(16)).astype(np.int32)
    bucket = np.where(dd < 16, dd, np.minimum(large, 31))
    hot = np.zeros((P, 384), np.float32)
    hot[bucket[inside], j[inside]] = 1.0
    hot[32, ~inside] = NEG
    return {"k_base": base.astype(np.float32), "k_first": first.astype(np.float32),
            "k_second": second.astype(np.float32), "k_hot": hot}


class Program:

    def __init__(self, nc, ctx, A):
        self.nc, self.A, self.ctx = nc, A, ctx
        base = -(-nc.sbuf_base // 64) * 64
        self.top = base

        def region(nbytes):
            at = self.top
            self.top += -(-nbytes // 64) * 64
            return at

        def at(name, offset, shape, dt=F32):
            return nc.alloc_sbuf_tensor_at(name, [P] + shape, dt, offset=offset)

        self.h = at("h", region(KD * TOK * 4), [KD, TOK])
        r_x = region(2 * KD * TOK * 4)
        self.x_hi = at("x_hi", r_x, [KD, TOK], F32R)
        self.x_lo = at("x_lo", r_x + KD * TOK * 4, [KD, TOK], F32R)
        r_g = region(2 * HALF * TOK * 4)
        self.r_x, self.r_g = r_x, r_g
        self.g_hi = at("g_hi", r_g, [HALF, TOK], F32R)
        self.g_lo = at("g_lo", r_g + HALF * TOK * 4, [HALF, TOK], F32R)
        w = HALF * P * 4
        self.raw = at("raw", region(2 * w), [2, HALF * P])
        self.w_hi = at("w_hi", region(2 * w), [2, HALF * P], F32R)
        self.w_lo = at("w_lo", region(2 * w), [2, HALF * P], F32R)
        self.prm = at("prm", region(PT * P * 4), [PT * P])
        self.kb = at("kb", region(3 * P * 4), [3 * P])
        self.mods = at("mods", region(96 * 2 * 4), [96, 2])
        self.scg = at("scg", region(64 * 4), [2, 2, 2, KD])
        self.b2g1 = at("b2g1", region(16 * 4), [2, KD])
        self.sc = at("sc", region(16 * 4), [2 * KD])
        self.sinks = at("sinks", region(24 * 4), [24])
        self.one = at("one", region(32), [8])
        self.sm_max = at("sm_max", region(64), [2])
        self.sm_neg = at("sm_neg", region(64), [2])
        self.sm_sum = at("sm_sum", region(64), [2])
        self.sm_sink = at("sm_sink", region(64), [2])
        self.sm_den = at("sm_den", region(64), [2])
        self.sm_rd = at("sm_rd", region(64), [2])
        self.sinkg = at("sinkg", region(64), [4])
        self.cend = at("cend", region(48 * 4), [4, 3, 4])
        self.gn = at("gn", region(6 * 6 * 4), [6, 6])
        r_s = region(8 * TOK * 4)
        self.r_s = r_s
        assert self.top <= nc.sbuf_usable_end, (self.top, nc.sbuf_usable_end)
        self.left = nc.sbuf_usable_end - self.top

        ln = TOK * 4
        self.n_sq = at("n_sq", r_s, [2, TOK])
        self.n_t = at("n_t", r_s + 2 * ln, [2, TOK])
        self.n_y = at("n_y", r_s + 4 * ln, [2, TOK])
        self.f_a = at("f_a", r_s, [2, TOK])
        self.f_b = at("f_b", r_s + 2 * ln, [2, TOK])
        self.gate = at("gate", r_s + 6 * ln, [2, TOK])

        self.x_rows = at("x_rows", r_g, [6, D])
        self.p_rows = at("p_rows", r_g + 6 * D * 4, [PT, P])
        self.m_rows = at("m_rows", r_g, [2, D])
        self.ada = at("ada", r_x, [6, KD, 256])
        self.vw = SEQ + CTX + 4 * PAD
        self.vp = at("vp", r_g, [KD, self.vw])
        self.cv = at("cv", r_g + KD * self.vw * 4, [KD, TOK])
        o = r_g
        def nxt(name, shape, dt=F32):
            nonlocal o
            t = at(name, o, shape, dt)
            o += int(np.prod(shape)) * 4
            return t
        self.s_sb = nxt("s_sb", [2, 640])
        self.kf = nxt("kf", [3 * P + 2 * SEQ + 3 * P])
        self.q_ = nxt("q_", [8, SEQ])
        self.k_ = nxt("k_", [2, TOK])
        self.v_ = nxt("v_", [2, TOK])
        self.vt = nxt("vt", [6, 256])
        self.kd = nxt("kd", [4, TOK])
        assert o <= r_g + 2 * HALF * TOK * 4, o - r_g
        o = r_s
        self.qg = nxt("qg", [2, SEQ])
        self.p_sb = nxt("p_sb", [2, 640])
        self.pt_sb = nxt("pt_sb", [2, 640])
        self.o_t = nxt("o_t", [4, 256])
        self.kg = nxt("kg", [TOK])
        self.vg = nxt("vg", [6, HD])
        assert o <= r_s + 8 * ln
        o = r_g + 2 * 640 * 4
        self.pj = nxt("pj", [17, SEQ])
        r_mkv = o
        self.mkv = nxt("mkv", [4, CTX])
        self.ks = nxt("ks", [3 * P + 2 * P + 4 * P + 7 * P])
        r_b = o
        self.bias = nxt("bias", [6, 2 * P])
        self.lw = nxt("lw", [384])
        self.w0b = nxt("w0b", [384])
        r_av = o
        self.av = nxt("av", [3, SEQ])
        assert o <= r_g + 2 * HALF * TOK * 4, o - r_g
        o = r_av
        self.hot = nxt("hot", [384])
        self.rr = nxt("rr", [384])
        self.relb = nxt("relb", [8])
        self.tz = at("tz", r_s + 4096, [6, 2 * P])
        o = r_s
        self.sig = nxt("sig", [4, 384])
        self.ex = nxt("ex", [3, SEQ])
        self.dd = nxt("dd", [2, SEQ])
        self.hq = nxt("hq", [2, SEQ])
        o = r_s
        self.m4 = nxt("m4", [6, 512])
        self.inv = nxt("inv", [6, P])
        self.inv_t = nxt("inv_t", [6, P])
        self.mt = nxt("mt", [6, P])
        self.lv = nxt("lv", [6, P])
        assert o <= r_s + 8 * ln
        o = r_b
        self.tok = nxt("tok", [3, 384])
        self.y = nxt("y", [384])
        o = r_mkv
        self.x0 = nxt("x0", [384])
        self.u = nxt("u", [384])
        self.z = nxt("z", [3, HD])
        o = r_g
        self.y1 = nxt("y1", [3, P])
        self.ysq = nxt("ysq", [384])
        self.at = at

        self.ps = ctx.enter_context(nc.psum_tensor("ps", [P, 4096], F32))
        self.counting = []

    def sem(self, name, counting=True):
        s = self.ctx.enter_context(self.nc.semaphore(name))
        if counting:
            self.counting.append(s)
        return s

    def pair(self, n, lo=0, hi=TOK):
        return self.ps[:, n * 1024 + lo:n * 1024 + hi]

    def col(self, name, r=0):
        c = COL[name] + r
        return self.prm[:, c:c + 1]

    def col_at(self, name, r):
        return self.prm[:, bass.ds(r + COL[name], 1)]


def chunks(eng, n):
    full = (n - 2) // 4
    if full >= 2:
        with eng.Fori(0, full) as it:
            for u in range(4):
                yield it, u
    else:
        full = 0
    for i in range(4 * full, n):
        yield i // 4, i % 4


def build(nc, A, out, stop=None, dump=None):
    with ExitStack() as ctx:
        build_in(nc, ctx, A, out, stop, dump)


def build_in(nc, ctx, A, out, stop, dump):
    M = Program(nc, ctx, A)
    sem = M.sem
    ident, ones, head1 = M.kb[:, 0:P], M.kb[:, P:2 * P], M.kb[:, 2 * P:3 * P]

    s_cst = sem("s_cst", False)
    s_rows = sem("s_rows", False)
    s_raw = [sem(f"s_raw{i}", False) for i in range(2)]
    s_ada = [sem(f"s_ada{i}", False) for i in range(6)]
    s_kf = sem("s_kf", False)
    s_mem = sem("s_mem", False)
    s_out = sem("s_out", False)
    hi_ready = sem("hi_ready")
    lo_ready = sem("lo_ready")
    tile_done = sem("tile_done")
    evac = sem("evac")
    ada_used = sem("ada_used")
    start_t = sem("start_t")
    start_c = sem("start_c")
    zero_ready = sem("zero_ready")
    sc_ready = sem("sc_ready")
    mod_ready = sem("mod_ready")
    sq_ready = sem("sq_ready")
    sq_used = sem("sq_used")
    rms_ready = sem("rms_ready")
    rstd_ready = sem("rstd_ready")
    t_ready = sem("t_ready")
    y_ready = sem("y_ready")
    x_ready = sem("x_ready")
    h_ready = sem("h_ready")
    gate_ready = sem("gate_ready")
    v_ready = sem("v_ready")
    tap_done = sem("tap_done")
    cv_ready = sem("cv_ready")
    cv_cent = sem("cv_cent")
    mu_ready = sem("mu_ready")
    mid_ready = sem("mid_ready")
    taps_ready = sem("taps_ready")
    silu_ready = sem("silu_ready")
    prod_ready = sem("prod_ready")
    ghi_ready = sem("ghi_ready")
    g_ready = sem("g_ready")
    f_res = sem("f_res")

    rope_r = sem("rope_r")
    rope_c = sem("rope_c")
    turn_t = sem("turn_t")
    turn_c = sem("turn_c")
    grp_ready = sem("grp_ready")
    att_s = sem("att_s")
    att_m = sem("att_m")
    att_p = sem("att_p")
    att_r = sem("att_r")
    att_t = sem("att_t")
    att_c = sem("att_c")
    att_o = sem("att_o")
    att_e = sem("att_e")
    otr_t = sem("otr_t")
    otr_h = sem("otr_h")
    xa_ready = sem("xa_ready")

    H_STAGE = ["start", "pw2", "down00", "down01", "wo", "down10", "down11", "final", "w_out",
               "down20", "down21"]
    H = {s: 8 * (i + 1) for i, s in enumerate(H_STAGE)}

    order = ["start", "ada", "n10", "pw1", "ln", "pw2", "n20", "ffn0", "n11", "qkv", "attn", "wo",
             "n21", "ffn1", "final", "mix", "w_in", "mixers", "w_out", "ffn2_norm", "ffn2"]
    if stop:
        order = order[:order.index(stop) + 1]
    streams_of = {"pw1": ["pw1"], "pw2": ["pw2"], "qkv": ["qkv"], "wo": ["wo"],
                  "w_in": ["w_in", "mem_kv"], "w_out": ["w_out"]}
    for b in range(3):
        streams_of[f"ffn{b}"] = [f"{d}{b}{hf}" for hf in (0, 1) for d in ("up", "down")]
    used_streams = [s for st in order for s in streams_of.get(st, [])]
    q_end = sum(N_CHUNKS[s] for s in used_streams)

    def rows(ap, kt):
        return ap.rearrange("(kt p) c -> p kt c", p=P)

    w_src = {"pw1": rows(A["conv_w_pw1"][0], 8), "pw2": rows(A["conv_w_pw2"][0], 8),
             "qkv": rows(A["attn_w_qkv"][0], 8), "wo": rows(A["attn_w_o"][0], 8),
             "w_in": rows(A["w_in_2"][0], 8), "mem_kv": rows(A["w_mem_kv_2"][0], 8),
             "w_out": rows(A["w_out_2"][0], 8)}
    for b in range(3):
        up = A["w_up_2"][0] if b == 2 else A["ffn_w_up"][b]
        down = A["w_down_2"][0] if b == 2 else A["ffn_w_down"][b]
        for hf in (0, 1):
            w_src[f"up{b}{hf}"] = rows(up, 8)
            w_src[f"down{b}{hf}"] = rows(down[hf * HALF * P:(hf + 1) * HALF * P, :], HALF)

    def column(name, it, u):
        if name == "pw1":
            return it * 256 + ((u % 2) * 8 + u // 2) * P
        if name.startswith("up"):
            return it * 256 + ((u % 2) * FT + int(name[3]) * HALF + u // 2) * P
        return it * 512 + u * P

    def load_stream(sp, name):
        K, q0 = ROWS_OF[name], Q0[name]
        n, full = N_CHUNKS[name], N_CHUNKS[name] // 4
        def one(it, u):
            slot = (q0 + u) % 2
            c = column(name, it, u)
            if not isinstance(c, int):
                c = sp.snap(c)
            sp.wait_ge(lo_ready, done(q0 + 4 * it + u - 1))
            sp.dma_start(M.raw[:, slot, 0:K * P].rearrange("p (k c) -> p k c", c=P),
                         w_src[name][:, :, bass.ds(c, P)]).then_inc(s_raw[slot], 16)
        if full >= 2:
            with sp.Fori(0, full) as it:
                for u in range(4):
                    one(it, u)
        else:
            full = 0
        for i in range(4 * full, n):
            one(i // 4, i % 4)

    def raw_count(q0, it, u):
        return 16 * (2 * it + (q0 + u) // 2 + 1)

    def low_stream(pool, name):
        K, q0 = ROWS_OF[name], Q0[name]
        n, full = N_CHUNKS[name], N_CHUNKS[name] // 4
        def one(it, u):
            slot = (q0 + u) % 2
            pool.wait_ge(hi_ready, done(q0 + 4 * it + u + 1))
            pool.tensor_tensor(M.w_lo[:, slot, 0:K * P], M.raw[:, slot, 0:K * P],
                               M.w_hi[:, slot, 0:K * P].bitcast(F32), ALU.subtract).then_inc(lo_ready, 1)
        if full >= 2:
            with pool.Fori(0, full) as it:
                for u in range(4):
                    one(it, u)
        else:
            full = 0
        for i in range(4 * full, n):
            one(i // 4, i % 4)

    def high(act, name, it, u):
        q0 = Q0[name]
        if isinstance(it, int):
            q = q0 + 4 * it + u + 2
            if q >= q_end:
                return
            K = ROWS_AT[q]
        else:
            K = ROWS_OF[name]
        slot = (q0 + u) % 2
        act.wait_ge(s_raw[slot], raw_count(q0, it, u + 2))
        act.wait_ge(tile_done, done(q0 + 4 * it + u + 1))
        act.activation(M.w_hi[:, slot, 0:K * P], M.raw[:, slot, 0:K * P], ACT.Copy).then_inc(hi_ready, 1)

    def high_first(act):
        for q in range(min(2, q_end)):
            act.wait_ge(s_raw[q], 16)
            act.activation(M.w_hi[:, q, 0:ROWS_AT[q] * P], M.raw[:, q, 0:ROWS_AT[q] * P], ACT.Copy)\
                .then_inc(hi_ready, 1)

    LAT, BOTH, MEM = [(0, SEQ)], [(0, SEQ), (SEQ, CTX)], [(SEQ, CTX)]

    def products(pe, name, it, u, segs, from_g=0):
        K, q0 = ROWS_OF[name], Q0[name]
        slot, pair = (q0 + u) % 2, (q0 + u) % 4
        hi, lo = (M.g_hi, M.g_lo) if from_g else (M.x_hi, M.x_lo)
        pe.wait_ge(lo_ready, done(q0 + 4 * it + u + 1))
        pe.wait_ge(evac, done(q0 + 4 * it + u - 3))
        for n, (t0, tn) in enumerate(segs):
            for k in range(K):
                if from_g and n == 0 and u == 0 and isinstance(it, int) and it == 0:
                    pe.wait_ge(g_ready, done(from_g - HALF + k + 1))
                wh = M.w_hi[:, slot, k * P:(k + 1) * P]
                wl = M.w_lo[:, slot, k * P:(k + 1) * P]
                o = M.pair(pair, t0, t0 + tn)
                pe.matmul(o, wh, hi[:, k, t0:t0 + tn], start=(k == 0), stop=False)
                pe.matmul(o, wh, lo[:, k, t0:t0 + tn], start=False, stop=False)
                mm = pe.matmul(o, wl, hi[:, k, t0:t0 + tn], start=False, stop=(k == K - 1))
        mm.then_inc(tile_done, 1)

    def stream_pe(pe, name, segs_of, from_g=0):
        for it, u in chunks(pe, N_CHUNKS[name]):
            products(pe, name, it, u, segs_of(it, u), from_g)


    def start_sp(sp):
        sp.dma_start(M.kb[:, :], A["k_base"]).then_inc(s_cst, 16)
        sp.wait_ge(zero_ready, done(1))
        for name, r in PARAM_ROWS:
            src = A[name]
            if name.endswith("norm_2") and r == 1:
                c = COL[name]
                for half in (0, 1):
                    sp.dma_start(M.p_rows[c % P:c % P + 1, c // P, half * HD:(half + 1) * HD], src)\
                        .then_inc(s_cst, 16)
                continue
            dims = " ".join(f"d{i}" for i in range(len(src.shape)))
            flat = src.rearrange(f"{dims} -> ({dims})") if len(src.shape) > 1 else src
            flat = flat.rearrange("(r c) -> r c", c=P)
            r0 = 0
            while r0 < r:
                c = COL[name] + r0
                n = min(r - r0, P - c % P)
                sp.dma_start(M.p_rows[c % P:c % P + n, c // P, :], flat[r0:r0 + n, :]).then_inc(s_cst, 16)
                r0 += n
        sp.dma_start(M.sinks[:, 0:16], A["attn_sink"][0:1, :].to_broadcast([P, 16])).then_inc(s_cst, 16)
        sp.dma_start(M.sinks[:, 16:22], A["attn_sinks_2"][0:1, :].to_broadcast([P, 6])).then_inc(s_cst, 16)
        sp.dma_start(M.x_rows[:, 0:4, :], A["x"][0].rearrange("(t p) d -> p t d", p=P)).then_inc(s_rows, 16)
        sp.dma_start(M.x_rows[:, 4:6, :], A["ctx"][0].rearrange("(t p) d -> p t d", p=P)).then_inc(s_rows, 16)

    ada_src = A["ada_w"].rearrange("l (kt p) c -> p l kt c", p=P)

    def ada_sp(sp):
        for l in (0, 1):
            with sp.Fori(0, 4) as it:
                for u in range(6):
                    c = sp.snap(it * (6 * 256) + u * 256)
                    sp.wait_ge(ada_used, done(24 * l + 6 * it + u - 5))
                    sp.dma_start(M.ada[:, u, :, :], ada_src[:, l, :, bass.ds(c, 256)]).then_inc(s_ada[u], 16)

    def start_pe(pe):
        pe.wait_ge(s_cst, 16 * M.n_param_dma)
        for t in range(PT):
            bank = t // 4
            mm = pe.transpose(M.ps[:, bank * 512 + (t % 4) * P:bank * 512 + (t % 4 + 1) * P],
                              M.p_rows[:, t, :], ident)
            if t % 4 == 3 or t == PT - 1:
                mm.then_inc(start_t, 1)
        pe.wait_ge(s_rows, 32)
        for k in range(KD):
            pair = (k + 2) % 4
            if k >= 2:
                pe.wait_ge(start_c, done(k))
            for t in range(6):
                mm = pe.transpose(M.pair(pair, t * P, (t + 1) * P), M.x_rows[:, t, k * P:(k + 1) * P], ident)
            mm.then_inc(start_t, 1)

    def start_act(act):
        act.wait_ge(start_t, done(1))
        act.activation(M.prm[:, 0:512], M.ps[:, 0:512], ACT.Copy).then_inc(start_c, 1)
        act.wait_ge(start_t, done(2))
        act.activation(M.prm[:, 512:1024], M.ps[:, 512:1024], ACT.Copy).then_inc(start_c, 1)
        act.wait_ge(start_t, done(3))
        act.activation(M.prm[:, 1024:PT * P], M.ps[:, 1024:PT * P], ACT.Copy).then_inc(start_c, 1)
        act.wait_ge(start_c, done(3))
        act.activation(M.sc[:, :], M.prm[:, COL["c"]:COL["c"] + 16], ACT.Silu).then_inc(sc_ready, 1)
        for k in range(KD):
            act.wait_ge(start_t, done(4 + k))
            act.activation(M.h[:, k, :], M.pair((k + 2) % 4), ACT.Copy).then_inc(start_c, 1)

    def ada_pe(pe):
        pe.wait_ge(sc_ready, done(1))
        pe.wait_ge(start_c, done(3 + KD))
        cond = M.sc[:, :].rearrange("p (s k) -> p k s", s=2)
        for l in (0, 1):
            with pe.Fori(0, 4) as it:
                for u in range(6):
                    pe.wait_ge(s_ada[u], 16 * (4 * l + it + 1))
                    for t in (0, 1):
                        o = M.ps[:, bass.ds(it * 24 + (96 * l + 4 * u + 2 * t), 2)]
                        for k in range(KD):
                            mm = pe.matmul(o, M.ada[:, u, k, t * P:(t + 1) * P], cond[:, k, :],
                                           start=(k == 0), stop=(k == KD - 1))
                    mm.then_inc(ada_used, 1)

    def ada_dve(dve):
        dve.wait_ge(ada_used, done(48))
        dve.wait_ge(start_c, done(3))
        raw = M.ps[:, 0:192].rearrange("p (m s) -> p m s", s=2)
        for s in (0, 1):
            dve.tensor_tensor(M.mods[:, :, s], raw[:, :, s],
                              M.prm[:, COL["ada_b"]:COL["ada_b"] + 96], ALU.add)
        dve.drain()
        for l in (0, 1):
            for w, g in ((0, "norm1_g"), (1, "norm2_g")):
                m0 = 48 * l + 8 * (1 + 3 * w)
                for s in (0, 1):
                    c = COL[g] + 8 * l
                    dve.scalar_tensor_tensor(out=M.scg[:, l, w, s, :], in0=M.mods[:, m0:m0 + 8, s], scalar=1.0,
                                             in1=M.prm[:, c:c + 8], op0=ALU.add, op1=ALU.mult)
        for s in (0, 1):
            c = COL["conv_b_pw2"]
            dve.tensor_tensor(M.b2g1[:, s, :], M.mods[:, 16:24, s], M.prm[:, c:c + 8], ALU.mult)
        dve.drain().then_inc(mod_ready, 1)

    def scale_of(name, k, s):
        if name in ("n10", "n20", "n11", "n21"):
            l, w = int(name[2]), int(name[1]) - 1
            return M.scg[:, l, w, s, k:k + 1], M.mods[:, 48 * l + 24 * w + k, s:s + 1]
        if name == "ln":
            return M.col("conv_ln_g", k), M.col("conv_ln_b", k)
        if name == "final":
            return M.col("final_g", k), 0.0
        if name == "mix":
            return M.col("mem_norm_g_2" if s else "mix_norm_g_2", k), 0.0
        return M.col("ffn_norm_g_2", k), 0.0

    NORM_W = {"n10": TOK, "ln": TOK, "n20": TOK, "n11": TOK, "n21": SEQ, "final": SEQ, "mix": TOK,
              "ffn2_norm": SEQ}
    NORM_Q = {"n10": 0, "ln": Q0["pw2"], "n20": Q0["up00"], "n11": Q0["qkv"], "n21": Q0["up10"],
              "final": Q0["w_in"], "mix": Q0["w_in"] + 1, "ffn2_norm": Q0["up20"]}
    NORM_H = {"n10": "start", "n20": "pw2", "n11": "down01", "n21": "wo", "final": "down11",
              "mix": "final", "ffn2_norm": "w_out"}

    def norm_segs(name):
        w = NORM_W[name]
        if name == "ln":
            return [(0, 0, w)]
        return [(0, 0, SEQ)] + ([(1, SEQ, TOK)] if w == TOK else [])

    def norm_source(eng, name, k):
        if name == "ln":
            eng.wait_ge(cv_cent, done(k + 1))
            return M.cv[:, k, 0:TOK]
        if name == "n10":
            eng.wait_ge(start_c, done(3 + k + 1))
        else:
            eng.wait_ge(h_ready, done(H[NORM_H[name]] - 8 + k + 1))
            if name == "mix":
                eng.wait_ge(mem_ready, done(k + 1))
        return M.h[:, k, 0:NORM_W[name]]

    mem_ready = sem("mem_ready")
    mem_t = sem("mem_t")

    def norm_pe(pe, name):
        i, pair, w = NN[name], NORM_Q[name] % 4, NORM_W[name]
        if name == "mix":
            pe.wait_ge(mem_ready, done(KD))
        pe.wait_ge(evac, done(min(NORM_Q[name], {"final": Q0["w_in"], "mix": Q0["w_in"]}.get(name, 10**6))))
        if name == "ln":
            pair = (pair + 1) % 4
        for k in range(KD):
            pe.wait_ge(sq_ready, done(8 * i + k + 1))
            for t0, tn in ([(0, SEQ), (SEQ, CTX)] if w == TOK else [(0, SEQ)]):
                mm = pe.matmul(M.pair(pair, t0, t0 + tn), ones, M.n_sq[:, k % 2, t0:t0 + tn],
                               start=(k == 0), stop=(k == KD - 1))
            mm.then_inc(sq_used, 1)

    def norm_act(act, name):
        i, pair, w = NN[name], NORM_Q[name] % 4, NORM_W[name]
        if name == "ln":
            pair = (pair + 1) % 4
        for k in range(KD):
            src = norm_source(act, name, k)
            act.wait_ge(sq_used, done(8 * i + k - 1))
            if k < 2:
                act.wait_ge(x_ready, done(8 * i if i else 0))
                if name in ("n11", "final", "n21", "ffn2_norm"):
                    act.wait_ge(evac, done(min(NORM_Q[name], Q0["w_in"])))
            act.activation(M.n_sq[:, k % 2, 0:w], src, ACT.Square).then_inc(sq_ready, 1)
        act.wait_ge(sq_used, done(8 * i + KD))
        act.activation(M.n_y[:, 0, 0:w], M.pair(pair, 0, w), ACT.Sqrt, scale=1.0 / D, bias=eps_col)\
            .then_inc(rms_ready, 1)
        for k in range(KD):
            act.wait_ge(t_ready, done(8 * i + k + 1))
            if k >= 2:
                act.wait_ge(x_ready, done(8 * i + k - 1))
            else:
                act.wait_ge(rstd_ready, done(i + 1))
            fn = ACT.Silu if name == "ln" else ACT.Identity
            dst = M.h[:, k, :] if name == "final" else M.n_y[:, k % 2, :]
            for s, t0, t1 in norm_segs(name):
                scale, shift = scale_of(name, k, s)
                ins = act.activation(dst[:, t0:t1], M.n_t[:, k % 2, t0:t1], fn, scale=scale, bias=shift)
            if name == "final":
                ins.then_inc(y_ready, 1)
                continue
            act.drain()
            act.activation(M.x_hi[:, k, 0:w], M.n_y[:, k % 2, 0:w], ACT.Copy).then_inc(y_ready, 1)

    def norm_dve(dve, name):
        i, pair, w = NN[name], NORM_Q[name] % 4, NORM_W[name]
        if name == "ln":
            pair = (pair + 1) % 4
        dve.wait_ge(rms_ready, done(i + 1))
        dve.reciprocal(M.pair(pair, 0, w), M.n_y[:, 0, 0:w]).then_inc(rstd_ready, 1)
        dve.wait_ge(rstd_ready, done(i + 1))

        def low(k):
            dve.wait_ge(y_ready, done(8 * i + k + 1))
            if name == "final":
                dve.drain().then_inc(x_ready, 1)
                dve.drain().then_inc(h_ready, 1)
                return
            dve.tensor_tensor(M.x_lo[:, k, 0:w], M.n_y[:, k % 2, 0:w], M.x_hi[:, k, 0:w].bitcast(F32),
                              ALU.subtract).then_inc(x_ready, 1)
        for k in range(KD):
            src = norm_source(dve, name, k)
            dve.tensor_tensor(M.n_t[:, k % 2, 0:w], M.pair(pair, 0, w), src, ALU.mult).then_inc(t_ready, 1)
            if k:
                low(k - 1)
        low(KD - 1)

    def prime(eng, sems):
        for s_ in sems:
            eng.drain().then_inc(s_, LEAD)

    def count_param_dmas():
        n = 1 + 2
        for name, r in PARAM_ROWS:
            if name.endswith("norm_2") and r == 1:
                n += 2
                continue
            c = COL[name]
            n += (c + r - 1) // P - c // P + 1
        return n

    rows_out = M.at("rows_out", M.r_g, [4, D])
    out_t = sem("out_t")
    out_c = sem("out_c")
    h_count = {"start": "start", "ada": "start", "n10": "start", "pw1": "start", "ln": "start", "pw2": "pw2",
               "n20": "pw2", "ffn0": "down01", "n11": "down01", "qkv": "down01", "attn": "down01", "wo": "wo",
               "n21": "wo", "ffn1": "down11", "final": "final", "mix": "final", "w_in": "final",
               "mixers": "final", "w_out": "w_out", "ffn2_norm": "w_out", "ffn2": "down21"}

    def finish_pe(pe):
        pe.wait_ge(h_ready, done(H[h_count[order[-1]]]))
        pe.wait_ge(evac, done(q_end))
        pe.wait_ge(x_ready, done(8 * sum(st in NN for st in order)))
        for t in range(SEQ // P):
            for k in range(KD):
                mm = pe.transpose(M.pair(t, k * P, (k + 1) * P), M.h[:, k, t * P:(t + 1) * P], ident)
            mm.then_inc(out_t, 1)

    def finish_dve(dve):
        for t in range(SEQ // P):
            dve.wait_ge(out_t, done(t + 1))
            dve.tensor_copy(M.rows_out_t[:, t, :], M.pair(t, 0, D)).then_inc(out_c, 1)

    def finish_sp(sp):
        for t in range(SEQ // P):
            sp.wait_ge(out_c, done(t + 1))
            sp.dma_start(out[0, t * P:(t + 1) * P, :], M.rows_out_t[:, t, :]).then_inc(s_out, 16)
        sp.wait_ge(s_out, 16 * (SEQ // P))

    M.rows_out_t = rows_out
    eps_col = M.one[:, 0:1]
    gn_eps_col = M.one[:, 1:2]
    zero_col = M.one[:, 2:3]

    VLAT, VCTX = PAD, SEQ + 3 * PAD

    def pw1_dve(dve):
        q0 = Q0["pw1"]
        cw = COL["conv_w_dw"]
        for j in range(8):
            pair = (q0 + 2 * j) % 4
            dve.wait_ge(tile_done, done(q0 + 2 * j + 2))
            dve.wait_ge(gate_ready, done(j + 1))
            dve.wait_ge(zero_ready, done(2))
            for t0, t1, at in ((0, SEQ, VLAT), (SEQ, TOK, VCTX)):
                ins = dve.scalar_tensor_tensor(out=M.vp[:, j, at:at + t1 - t0], in0=M.pair(pair, t0, t1),
                                               scalar=M.col("conv_b_pw1", j), in1=M.gate[:, j % 2, t0:t1],
                                               op0=ALU.add, op1=ALU.mult)
            ins.then_inc(v_ready, 1)
            dve.wait_ge(v_ready, done(j + 1))
            for tap in range(TAPS):
                for n, (t0, t1, at) in enumerate(((0, SEQ, VLAT), (SEQ, TOK, VCTX))):
                    src = M.vp[:, j, at - PAD + tap:at - PAD + tap + t1 - t0]
                    w = M.prm[:, cw + tap * 8 + j:cw + tap * 8 + j + 1]
                    o = M.pair(pair, t0, t1)
                    step = 2 * (TAPS * j + tap) + n
                    if tap == 0:
                        ins = dve.tensor_scalar(o, src, w, M.col("conv_b_dw", j), ALU.mult, ALU.add)
                    else:
                        dve.wait_ge(tap_done, done(step - 1))
                        ins = dve.scalar_tensor_tensor(out=o, in0=src, scalar=w, in1=o, op0=ALU.mult, op1=ALU.add)
                    ins.then_inc(tap_done, 1)

    def pw1_act(act):
        for i in range(16):
            it, u = i // 4, i % 4
            high(act, "pw1", it, u)
            if u % 2 == 0:
                continue
            j, slot, pair_g = i // 2, (i // 2) % 2, (Q0["pw1"] + u) % 4
            act.wait_ge(tile_done, done(Q0["pw1"] + i + 1))
            if j >= 2:
                act.wait_ge(v_ready, done(j - 1))
            act.activation(M.gate[:, slot, :], M.pair(pair_g), ACT.Sigmoid,
                           bias=M.col("conv_b_pw1", j + 8)).then_inc(gate_ready, 1)
            if j:
                copy_conv(act, j - 1)
        copy_conv(act, 7)

    def copy_conv(act, j):
        pair = (Q0["pw1"] + 2 * j) % 4
        act.wait_ge(tap_done, done(2 * TAPS * (j + 1)))
        act.activation(M.cv[:, j, :], M.pair(pair), ACT.Copy).then_inc(cv_ready, 1)
        act.wait_ge(cv_ready, done(j + 1))
        act.drain().then_inc(evac, 2)

    def mean_pe(pe):
        pair = Q0["pw2"] % 4
        pe.wait_ge(evac, done(Q0["pw2"]))
        for k in range(KD):
            pe.wait_ge(cv_ready, done(k + 1))
            for t0, tn in BOTH:
                mm = pe.matmul(M.pair(pair, t0, t0 + tn), ones, M.cv[:, k, t0:t0 + tn],
                               start=(k == 0), stop=(k == KD - 1))
        mm.then_inc(mu_ready, 1)

    def mean_dve(dve):
        pair = Q0["pw2"] % 4
        dve.wait_ge(mu_ready, done(1))
        for k in range(KD):
            dve.scalar_tensor_tensor(out=M.cv[:, k, :], in0=M.pair(pair), scalar=-1.0 / D, in1=M.cv[:, k, :],
                                     op0=ALU.mult, op1=ALU.add).then_inc(cv_cent, 1)

    def pw2_act(act):
        q0 = Q0["pw2"]
        for m in range(8):
            high(act, "pw2", m // 4, m % 4)
            act.wait_ge(tile_done, done(q0 + m + 1))
            for s, (t0, tn) in enumerate(BOTH):
                o = M.pair((q0 + m) % 4, t0, t0 + tn)
                ins = act.activation(o, o, ACT.Identity, scale=M.mods[:, 16 + m, s:s + 1],
                                     bias=M.b2g1[:, s, m:m + 1])
            ins.then_inc(f_res, 1)

    def pw2_dve(dve):
        q0 = Q0["pw2"]
        for m in range(8):
            dve.wait_ge(f_res, done(m + 1))
            dve.tensor_tensor(M.h[:, m, :], M.pair((q0 + m) % 4), M.h[:, m, :], ALU.add).then_inc(evac, 1)
            dve.drain().then_inc(h_ready, 1)

    def ffn_cols(b, tap, t, hf, j):
        r = t * FT + HALF * hf
        if b == 2:
            return M.col_at("conv_b_2" if tap is None else "conv_w_2", j + ((tap or 0) * 2 * FT + r))
        if tap is None:
            return M.col_at("ffn_b_dw", j + (b * 2 * FT + r))
        return M.col_at("ffn_w_dw", j + ((b * 3 + tap) * 2 * FT + r))

    SHIFTS = {0: (-1, 0, 1), 1: (-1, 0, 1), 2: (-2, -1, 0)}

    def up_act(act, b, hf, w):
        name = f"up{b}{hf}"
        q0, g0 = Q0[name], HALF * (2 * b + hf)
        zero_tap = SHIFTS[b].index(0)
        for it, u in chunks(act, 2 * HALF):
            high(act, name, it, u)
            if u % 2 == 0:
                continue
            j, slot = 2 * it + u // 2, u // 2
            pa, pb = (q0 + u - 1) % 4, (q0 + u) % 4
            g = 2 * it + (g0 + u // 2)
            act.wait_ge(tile_done, done(q0 + 4 * it + u + 1))
            for t, pr, dst in ((0, pa, M.f_a), (1, pb, M.f_b)):
                ins = act.activation(dst[:, slot, 0:w], M.pair(pr, 0, w), ACT.Identity,
                                     scale=ffn_cols(b, zero_tap, t, hf, j), bias=ffn_cols(b, None, t, hf, j))
            ins.then_inc(mid_ready, 1)
            act.wait_ge(taps_ready, done(g + 1))
            act.activation(M.pair(pa, 0, w), M.f_a[:, slot, 0:w], ACT.Silu).then_inc(silu_ready, 1)
            act.wait_ge(prod_ready, done(g + 1))
            act.activation(M.g_hi[:, bass.ds(j, 1), 0:w], M.pair(pb, 0, w), ACT.Copy).then_inc(ghi_ready, 1)

    def up_dve(dve, b, hf, w):
        name = f"up{b}{hf}"
        q0, g0 = Q0[name], HALF * (2 * b + hf)
        segs = [(0, SEQ)] + ([(SEQ, TOK)] if w == TOK else [])
        for it, u in chunks(dve, 2 * HALF):
            if u % 2 == 0:
                continue
            j, slot = 2 * it + u // 2, u // 2
            pa, pb = (q0 + u - 1) % 4, (q0 + u) % 4
            g = 2 * it + (g0 + u // 2)
            dve.wait_ge(mid_ready, done(g + 1))
            for n, tap in enumerate(t for t in range(3) if SHIFTS[b][t]):
                sh = SHIFTS[b][tap]
                if n:
                    dve.drain()
                for t, pr, dst in ((0, pa, M.f_a), (1, pb, M.f_b)):
                    for t0, t1 in segs:
                        o0, o1 = (t0 - sh, t1) if sh < 0 else (t0, t1 - sh)
                        ins = dve.scalar_tensor_tensor(
                            out=dst[:, slot, o0:o1], in0=M.pair(pr, o0 + sh, o1 + sh),
                            scalar=ffn_cols(b, tap, t, hf, j), in1=dst[:, slot, o0:o1],
                            op0=ALU.mult, op1=ALU.add)
            ins.then_inc(taps_ready, 1)
            dve.wait_ge(silu_ready, done(g + 1))
            dve.tensor_tensor(M.pair(pb, 0, w), M.pair(pa, 0, w), M.f_b[:, slot, 0:w], ALU.mult)\
                .then_inc(prod_ready, 1)
            dve.wait_ge(ghi_ready, done(g + 1))
            dve.tensor_tensor(M.g_lo[:, bass.ds(j, 1), 0:w], M.pair(pb, 0, w),
                              M.g_hi[:, bass.ds(j, 1), 0:w].bitcast(F32), ALU.subtract).then_inc(g_ready, 1)
            dve.drain().then_inc(evac, 2)

    def plain_high(act, name):
        for it, u in chunks(act, N_CHUNKS[name]):
            high(act, name, it, u)

    def down_dve(dve, b, hf, w):
        name = f"down{b}{hf}"
        q0 = Q0[name]
        for m in range(8):
            dve.wait_ge(tile_done, done(q0 + m + 1))
            for s, (t0, tn) in enumerate(BOTH if w == TOK else LAT):
                o = M.h[:, m, t0:t0 + tn]
                src = M.pair((q0 + m) % 4, t0, t0 + tn)
                if b == 2:
                    dve.tensor_tensor(o, src, o, ALU.add)
                else:
                    dve.scalar_tensor_tensor(out=o, in0=src, scalar=M.mods[:, 48 * b + 40 + m, s:s + 1],
                                             in1=o, op0=ALU.mult, op1=ALU.add)
            dve.drain().then_inc(evac, 1)
            dve.drain().then_inc(h_ready, 1)

    class Unit:

        def __init__(self, q, keys, pieces, sink, values, out):
            self.q, self.keys, self.pieces, self.sink, self.values, self.out = q, keys, pieces, sink, values, out
            self.nk = sum(n for _, n, _, _ in pieces)

    SCALE = HD ** -0.5

    def att_pe(pe, units, n0):
        def scores(u):
            x = units[u]
            pe.wait_ge(att_m, done(n0 + max(u - 1, 0)))
            for off, n, rhs in x.keys:
                mm = pe.matmul(M.pair(u % 2, off, off + n), x.q, rhs, start=True, stop=True)
            mm.then_inc(att_s, 1)

        def turn(u):
            x = units[u]
            pe.wait_ge(att_p, done(n0 + u + 1))
            pe.wait_ge(att_c, done(n0 + max(u - 1, 0)))
            pe.wait_ge(att_e, done(n0 + max(u - 1, 0)))
            for k in range(x.nk // P):
                mm = pe.transpose(M.pair(2 + u % 2, k * P, (k + 1) * P), M.p_sb[:, u % 2, k * P:(k + 1) * P],
                                  ident)
            mm.then_inc(att_t, 1)

        def values(u):
            x = units[u]
            pe.wait_ge(att_c, done(n0 + u + 1))
            for k, v in enumerate(x.values):
                mm = pe.matmul(M.pair(2 + u % 2, 640, 640 + HD), M.pt_sb[:, u % 2, k * P:(k + 1) * P], v,
                               start=(k == 0), stop=(k == len(x.values) - 1))
            mm.then_inc(att_o, 1)

        scores(0)
        for u in range(len(units)):
            if u + 1 < len(units):
                scores(u + 1)
            turn(u)
            if u:
                values(u - 1)
        values(len(units) - 1)

    def att_dve(dve, units, n0):
        def scaled(u):
            x, b = units[u], u % 2
            dve.wait_ge(att_s, done(n0 + u + 1))
            dve.wait_ge(att_p, done(n0 + max(u - 1, 0)))
            at = 0
            for off, n, mask, _ in x.pieces:
                o, i = M.s_sb[:, b, at:at + n], M.pair(b, off, off + n)
                if mask is None:
                    dve.tensor_scalar(o, i, SCALE, None, ALU.mult)
                else:
                    dve.scalar_tensor_tensor(out=o, in0=i, scalar=SCALE, in1=mask, op0=ALU.mult, op1=ALU.add)
                at += n
            dve.drain()
            dve.tensor_reduce(M.sm_max[:, b:b + 1], M.s_sb[:, b, 0:x.nk], AX.X, ALU.max)
            dve.drain()
            if x.sink is None:
                dve.tensor_scalar(M.sm_neg[:, b:b + 1], M.sm_max[:, b:b + 1], -1.0, None, ALU.mult)\
                    .then_inc(att_m, 1)
            else:
                dve.tensor_scalar(M.sm_neg[:, b:b + 1], M.sm_max[:, b:b + 1], x.sink, -1.0, ALU.max, ALU.mult)\
                    .then_inc(att_m, 1)

        def denominator(u):
            x, b = units[u], u % 2
            dve.wait_ge(att_p, done(n0 + u + 1))
            dve.wait_ge(att_e, done(n0 + max(u - 1, 0)))
            den = M.sm_sum
            if x.sink is not None:
                den = M.sm_den
                dve.tensor_tensor(den[:, b:b + 1], M.sm_sum[:, b:b + 1], M.sm_sink[:, b:b + 1], ALU.add)
                dve.drain()
            dve.reciprocal(M.sm_rd[:, b:b + 1], den[:, b:b + 1]).then_inc(att_r, 1)

        scaled(0)
        for u in range(len(units)):
            if u + 1 < len(units):
                scaled(u + 1)
            denominator(u)

    def att_act(act, units, n0):
        def exps(u):
            x, b = units[u], u % 2
            act.wait_ge(att_m, done(n0 + u + 1))
            act.wait_ge(att_t, done(n0 + max(u - 1, 0)))
            act.wait_ge(att_r, done(n0 + max(u - 1, 0)))
            if x.sink is not None:
                act.activation(M.sm_sink[:, b:b + 1], x.sink, ACT.Exp, bias=M.sm_neg[:, b:b + 1])
            act.activation(M.p_sb[:, b, 0:x.nk], M.s_sb[:, b, 0:x.nk], ACT.Exp, bias=M.sm_neg[:, b:b + 1],
                           accum_out=M.sm_sum[:, b:b + 1]).then_inc(att_p, 1)

        def copied(u):
            x, b = units[u], u % 2
            act.wait_ge(att_t, done(n0 + u + 1))
            act.wait_ge(att_o, done(n0 + max(u - 1, 0)))
            act.activation(M.pt_sb[:, b, 0:x.nk], M.pair(2 + b, 0, x.nk), ACT.Copy).then_inc(att_c, 1)

        def divided(u):
            x, b = units[u], u % 2
            act.wait_ge(att_o, done(n0 + u + 1))
            act.wait_ge(att_r, done(n0 + u + 1))
            act.activation(x.out, M.pair(2 + b, 640, 640 + HD), ACT.Copy, scale=M.sm_rd[:, b:b + 1])\
                .then_inc(att_e, 1)

        exps(0)
        for u in range(len(units)):
            if u + 1 < len(units):
                exps(u + 1)
            copied(u)
            if u:
                divided(u - 1)
        divided(len(units) - 1)

    kf_rot, kf_low, kf_high = (M.kf[:, i * P:(i + 1) * P] for i in range(3))
    kf_cos, kf_sin = M.kf[:, 3 * P:3 * P + SEQ], M.kf[:, 3 * P + SEQ:3 * P + 2 * SEQ]
    kf_mask = 3 * P + 2 * SEQ

    def qkv_segs(it, u):
        return LAT if not isinstance(it, int) or 4 * it + u < 8 else BOTH

    def qkv_act(act):
        q0 = Q0["qkv"]
        for it, u in chunks(act, 12):
            high(act, "qkv", it, u)
            act.wait_ge(tile_done, done(q0 + 4 * it + u + 1))
            i = 4 * it + u
            pr = (q0 + u) % 4
            if not isinstance(it, int) or i < 8:
                act.activation(M.q_[:, bass.ds(i, 1), :].rearrange("p a t -> p (a t)"), M.pair(pr, 0, SEQ),
                               ACT.Copy).then_inc(evac, 1)
            else:
                dst = (M.k_ if i < 10 else M.v_)[:, i % 2, :]
                act.activation(dst, M.pair(pr), ACT.Copy).then_inc(evac, 1)

    def rope_tiles():
        return [M.q_[:, i, :] for i in range(8)] + [M.k_[:, i, 0:SEQ] for i in range(2)]

    def prep_pe(pe):
        pe.wait_ge(s_kf, 16)
        pe.wait_ge(evac, done(Q0["wo"]))
        for n, x in enumerate(rope_tiles()):
            pe.wait_ge(rope_c, done(n - 3))
            pe.matmul(M.pair(n % 4, 0, SEQ), kf_rot, x, start=True, stop=True).then_inc(rope_r, 1)
        for g in range(4):
            pe.wait_ge(rope_c, done(10))
            for t0, tn in BOTH:
                mm = pe.matmul(M.pair(g, t0, t0 + tn), (kf_low, kf_high)[g % 2], M.k_[:, g // 2, t0:t0 + tn],
                               start=True, stop=True)
            mm.then_inc(turn_t, 1)
        pe.wait_ge(turn_c, done(2))
        for t in range(6):
            for c in range(2):
                at = t * 256 + c * P
                mm = pe.transpose(M.ps[:, at:at + P], M.v_[:, c, t * P:(t + 1) * P], ident)
        mm.then_inc(turn_t, 1)

    def prep_dve(dve):
        dve.wait_ge(s_kf, 16)
        dve.wait_ge(evac, done(Q0["wo"]))
        for n, x in enumerate(rope_tiles()):
            dve.tensor_tensor(M.gate[:, n % 2, 0:SEQ], x, kf_cos, ALU.mult)
            dve.wait_ge(rope_r, done(n + 1))
            dve.tensor_tensor(M.pair(n % 4, 0, SEQ), M.pair(n % 4, 0, SEQ), kf_sin, ALU.mult)
            dve.drain()
            dve.tensor_tensor(x, M.pair(n % 4, 0, SEQ), M.gate[:, n % 2, 0:SEQ], ALU.add).then_inc(rope_c, 1)

    def prep_act(act):
        for g in range(4):
            act.wait_ge(turn_t, done(g + 1))
            act.activation(M.kd[:, g, :], M.pair(g), ACT.Copy).then_inc(turn_c, 1)
        act.wait_ge(turn_t, done(5))
        act.activation(M.vt[:, :, :].rearrange("p t c -> p (t c)"), M.ps[:, 0:1536], ACT.Copy).then_inc(turn_c, 1)

    def units1():
        out_ = []
        for i in range(4):
            lo, hi = max(i - 1, 0), min(i + 1, 3)
            nb = (hi - lo + 1) * P
            for r in range(4):
                half = HD * (r % 2)
                q = M.qg[half:half + HD, r // 2, i * P:(i + 1) * P]
                k = M.kg[half:half + HD, :]
                mask = M.kf[:, kf_mask + (lo - i + 1) * P:kf_mask + (lo - i + 1) * P + nb]
                out_.append(Unit(q, [(0, nb, k[:, lo * P:(hi + 1) * P]), (SEQ, CTX, k[:, SEQ:TOK])],
                                 [(0, nb, mask, 0), (SEQ, CTX, None, 0)], M.sinkg[:, r:r + 1],
                                 [M.vg[:, t, :] for t in list(range(lo, hi + 1)) + [4, 5]],
                                 M.o_t[:, i, r * HD:(r + 1) * HD]))
        return out_

    def attn_pe(pe):
        pe.wait_ge(turn_c, done(5))
        with pe.Fori(0, 4) as g:
            pe.wait_ge(grp_ready, done(g + 1))
            att_pe(pe, units1(), 16 * g)
            pe.wait_ge(att_e, done(16 * g + 16))
            for c in range(2):
                for i in range(4):
                    mm = pe.transpose(M.pair(0, c * SEQ + i * P, c * SEQ + (i + 1) * P),
                                      M.o_t[:, i, c * P:(c + 1) * P], ident)
            mm.then_inc(otr_t, 1)

    def attn_dve(dve):
        dve.wait_ge(turn_c, done(5))
        with dve.Fori(0, 4) as g:
            dve.wait_ge(otr_t, done(g))
            dve.tensor_copy(M.qg[:, :, :], M.q_[:, bass.ds(2 * g, 2), :])
            dve.tensor_copy(M.kg[:, :], M.kd[:, bass.ds(g, 1), :].rearrange("p a t -> p (a t)"))
            dve.tensor_copy(M.vg[:, :, :], M.vt[:, :, bass.ds(HD * g, HD)])
            dve.tensor_copy(M.sinkg[:, :], M.sinks[:, bass.ds(4 * g, 4)])
            dve.drain().then_inc(grp_ready, 1)
            att_dve(dve, units1(), 16 * g)
            dve.wait_ge(otr_h, done(g + 1))
            dve.tensor_tensor(M.x_lo[:, bass.ds(2 * g, 2), 0:SEQ], M.pair(0, 0, 1024).rearrange("p (c t) -> p c t", c=2),
                              M.x_hi[:, bass.ds(2 * g, 2), 0:SEQ].bitcast(F32), ALU.subtract)
            dve.drain().then_inc(xa_ready, 2)

    def attn_act(act):
        with act.Fori(0, 4) as g:
            att_act(act, units1(), 16 * g)
            act.wait_ge(otr_t, done(g + 1))
            act.activation(M.x_hi[:, bass.ds(2 * g, 2), 0:SEQ], M.pair(0, 0, 1024).rearrange("p (c t) -> p c t", c=2),
                           ACT.Copy).then_inc(otr_h, 1)

    def wo_dve(dve):
        q0 = Q0["wo"]
        for m in range(8):
            dve.wait_ge(tile_done, done(q0 + m + 1))
            o = M.h[:, m, 0:SEQ]
            dve.scalar_tensor_tensor(out=o, in0=M.pair((q0 + m) % 4, 0, SEQ), scalar=M.mods[:, 48 + 16 + m, 0:1],
                                     in1=o, op0=ALU.mult, op1=ALU.add).then_inc(evac, 1)
            dve.drain().then_inc(h_ready, 1)

    class Steps:

        def __init__(self, name, names):
            self.sem, self.names, self.next = sem(name), names, 0

        def after(self, eng, name):
            eng.wait_ge(self.sem, done(self.names.index(name) + 1))

        def mark(self, ins, name):
            assert self.names[self.next] == name, (self.names[self.next], name)
            self.next += 1
            ins.then_inc(self.sem, 1)

    N4, C3 = range(4), range(3)
    T_S = Steps("step_t", [f"head{i}" for i in range(8)] + ["kd", "vt", "mv", "rr", "bias", "out"]
                + [f"z{n}" for n in N4] + [f"a{c}" for c in C3] + [f"g{c}" for c in C3]
                + [x for c in C3 for x in (f"kk{c}", f"bonus{c}")]
                + [f"cum{c}" for c in C3]
                + [x for n in N4 for x in
                   [f"mat{n}", f"m0{n}"] + [f"{y}{e}{n}" for e in range(1, 7) for y in ("mt", "inv", "invt")
                                            if (y, e) != ("inv", 6)]
                   + [f"tok{n}", f"x0{n}", f"u{n}", f"y{n}"] + ([f"s{n}"] if n < 3 else []) + [f"yt{n}"]])
    S_S = Steps("step_s", [x for i in range(8) for x in (f"sq{i}", f"rms{i}")]
                + ["kd", "vt", "mv", "rr", "bias", "out", "low"]
                + [f"sig{n}" for n in N4] + [f"a{c}" for c in C3] + [f"g{c}" for c in C3]
                + [f"kk{c}" for c in C3]
                + [x for c in C3 for x in (f"cend{c}", f"exp{c}")] + ["ez"]
                + [x for n in N4 for x in [f"mt{e}{n}" for e in range(1, 7)]
                   + [f"tok{n}", f"x0{n}", f"u{n}", f"sd{n}", f"yt{n}", f"hi{n}"]])
    V_S = Steps("step_v", [f"head{i}" for i in range(8)] + ["out"] + ["shift"] + [f"z{n}" for n in N4]
                + [x for c in C3 for x in (f"kk{c}", f"rk{c}", f"kn{c}", f"bonus{c}")]
                + [x for c in C3 for x in (f"cend{c}", f"abc{c}")] + ["ezs"]
                + [x for n in N4 for x in
                   [f"mask{n}", f"lv0{n}", f"inv0{n}"] + [y for e in range(1, 7) for y in (f"lv{e}{n}", f"inv{e}{n}")]
                   + ([f"st{n}"] if n < 3 else []) + [f"var{n}", f"yn{n}", f"y3{n}", f"lo{n}"]])
    s_k2 = sem("s_k2", False)
    s_rr = sem("s_rr", False)
    s_tz = sem("s_tz", False)

    k_low, k_high, k_anti = (M.ks[:, i * P:(i + 1) * P] for i in range(3))
    k_tri = M.ks[:, 3 * P:5 * P]
    k_mask4 = M.ks[:, 5 * P:9 * P]

    def k_level(e):
        return M.ks[:, (9 + e) * P:(10 + e) * P]

    rr_dram = nc.dram_tensor("rr_scratch", (6, 384), F32, kind="Internal").ap()

    def tables_act(act):
        act.wait_ge(tile_done, done(Q0["w_in"]))
        act.wait_ge(g_ready, done(4 * HALF))
        act.dma_start(M.m_rows[:, :, :], A["mem_2"][0].rearrange("(t p) d -> p t d", p=P)).then_inc(s_mem, 16)
        act.dma_start(M.ks[:, :], A["k_second"]).then_inc(s_k2, 16)
        act.dma_start(M.lw[0:32, :], A["rwkv_w2_2"][0]).then_inc(s_k2, 16)
        act.dma_start(M.lw[32:64, :], A["rwkv_a2_2"][0]).then_inc(s_k2, 16)
        act.dma_start(M.lw[64:128, :], A["rwkv_g2_2"][0]).then_inc(s_k2, 16)
        act.dma_start(M.w0b[:, :], A["rwkv_w0_2"][0:1, :].to_broadcast([P, 384])).then_inc(s_k2, 16)
        act.dma_start(M.hot[:, :], A["k_hot"]).then_inc(s_k2, 16)
        act.activation(M.relb[:, :], M.kb[:, P:P + 8], ACT.Copy)
        act.drain()
        act.dma_start(M.relb[0:32, 0:6], A["rel_bias_2"]).then_inc(s_k2, 16)

    def mem_pe(pe):
        pe.wait_ge(s_mem, 16)
        pe.wait_ge(x_ready, done(8 * (NN["final"] + 1)))
        for k in range(KD):
            pe.wait_ge(mem_ready, done(k - 3))
            for t in range(2):
                mm = pe.transpose(M.pair(k % 4, t * P, (t + 1) * P), M.m_rows[:, t, k * P:(k + 1) * P], ident)
            mm.then_inc(mem_t, 1)

    def mem_act(act):
        for k in range(KD):
            act.wait_ge(mem_t, done(k + 1))
            act.activation(M.h[:, k, SEQ:TOK], M.pair(k % 4, 0, CTX), ACT.Copy).then_inc(mem_ready, 1)

    def w_in_act(act):
        for name, n, w0_, w1_ in (("w_in", 17, 0, SEQ), ("mem_kv", 4, SEQ, TOK)):
            for it, u in chunks(act, n):
                high(act, name, it, u)
                act.wait_ge(tile_done, done(Q0[name] + 4 * it + u + 1))
                if name == "w_in":
                    dst = M.pj[:, bass.ds(4 * it + u, 1), :].rearrange("p a t -> p (a t)")
                else:
                    dst = M.mkv[:, 4 * it + u, :]
                act.activation(dst, M.pair((Q0[name] + u) % 4, w0_, w1_), ACT.Copy).then_inc(evac, 1)

    def head_tiles():
        return ([(M.pj[:, i, :], SEQ, "attn_q_norm_2") for i in range(3)] + [(M.pj[:, 3, :], SEQ, "attn_k_norm_2")]
                + [(M.pj[:, i, :], SEQ, "mem_q_norm_2") for i in (15, 16)]
                + [(M.mkv[:, i, :], CTX, "mem_k_norm_2") for i in (0, 1)])

    def mix_prep_pe(pe):
        pe.wait_ge(evac, done(Q0["w_out"]))
        pe.wait_ge(s_k2, 16 * 7)
        for i, (x, w, _) in enumerate(head_tiles()):
            S_S.after(pe, f"sq{i}")
            if i >= 4:
                V_S.after(pe, f"head{i - 4}")
            T_S.mark(pe.matmul(M.pair(i % 4, 0, w), head1, M.n_sq[:, i % 2, 0:w], start=True, stop=True), f"head{i}")
        V_S.after(pe, "head7")
        for g in (0, 1):
            mm = pe.matmul(M.ps[:, g * SEQ:(g + 1) * SEQ], (k_low, k_high)[g], M.pj[:, 3, :], start=True, stop=True)
        T_S.mark(mm, "kd")
        for t in range(4):
            mm = pe.transpose(M.pair(1, t * P, (t + 1) * P), M.pj[:, 4, t * P:(t + 1) * P], ident)
        T_S.mark(mm, "vt")
        for t in range(2):
            for c in range(2):
                at = t * 256 + c * P
                mm = pe.transpose(M.pair(2, at, at + P), M.mkv[:, 2 + c, t * P:(t + 1) * P], ident)
        T_S.mark(mm, "mv")
        T_S.mark(pe.matmul(M.ps[0:6, 3072:3072 + 384], M.relb[0:33, 0:6], M.hot[0:33, :], start=True, stop=True), "rr")
        pe.wait_ge(s_tz, 16)
        S_S.after(pe, "rr")
        for n in range(3):
            mm = pe.matmul(M.ps[:, 2048 + n * 512:2560 + n * 512], k_anti,
                           M.tz[:, 2 * n:2 * n + 2, :].rearrange("p h k -> p (h k)"), start=True, stop=True)
        T_S.mark(mm, "bias")

    def mix_prep_act(act):
        act.wait_ge(evac, done(Q0["w_out"]))
        tiles = head_tiles()
        def square(i):
            x, w, _ = tiles[i]
            if i >= 2:
                T_S.after(act, f"head{i - 2}")
            S_S.mark(act.activation(M.n_sq[:, i % 2, 0:w], x, ACT.Square), f"sq{i}")
        for i, (x, w, _) in enumerate(tiles):
            square(i)
            T_S.after(act, f"head{i}")
            if i >= 2:
                V_S.after(act, f"head{i - 2}")
            S_S.mark(act.activation(M.n_t[:, i % 2, 0:w], M.pair(i % 4, 0, w), ACT.Sqrt, scale=1.0 / HD,
                                    bias=eps_col), f"rms{i}")
        T_S.after(act, "kd")
        V_S.after(act, "head7")
        S_S.mark(act.activation(M.qg[:, :, :].rearrange("p g t -> p (g t)"), M.ps[:, 0:1024], ACT.Copy), "kd")
        T_S.after(act, "vt")
        S_S.mark(act.activation(M.kg[:, 0:SEQ], M.pair(1, 0, SEQ), ACT.Copy), "vt")
        T_S.after(act, "mv")
        S_S.mark(act.activation(M.pj[:, 3, :], M.pair(2, 0, SEQ), ACT.Copy), "mv")
        T_S.after(act, "rr")
        S_S.mark(act.activation(M.rr[0:6, :], M.ps[0:6, 3072:3072 + 384], ACT.Copy), "rr")
        S_S.after(act, "rr")
        act.dma_start(rr_dram, M.rr[0:6, :]).then_inc(s_rr, 16)
        act.wait_ge(s_rr, 16)
        skew = bass.AP(rr_dram.tensor, 0, [[1, P], [384, 6], [1, 2 * P]])
        act.dma_start(M.tz[:, :, :], skew).then_inc(s_tz, 16)
        T_S.after(act, "bias")
        S_S.mark(act.activation(M.bias[:, :, :].rearrange("p h k -> p (h k)"), M.ps[:, 2048:2048 + 1536], ACT.Copy),
                 "bias")

    def mix_prep_dve(dve):
        dve.wait_ge(evac, done(Q0["w_out"]))
        for i, (x, w, gain) in enumerate(head_tiles()):
            S_S.after(dve, f"rms{i}")
            dve.reciprocal(M.pair(i % 4, 0, w), M.n_t[:, i % 2, 0:w])
            dve.drain()
            V_S.mark(dve.scalar_tensor_tensor(out=x, in0=x, scalar=M.col(gain), in1=M.pair(i % 4, 0, w),
                                              op0=ALU.mult, op1=ALU.mult), f"head{i}")

    def units2():
        out_ = []
        for i in range(4):
            lo = max(i - 1, 0)
            nb = (i - lo + 1) * P
            for hh in range(6):
                half, g = HD * (hh % 2), hh // 3
                out_.append(Unit(M.pj[half:half + HD, hh // 2, i * P:(i + 1) * P],
                                 [(0, nb, M.qg[half:half + HD, g, lo * P:(i + 1) * P])],
                                 [(0, nb, M.bias[:, hh, 2 * P - nb:2 * P], 0)], M.sinks[:, 16 + hh:17 + hh],
                                 [M.kg[:, t * P + g * HD:t * P + (g + 1) * HD] for t in range(lo, i + 1)],
                                 M.h[:, 2 * i + hh // 4, SEQ + (hh % 4) * HD:SEQ + (hh % 4 + 1) * HD]))
        for i in range(4):
            for hh in range(4):
                half = HD * (hh % 2)
                out_.append(Unit(M.pj[half:half + HD, 15 + hh // 2, i * P:(i + 1) * P],
                                 [(0, CTX, M.mkv[half:half + HD, hh // 2, :])], [(0, CTX, None, 0)], None,
                                 [M.pj[:, 3, t * 256 + hh * HD:t * 256 + (hh + 1) * HD] for t in range(2)],
                                 M.o_t[:, i, hh * HD:(hh + 1) * HD]))
        return out_

    OUT_TILES = [0, 1, 2, 6, 7]

    def mix_out_pe(pe):
        pe.wait_ge(att_e, done(64 + 40))
        for n in range(5):
            for i in range(4):
                src = M.h[:, 2 * i + n // 2, SEQ + (n % 2) * P:SEQ + (n % 2 + 1) * P] if n < 3 \
                    else M.o_t[:, i, (n - 3) * P:(n - 2) * P]
                mm = pe.transpose(M.ps[:, n * 512 + i * P:n * 512 + (i + 1) * P], src, ident)
        T_S.mark(mm, "out")

    def mix_out_act(act):
        T_S.after(act, "out")
        for n, c in enumerate(OUT_TILES):
            ins = act.activation(M.x_hi[:, c, 0:SEQ], M.ps[:, n * 512:(n + 1) * 512], ACT.Copy)
        S_S.mark(ins, "out")

    def mix_out_dve(dve):
        S_S.after(dve, "out")
        for n, c in enumerate(OUT_TILES):
            ins = dve.tensor_tensor(M.x_lo[:, c, 0:SEQ], M.ps[:, n * 512:(n + 1) * 512],
                                    M.x_hi[:, c, 0:SEQ].bitcast(F32), ALU.subtract)
        V_S.mark(ins, "out")

    r_t = [M.pj[:, 5 + c, :] for c in C3]
    k_t = [M.pj[:, 8 + c, :] for c in C3]
    v_t = [M.pj[:, 11 + c, :] for c in C3]
    lor = M.pj[:, 14, :]
    g_t = [M.pj[:, c, :] for c in C3]
    kk_t = [M.pj[:, 3, :], M.pj[:, 4, :], M.pj[:, 15, :]]
    a_t = [M.av[:, c, :] for c in C3]
    bonus_t = [M.h[:, 2 * c:2 * c + 2, SEQ:TOK] for c in C3]
    H6 = range(6)

    def two(ap):
        return ap.rearrange("p (a b) -> p a b", a=2)

    def rw_pre_dve(dve):
        for i in range(10):
            x, d = M.pj[:, 5 + i, :], M.dd[:, i % 2, :]
            dve.tensor_tensor(d[:, 1:SEQ], x[:, 0:SEQ - 1], x[:, 1:SEQ], ALU.subtract)
            dve.tensor_scalar(d[:, 0:1], x[:, 0:1], -1.0, None, ALU.mult)
            dve.drain()
            ins = dve.scalar_tensor_tensor(out=x, in0=d, scalar=M.col("rwkv_mu_2", i), in1=x, op0=ALU.mult, op1=ALU.add)
        V_S.mark(ins, "shift")
        for n in N4:
            T_S.after(dve, f"z{n}")
            V_S.mark(dve.tensor_tensor(M.sig[:, n, :], M.pair(n, 0, 384), M.w0b[:, :], ALU.add), f"z{n}")
        for c in C3:
            dve.tensor_scalar(kk_t[c], k_t[c], M.col("rwkv_k_k_2", c), None, ALU.mult)
            dve.drain()
            V_S.mark(dve.tensor_tensor(M.hq[:, 0, :], kk_t[c], kk_t[c], ALU.mult), f"kk{c}")
            S_S.after(dve, f"a{c}")
            dve.tensor_scalar(M.dd[:, 0, :], a_t[c], 1.0, M.col("rwkv_k_a_2", c), ALU.subtract, ALU.mult)
            dve.drain()
            dve.scalar_tensor_tensor(out=k_t[c], in0=M.dd[:, 0, :], scalar=1.0, in1=k_t[c], op0=ALU.add, op1=ALU.mult)
            dve.drain()
            V_S.mark(dve.scalar_tensor_tensor(out=M.hq[:, 1, :], in0=r_t[c], scalar=M.col("rwkv_r_k_2", c),
                                              in1=k_t[c], op0=ALU.mult, op1=ALU.mult), f"rk{c}")
            S_S.after(dve, f"kk{c}")
            dve.tensor_scalar(M.dd[:, 1, :], M.dd[:, 1, :], L2_EPS, None, ALU.max)
            dve.drain()
            dve.reciprocal(M.dd[:, 1, :], M.dd[:, 1, :])
            dve.drain()
            V_S.mark(dve.tensor_tensor(kk_t[c], kk_t[c], M.dd[:, 1, :], ALU.mult), f"kn{c}")
            T_S.after(dve, f"bonus{c}")
            V_S.mark(dve.tensor_tensor(bonus_t[c], two(M.pair(1, 0, SEQ)), two(v_t[c]), ALU.mult), f"bonus{c}")
        for c in C3:
            S_S.after(dve, f"cend{c}")
            V_S.mark(dve.tensor_scalar(M.cend[:, 1, c, :], M.cend[:, 0, c, :], -1.0, None, ALU.mult), f"cend{c}")
            S_S.after(dve, f"exp{c}")
            dve.tensor_tensor(a_t[c], a_t[c], kk_t[c], ALU.mult)
            dve.tensor_tensor(r_t[c], r_t[c], M.ex[:, 0, :], ALU.mult)
            dve.tensor_tensor(k_t[c], k_t[c], M.ex[:, 2, :], ALU.mult)
            dve.drain()
            dve.scalar_tensor_tensor(out=kk_t[c], in0=kk_t[c], scalar=-1.0, in1=M.ex[:, 1, :],
                                     op0=ALU.mult, op1=ALU.mult)
            dve.tensor_tensor(a_t[c], a_t[c], M.ex[:, 2, :], ALU.mult)
            V_S.mark(dve.drain(), f"abc{c}")
        V_S.mark(dve.tensor_tensor(M.cend[:, 2, :, 0:3], M.cend[:, 0, :, 0:3], M.cend[:, 0, :, 1:4], ALU.add), "ezs")

    def rw_pre_act(act):
        V_S.after(act, "shift")
        act.activation(lor[0:32, :], lor[0:32, :], ACT.Tanh)
        S_S.mark(act.activation(lor[64:128, :], lor[64:128, :], ACT.Sigmoid), "low")
        for n in N4:
            V_S.after(act, f"z{n}")
            S_S.mark(act.activation(M.sig[:, n, :], M.sig[:, n, :], ACT.Sigmoid), f"sig{n}")
        for c in C3:
            T_S.after(act, f"a{c}")
            S_S.mark(act.activation(a_t[c], M.pair(c, 0, SEQ), ACT.Sigmoid, bias=M.col("rwkv_a0_2", c)), f"a{c}")
        for c in C3:
            T_S.after(act, f"g{c}")
            S_S.mark(act.activation(g_t[c], M.pair(c, SEQ, 2 * SEQ), ACT.Copy), f"g{c}")
        for c in C3:
            T_S.after(act, f"kk{c}")
            if c:
                V_S.after(act, f"kn{c - 1}")
            V_S.after(act, f"rk{c}")
            S_S.mark(act.activation(M.dd[:, 1, :], M.pair(0, 0, SEQ), ACT.Sqrt), f"kk{c}")
        for c in C3:
            T_S.after(act, f"cum{c}")
            if c:
                V_S.after(act, f"abc{c - 1}")
            ps = M.pair(2 * (c % 2) if c < 2 else 0, 0, 1024).rearrange("p (n s t) -> p n s t", n=4, s=2)
            S_S.mark(act.activation(M.cend[:, 0, c, :], ps[:, :, 0, P - 1], ACT.Copy, scale=KAPPA / 2), f"cend{c}")
            V_S.after(act, f"cend{c}")
            for n in N4:
                t = slice(n * P, (n + 1) * P)
                plus, minus = M.cend[:, 0, c, n:n + 1], M.cend[:, 1, c, n:n + 1]
                act.activation(M.ex[:, 0, t], ps[:, n, 0, :], ACT.Exp, scale=-KAPPA, bias=plus)
                act.activation(M.ex[:, 1, t], ps[:, n, 1, :], ACT.Exp, scale=-KAPPA, bias=plus)
                ins = act.activation(M.ex[:, 2, t], ps[:, n, 0, :], ACT.Exp, scale=KAPPA, bias=minus)
            S_S.mark(ins, f"exp{c}")
        V_S.after(act, "ezs")
        S_S.mark(act.activation(M.cend[:, 3, :, 0:3], M.cend[:, 2, :, 0:3], ACT.Exp, scale=-1.0), "ez")

    def rw_pre_pe(pe):
        S_S.after(pe, "low")
        V_S.after(pe, "out")
        for n in N4:
            T_S.mark(pe.matmul(M.pair(n, 0, 384), lor[0:32, n * P:(n + 1) * P], M.lw[0:32, :], start=True, stop=True),
                     f"z{n}")
        for c in C3:
            V_S.after(pe, f"z{c}")
            T_S.mark(pe.matmul(M.pair(c, 0, SEQ), M.lw[32:64, c * P:(c + 1) * P], lor[32:64, :], start=True, stop=True),
                     f"a{c}")
        for c in C3:
            T_S.mark(pe.matmul(M.pair(c, SEQ, 2 * SEQ), M.lw[64:128, c * P:(c + 1) * P], lor[64:128, :],
                               start=True, stop=True), f"g{c}")
        for c in C3:
            V_S.after(pe, f"kk{c}")
            S_S.after(pe, f"a0" if c == 0 else f"kk{c - 1}")
            T_S.mark(pe.matmul(M.pair(0, 0, SEQ), head1, M.hq[:, 0, :], start=True, stop=True), f"kk{c}")
            V_S.after(pe, f"rk{c}")
            S_S.after(pe, "a1")
            if c:
                V_S.after(pe, f"bonus{c - 1}")
            T_S.mark(pe.matmul(M.pair(1, 0, SEQ), head1, M.hq[:, 1, :], start=True, stop=True), f"bonus{c}")
        for c in C3:
            V_S.after(pe, "bonus2")
            S_S.after(pe, "g2" if c < 2 else "exp0")
            pr = 2 * (c % 2) if c < 2 else 0
            if c == 0:
                S_S.after(pe, "kk2")
            for n in N4:
                mm = pe.matmul(M.pair(pr, n * 256, (n + 1) * 256), M.sig[:, n, c * P:(c + 1) * P], k_tri,
                               start=True, stop=True)
            T_S.mark(mm, f"cum{c}")

    def head_rows(hh):
        return slice(HD * (hh % 2), HD * (hh % 2) + HD)

    X0_BANKS, Y_BANKS = (7, 3), (1, 4)

    def by_parity(banks, hh):
        at = banks[hh % 2] * 512 + (hh // 2) * HD
        return M.ps[:, at:at + HD]

    def of_parity(ap, p):
        return ap.rearrange("p (c a x) -> p a c x", c=3, a=2)[:, p, :, :]

    def rw_pe(pe):
        for n in N4:
            t = slice(n * P, (n + 1) * P)
            if n == 0:
                V_S.after(pe, "ezs")
            else:
                V_S.after(pe, f"lo{n - 1}")
            for hh in H6:
                r, c = head_rows(hh), hh // 2
                for q_, (lhs, rhs) in enumerate(((a_t, kk_t), (a_t, r_t), (k_t, kk_t), (k_t, r_t))):
                    at = hh * 512 + q_ * P
                    mm = pe.matmul(M.ps[:, at:at + P], lhs[c][r, t], rhs[c][r, t], start=True, stop=True)
            T_S.mark(mm, f"mat{n}")
            V_S.after(pe, f"lv0{n}")
            for hh in H6:
                mm = pe.transpose(M.pair(3, hh * P, (hh + 1) * P), M.lv[:, hh, :], ident)
            T_S.mark(mm, f"m0{n}")
            for e in range(1, 7):
                V_S.after(pe, f"inv{e - 1}{n}")
                V_S.after(pe, f"lv{e}{n}")
                for hh in H6:
                    mm = pe.matmul(M.pair(3, hh * P, (hh + 1) * P), M.lv[:, hh, :], M.inv[:, hh, :],
                                   start=True, stop=True)
                T_S.mark(mm, f"mt{e}{n}")
                S_S.after(pe, f"mt{e}{n}")
                if e < 6:
                    for hh in H6:
                        mm = pe.matmul(M.pair(0, hh * P, (hh + 1) * P), M.inv_t[:, hh, :], M.mt[:, hh, :],
                                       start=True, stop=True)
                    T_S.mark(mm, f"inv{e}{n}")
                for hh in H6:
                    mm = pe.matmul(M.pair(1, hh * P, (hh + 1) * P), M.mt[:, hh, :], M.inv_t[:, hh, :],
                                   start=True, stop=True)
                T_S.mark(mm, f"invt{e}{n}")
            S_S.after(pe, f"mt6{n}")
            for q_, src in enumerate((a_t, k_t, v_t)):
                for c in C3:
                    at = 2048 + (3 * q_ + c) * P
                    mm = pe.transpose(M.ps[:, at:at + P], src[c][:, t], ident)
            T_S.mark(mm, f"tok{n}")
            S_S.after(pe, f"tok{n}")
            V_S.after(pe, f"inv6{n}")
            if n:
                V_S.after(pe, f"st{n - 1}")
            for hh in H6:
                r, c = head_rows(hh), hh // 2
                o = by_parity(X0_BANKS, hh)
                mm = pe.matmul(o, M.m4[:, hh, 2 * P:3 * P], M.tok[:, 2, hh * HD:(hh + 1) * HD],
                               start=True, stop=(n == 0))
                if n:
                    mm = pe.matmul(o, kk_t[c][r, t], M.z[r, c, :], start=False, stop=True)
            T_S.mark(mm, f"x0{n}")
            S_S.after(pe, f"x0{n}")
            for hh in H6:
                mm = pe.matmul(M.ps[:, hh * HD:(hh + 1) * HD], M.inv_t[:, hh, :], M.x0[:, hh * HD:(hh + 1) * HD],
                               start=True, stop=True)
            T_S.mark(mm, f"u{n}")
            S_S.after(pe, f"u{n}")
            for hh in H6:
                r, c = head_rows(hh), hh // 2
                o = by_parity(Y_BANKS, hh)
                pe.matmul(o, M.m4[:, hh, 3 * P:4 * P], M.tok[:, 2, hh * HD:(hh + 1) * HD], start=True, stop=False)
                mm = pe.matmul(o, M.m4[:, hh, P:2 * P], M.u[:, hh * HD:(hh + 1) * HD], start=False, stop=(n == 0))
                if n:
                    mm = pe.matmul(o, r_t[c][r, t], M.z[r, c, :], start=False, stop=True)
            T_S.mark(mm, f"y{n}")
            if n < 3:
                for hh in H6:
                    r, c = head_rows(hh), hh // 2
                    o = M.ps[r, 1024 + c * HD:1024 + (c + 1) * HD]
                    pe.matmul(o, M.tok[:, 0, hh * HD:(hh + 1) * HD], M.u[:, hh * HD:(hh + 1) * HD],
                              start=True, stop=False)
                    mm = pe.matmul(o, M.tok[:, 1, hh * HD:(hh + 1) * HD], M.tok[:, 2, hh * HD:(hh + 1) * HD],
                                   start=False, stop=True)
                T_S.mark(mm, f"s{n}")
            V_S.after(pe, f"yn{n}")
            for c in C3:
                mm = pe.transpose(M.ps[:, 1536 + c * P:1536 + (c + 1) * P], M.y[:, c * P:(c + 1) * P], ident)
            T_S.mark(mm, f"yt{n}")

    def heads3(ap):
        return ap.rearrange("p (h x) -> p h x", h=6)

    def rw_act(act):
        for n in N4:
            for e in range(1, 7):
                T_S.after(act, f"mt{e}{n}")
                S_S.mark(act.activation(M.mt[:, :, :].rearrange("p h x -> p (h x)"), M.pair(3), ACT.Copy), f"mt{e}{n}")
            T_S.after(act, f"tok{n}")
            S_S.mark(act.activation(M.tok[:, :, :].rearrange("p a x -> p (a x)"), M.ps[:, 2048:2048 + 1152], ACT.Copy),
                     f"tok{n}")
            T_S.after(act, f"x0{n}")
            for p in (0, 1):
                b = X0_BANKS[p] * 512
                ins = act.activation(of_parity(M.x0[:, :], p), M.ps[:, b:b + 192].rearrange("p (c x) -> p c x", c=3),
                                     ACT.Copy)
            S_S.mark(ins, f"x0{n}")
            T_S.after(act, f"u{n}")
            S_S.mark(act.activation(M.u[:, :], M.ps[:, 0:384], ACT.Copy), f"u{n}")
            V_S.after(act, f"var{n}")
            S_S.mark(act.activation(M.gn[:, 2, :], M.gn[:, 1, :], ACT.Sqrt, scale=1.0 / HD, bias=gn_eps_col), f"sd{n}")
            T_S.after(act, f"yt{n}")
            for c in C3:
                ins = act.activation(M.y1[:, c, :], M.ps[:, 1536 + c * P:1536 + (c + 1) * P], ACT.Identity,
                                     scale=M.col("rwkv_ln_w_2", c), bias=M.col("rwkv_ln_b_2", c))
            S_S.mark(ins, f"yt{n}")
            V_S.after(act, f"y3{n}")
            S_S.mark(act.activation(M.x_hi[:, 3:6, n * P:(n + 1) * P], M.y1[:, :, :], ACT.Copy), f"hi{n}")

    def rw_dve(dve):
        inv, inv_t = (x[:, :, :] for x in (M.inv, M.inv_t))
        eye6 = ident.unsqueeze(1).to_broadcast([P, 6, P])

        def level(e, n):
            V_S.mark(dve.tensor_tensor(M.lv[:, :, :], M.m4[:, :, 0:P], k_level(e).unsqueeze(1).to_broadcast([P, 6, P]),
                                       ALU.mult), f"lv{e}{n}")

        dve.wait_ge(zero_ready, done(3))
        for n in N4:
            T_S.after(dve, f"mat{n}")
            V_S.mark(dve.copy_predicated(M.m4[:, :, :], k_mask4.bitcast(U32).unsqueeze(1).to_broadcast([P, 6, 512]),
                                         M.ps[:, 0:3072].rearrange("p (h x) -> p h x", h=6)), f"mask{n}")
            V_S.after(dve, f"mask{n}")
            level(0, n)
            V_S.after(dve, f"lv0{n}")
            dve.tensor_tensor(inv_t, M.lv[:, :, :], eye6, ALU.add)
            T_S.after(dve, f"m0{n}")
            dve.tensor_tensor(inv, M.pair(3).rearrange("p (h x) -> p h x", h=6), eye6, ALU.add)
            V_S.mark(dve.drain(), f"inv0{n}")
            for e in range(1, 7):
                if e == 1:
                    level(e, n)
                T_S.after(dve, f"invt{e}{n}")
                if e < 6:
                    dve.tensor_tensor(inv, M.pair(0).rearrange("p (h x) -> p h x", h=6), inv, ALU.add)
                dve.tensor_tensor(inv_t, M.pair(1).rearrange("p (h x) -> p h x", h=6), inv_t, ALU.add)
                V_S.mark(dve.drain(), f"inv{e}{n}")
                if e < 6:
                    level(e + 1, n)
            if n < 3:
                T_S.after(dve, f"s{n}")
                ps_s = M.ps[:, 1024:1024 + 192].rearrange("p (c x) -> p c x", c=3)
                if n:
                    dve.tensor_tensor(M.z[:, :, :], ps_s, M.z[:, :, :], ALU.add)
                    dve.drain()
                for c in C3:
                    src = M.z[:, c, :] if n else ps_s[:, c, :]
                    ins = dve.tensor_scalar(M.z[:, c, :], src, M.cend[:, 3, c, n:n + 1], None, ALU.mult)
                V_S.mark(ins, f"st{n}")
            else:
                T_S.after(dve, f"y{n}")
            y3, q3 = heads3(M.y[:, :]), heads3(M.ysq[:, :])
            def over_head(i):
                return M.gn[:, i, :].unsqueeze(2).to_broadcast([P, 6, HD])
            y_ps = [M.ps[:, b * 512:b * 512 + 192].rearrange("p (c x) -> p c x", c=3) for b in Y_BANKS]
            for p in (0, 1):
                dve.tensor_reduce(M.gn[:, 0, p:6:2], y_ps[p], AX.X, ALU.add)
            dve.drain()
            dve.tensor_scalar(M.gn[:, 0, :], M.gn[:, 0, :], -1.0 / HD, None, ALU.mult)
            dve.drain()
            for p in (0, 1):
                dve.tensor_tensor(of_parity(M.y[:, :], p), y_ps[p],
                                  M.gn[:, 0, p:6:2].unsqueeze(2).to_broadcast([P, 3, HD]), ALU.add)
            dve.drain()
            dve.tensor_tensor(q3, y3, y3, ALU.mult)
            dve.drain()
            V_S.mark(dve.tensor_reduce(M.gn[:, 1, :], q3, AX.X, ALU.add), f"var{n}")
            S_S.after(dve, f"sd{n}")
            dve.reciprocal(M.gn[:, 3, :], M.gn[:, 2, :])
            dve.drain()
            V_S.mark(dve.tensor_tensor(y3, y3, over_head(3), ALU.mult), f"yn{n}")
            S_S.after(dve, f"yt{n}")
            for c in C3:
                b = M.h[:, 2 * c + n // 2, SEQ + (n % 2) * P:SEQ + (n % 2 + 1) * P]
                dve.tensor_tensor(M.y1[:, c, :], M.y1[:, c, :], b, ALU.add)
            dve.drain()
            V_S.mark(dve.tensor_tensor(M.y1[:, :, :], M.y1[:, :, :], M.pj[:, 0:3, n * P:(n + 1) * P], ALU.mult), f"y3{n}")
            S_S.after(dve, f"hi{n}")
            V_S.mark(dve.tensor_tensor(M.x_lo[:, 3:6, n * P:(n + 1) * P], M.y1[:, :, :],
                                       M.x_hi[:, 3:6, n * P:(n + 1) * P].bitcast(F32), ALU.subtract), f"lo{n}")

    def w_out_dve(dve):
        q0 = Q0["w_out"]
        for m in range(8):
            dve.wait_ge(tile_done, done(q0 + m + 1))
            o = M.h[:, m, 0:SEQ]
            dve.tensor_tensor(o, M.pair((q0 + m) % 4, 0, SEQ), o, ALU.add).then_inc(evac, 1)
            dve.drain().then_inc(h_ready, 1)

    M.n_param_dma = count_param_dmas()
    block = ctx.enter_context(nc.Block())

    if True:
        @block.sync
        def _(sp):
            prime(sp, [])
            start_sp(sp)
            if "ada" in order:
                ada_sp(sp)
            for name in used_streams:
                load_stream(sp, name)
                if name == "qkv":
                    sp.wait_ge(tile_done, done(Q0["qkv"] + 1))
                    sp.dma_start(M.kf[:, :], A["k_first"]).then_inc(s_kf, 16)
            finish_sp(sp)

        @block.gpsimd
        def _(pool):
            prime(pool, [lo_ready, zero_ready])
            pool.memset(M.p_rows[:, PT - 1, :], 0.0)
            pool.memset(M.one[:, 0:1], EPS)
            pool.memset(M.one[:, 1:2], GN_EPS)
            pool.memset(M.one[:, 2:8], 0.0)
            pool.drain().then_inc(zero_ready, 1)
            if "pw1" in order:
                pool.wait_ge(start_c, done(3 + KD))
                pool.memset(M.vp[:, :, :], 0.0).then_inc(zero_ready, 1)
            for name in used_streams:
                if name == "w_out":
                    V_S.after(pool, "abc2")
                    pool.memset(M.m4[:, :, :], 0.0).then_inc(zero_ready, 1)
                low_stream(pool, name)

        @block.scalar
        def _(act):
            prime(act, [hi_ready, start_c, sc_ready, sq_ready, rms_ready, y_ready, gate_ready, cv_ready,
                        mid_ready, silu_ready, ghi_ready, f_res, mem_ready, turn_c, att_p, att_c, att_e, otr_h, S_S.sem])
            act.wait_ge(zero_ready, done(1))
            start_act(act)
            if q_end:
                high_first(act)
            act.wait_ge(mod_ready, done(1))
            for st in order:
                if st == "final":
                    tables_act(act)
                if st == "mix":
                    mem_act(act)
                if st in NN:
                    norm_act(act, st)
                if st == "w_in":
                    w_in_act(act)
                if st == "mixers":
                    mix_prep_act(act)
                    att_act(act, units2(), 64)
                    mix_out_act(act)
                    rw_pre_act(act)
                    rw_act(act)
                if st == "w_out":
                    plain_high(act, "w_out")
                if st == "pw1":
                    pw1_act(act)
                if st == "pw2":
                    pw2_act(act)
                if st == "qkv":
                    qkv_act(act)
                if st == "attn":
                    prep_act(act)
                    attn_act(act)
                if st == "wo":
                    plain_high(act, "wo")
                if st in ("ffn0", "ffn1", "ffn2"):
                    b, w = int(st[3]), TOK if st == "ffn0" else SEQ
                    for hf in (0, 1):
                        up_act(act, b, hf, w)
                        plain_high(act, f"down{b}{hf}")

        @block.tensor
        def _(pe):
            prime(pe, [tile_done, ada_used, start_t, sq_used, mu_ready, mem_t, out_t, rope_r, turn_t, att_s, att_t, att_o, otr_t, T_S.sem])
            start_pe(pe)
            ada_pe(pe)
            pe.wait_ge(mod_ready, done(1))
            for st in order:
                if st == "ln":
                    mean_pe(pe)
                if st == "mix":
                    mem_pe(pe)
                if st in NN:
                    norm_pe(pe, st)
                if st == "w_in":
                    pe.wait_ge(x_ready, done(8 * (NN["mix"] + 1)))
                    stream_pe(pe, "w_in", lambda it, u: LAT)
                    stream_pe(pe, "mem_kv", lambda it, u: MEM)
                if st == "mixers":
                    mix_prep_pe(pe)
                    S_S.after(pe, "bias")
                    att_pe(pe, units2(), 64)
                    mix_out_pe(pe)
                    rw_pre_pe(pe)
                    rw_pe(pe)
                if st == "w_out":
                    V_S.after(pe, "lo3")
                    stream_pe(pe, "w_out", lambda it, u: LAT)
                if st == "pw1":
                    pe.wait_ge(x_ready, done(8 * (NN["n10"] + 1)))
                    stream_pe(pe, "pw1", lambda it, u: BOTH)
                if st == "pw2":
                    pe.wait_ge(x_ready, done(8 * (NN["ln"] + 1)))
                    stream_pe(pe, "pw2", lambda it, u: BOTH)
                if st == "qkv":
                    pe.wait_ge(x_ready, done(8 * (NN["n11"] + 1)))
                    stream_pe(pe, "qkv", qkv_segs)
                if st == "attn":
                    prep_pe(pe)
                    attn_pe(pe)
                if st == "wo":
                    pe.wait_ge(xa_ready, done(8))
                    stream_pe(pe, "wo", lambda it, u: LAT)
                if st in ("ffn0", "ffn1", "ffn2"):
                    b, segs = int(st[3]), BOTH if st == "ffn0" else LAT
                    pe.wait_ge(x_ready, done(8 * (NN[["n20", "n21", "ffn2_norm"][b]] + 1)))
                    for hf in (0, 1):
                        stream_pe(pe, f"up{b}{hf}", lambda it, u: segs)
                        stream_pe(pe, f"down{b}{hf}", lambda it, u: segs, from_g=HALF * (2 * b + hf + 1))
            finish_pe(pe)

        @block.vector
        def _(dve):
            prime(dve, [evac, mod_ready, rstd_ready, t_ready, x_ready, h_ready, v_ready, tap_done, cv_cent,
                        taps_ready, prod_ready, g_ready, out_c, rope_c, grp_ready, att_m, att_r, xa_ready, V_S.sem])
            ada_dve(dve)
            dve.wait_ge(start_c, done(3 + KD))
            dve.drain().then_inc(h_ready, 8)
            for st in order:
                if st == "ln":
                    mean_dve(dve)
                if st in NN:
                    norm_dve(dve, st)
                if st == "mixers":
                    mix_prep_dve(dve)
                    S_S.after(dve, "bias")
                    att_dve(dve, units2(), 64)
                    mix_out_dve(dve)
                    rw_pre_dve(dve)
                    rw_dve(dve)
                if st == "w_out":
                    w_out_dve(dve)
                if st == "pw1":
                    pw1_dve(dve)
                if st == "pw2":
                    pw2_dve(dve)
                if st == "attn":
                    prep_dve(dve)
                    attn_dve(dve)
                if st == "wo":
                    wo_dve(dve)
                if st in ("ffn0", "ffn1", "ffn2"):
                    b, w = int(st[3]), TOK if st == "ffn0" else SEQ
                    for hf in (0, 1):
                        up_dve(dve, b, hf, w)
                        down_dve(dve, b, hf, w)
            finish_dve(dve)


_INS = ["x", "c", "ctx", "c_ctx", "ada_w", "ada_b", "norm1_g", "norm2_g", "final_g", "conv_w_pw1", "conv_b_pw1",
        "conv_w_dw", "conv_b_dw", "conv_ln_g", "conv_ln_b", "conv_w_pw2", "conv_b_pw2", "attn_w_qkv", "attn_w_o",
        "attn_sink", "ffn_w_up", "ffn_w_dw", "ffn_b_dw", "ffn_w_down", "mem_2", "rel_bias_2", "mix_norm_g_2",
        "w_in_2", "attn_q_norm_2", "attn_k_norm_2", "attn_sinks_2", "rwkv_mu_2", "rwkv_w0_2", "rwkv_w2_2",
        "rwkv_a0_2", "rwkv_a2_2", "rwkv_g2_2", "rwkv_k_k_2", "rwkv_k_a_2", "rwkv_r_k_2", "rwkv_ln_w_2",
        "rwkv_ln_b_2", "mem_norm_g_2", "w_mem_kv_2", "mem_q_norm_2", "mem_k_norm_2", "w_out_2", "ffn_norm_g_2",
        "w_up_2", "conv_w_2", "conv_b_2", "w_down_2"]
_OUT_SHAPE = (1, SEQ, D)


def kernel(**inputs):
    import numpy as _np
    import concourse.bacc as _bacc
    from concourse import mybir as _mybir
    from concourse.bass_utils import run_bass_kernel_spmd as _run

    nc = _bacc.Bacc("TRN2", target_bir_lowering=False, num_devices=1)
    arrays, aps = {}, {}
    given = {name: _np.ascontiguousarray(inputs[name]) for name in _INS}
    for name, a in list(given.items()) + list(constants().items()):
        arrays[f"in_{name}"] = a
        aps[name] = nc.dram_tensor(f"in_{name}", a.shape, _mybir.dt.from_np(a.dtype), kind="ExternalInput").ap()
    out = nc.dram_tensor("out_0", _OUT_SHAPE, F32, kind="ExternalOutput").ap()
    build(nc, aps, out)
    r = _run(nc, [arrays], core_ids=[0])
    return r.results[0]["out_0"]
```

```python
from contextlib import ExitStack

import concourse.bass as bass
from concourse import mybir
import numpy as np

P = 128
D = 1024
KD = D // P
SEQ = 512
CTX = 256
TOK = SEQ + CTX
DFF = 2816
FT = DFF // P
HALF = FT // 2
HD = 64
TAPS = 31
PAD = TAPS // 2
EPS = 1e-6
GN_EPS = 64e-5
L2_EPS = 1e-12
KAPPA = float(np.exp(-0.5))
NEG = -1e30

F32 = mybir.dt.float32
F32R = mybir.dt.float32r
U32 = mybir.dt.uint32
ALU = mybir.AluOpType
ACT = mybir.ActivationFunctionType
AX = mybir.AxisListType

LEAD = 8


def done(n):
    return n + LEAD


PARAM_ROWS = [
    ("c", 8), ("c_ctx", 8), ("ada_b", 96), ("norm1_g", 16), ("norm2_g", 16), ("final_g", 8),
    ("conv_b_pw1", 16), ("conv_w_dw", 8 * TAPS), ("conv_b_dw", 8), ("conv_ln_g", 8), ("conv_ln_b", 8),
    ("conv_b_pw2", 8), ("ffn_w_dw", 2 * 3 * 2 * FT), ("ffn_b_dw", 2 * 2 * FT),
    ("mix_norm_g_2", 8), ("mem_norm_g_2", 8), ("ffn_norm_g_2", 8), ("conv_w_2", 3 * 2 * FT),
    ("conv_b_2", 2 * FT), ("rwkv_mu_2", 10), ("rwkv_a0_2", 3), ("rwkv_k_k_2", 3), ("rwkv_k_a_2", 3),
    ("rwkv_r_k_2", 3), ("rwkv_ln_w_2", 3), ("rwkv_ln_b_2", 3),
    ("attn_q_norm_2", 1), ("attn_k_norm_2", 1), ("mem_q_norm_2", 1), ("mem_k_norm_2", 1),
]
COL, _n = {}, 0
for _name, _rows in PARAM_ROWS:
    COL[_name] = _n
    _n += _rows
N_ROWS = _n
PT = -(-N_ROWS // P)

STREAMS = [("pw1", 16, 8), ("pw2", 8, 8)]
for _h in (0, 1):
    STREAMS += [(f"up0{_h}", 2 * HALF, 8), (f"down0{_h}", 8, HALF)]
STREAMS += [("qkv", 12, 8), ("wo", 8, 8)]
for _h in (0, 1):
    STREAMS += [(f"up1{_h}", 2 * HALF, 8), (f"down1{_h}", 8, HALF)]
STREAMS += [("w_in", 17, 8), ("mem_kv", 4, 8), ("w_out", 8, 8)]
for _h in (0, 1):
    STREAMS += [(f"up2{_h}", 2 * HALF, 8), (f"down2{_h}", 8, HALF)]
Q0, ROWS_OF, _q = {}, {}, 0
ROWS_AT = []
for _name, _chunks, _rows in STREAMS:
    Q0[_name], ROWS_OF[_name] = _q, _rows
    ROWS_AT += [_rows] * _chunks
    _q += _chunks
N_CHUNKS = dict((s[0], s[1]) for s in STREAMS)
Q_ALL = _q

ADA_FIRST = 2 * D // 256

NORMS = ["n10", "ln", "n20", "n11", "n21", "final", "mix", "ffn2_norm"]
NN = {s: i for i, s in enumerate(NORMS)}


def constants():
    eye = np.eye(P, dtype=np.float32)
    ones = np.ones((P, P), np.float32)
    head = np.kron(np.eye(2, dtype=np.float32), np.ones((HD, HD), np.float32))
    base = np.concatenate([eye, ones, head], 1)

    rot = np.zeros((P, P), np.float32)
    for h in (0, HD):
        for d in range(HD // 2):
            rot[h + d + HD // 2, h + d] = -1.0
            rot[h + d, h + d + HD // 2] = 1.0
    low = np.zeros((P, P), np.float32)
    high = np.zeros((P, P), np.float32)
    for d in range(HD):
        low[d, d] = low[d, d + HD] = 1.0
        high[d + HD, d] = high[d + HD, d + HD] = 1.0
    n_freq = HD // 4
    inv = np.float32(10000.0) ** (-np.arange(n_freq, dtype=np.float32) / np.float32(n_freq))
    pos = np.arange(SEQ)
    row, col = (pos // 64).astype(np.float32), (pos % 64).astype(np.float32)
    ang = np.concatenate([row[None] * inv[:, None], col[None] * inv[:, None]], 0).astype(np.float32)
    cos, sin = np.tile(np.cos(ang), (4, 1)), np.tile(np.sin(ang), (4, 1))
    q, k = np.arange(P)[:, None], np.arange(P)[None]
    before = np.where(k >= q, 0.0, NEG).astype(np.float32)
    after = np.where(k <= q, 0.0, NEG).astype(np.float32)
    first = np.concatenate([rot, low, high, cos, sin, before, after], 1)

    anti = eye[:, ::-1].copy()
    s, t = q, k
    strict, upto = (s < t).astype(np.float32), (s <= t).astype(np.float32)
    tri = np.concatenate([upto, strict], 1)
    mask = np.concatenate([strict, upto, strict, upto], 1)
    levels = []
    for e in range(7):
        b = 1 << e
        levels.append(((s // (2 * b) == t // (2 * b)) & (s // b % 2 == 0) & (t // b % 2 == 1)).astype(np.float32))
    second = np.concatenate([low, high, anti, tri, mask] + levels, 1)

    j = np.arange(384)
    dist = 255 - j
    inside = (dist >= 0) & (dist < 128)
    dd = np.clip(dist, 0, 127)
    large = 16 + (np.log(np.maximum(dd, 1).astype(np.float32) / np.float32(16)) / np.float32(np.log(128 / 16))
                  * np.float32(16)).astype(np.int32)
    bucket = np.where(dd < 16, dd, np.minimum(large, 31))
    hot = np.zeros((P, 384), np.float32)
    hot[bucket[inside], j[inside]] = 1.0
    hot[32, ~inside] = NEG
    return {"k_base": base.astype(np.float32), "k_first": first.astype(np.float32),
            "k_second": second.astype(np.float32), "k_hot": hot}


class Program:

    def __init__(self, nc, ctx, A):
        self.nc, self.A, self.ctx = nc, A, ctx
        base = -(-nc.sbuf_base // 64) * 64
        self.top = base

        def region(nbytes):
            at = self.top
            self.top += -(-nbytes // 64) * 64
            return at

        def at(name, offset, shape, dt=F32):
            return nc.alloc_sbuf_tensor_at(name, [P] + shape, dt, offset=offset)

        self.h = at("h", region(KD * TOK * 4), [KD, TOK])
        r_x = region(2 * KD * TOK * 4)
        self.x_hi = at("x_hi", r_x, [KD, TOK], F32R)
        self.x_lo = at("x_lo", r_x + KD * TOK * 4, [KD, TOK], F32R)
        r_g = region(2 * HALF * TOK * 4)
        self.r_x, self.r_g = r_x, r_g
        self.g_hi = at("g_hi", r_g, [HALF, TOK], F32R)
        self.g_lo = at("g_lo", r_g + HALF * TOK * 4, [HALF, TOK], F32R)
        w = HALF * P * 4
        self.raw = at("raw", region(2 * w), [2, HALF * P])
        self.w_hi = at("w_hi", region(2 * w), [2, HALF * P], F32R)
        self.w_lo = at("w_lo", region(2 * w), [2, HALF * P], F32R)
        self.prm = at("prm", region(PT * P * 4), [PT * P])
        self.kb = at("kb", region(3 * P * 4), [3 * P])
        self.mods = at("mods", region(96 * 2 * 4), [96, 2])
        self.scg = at("scg", region(64 * 4), [2, 2, 2, KD])
        self.b2g1 = at("b2g1", region(16 * 4), [2, KD])
        self.sc = at("sc", region(16 * 4), [2 * KD])
        self.sinks = at("sinks", region(24 * 4), [24])
        self.one = at("one", region(32), [8])
        self.sm_max = at("sm_max", region(64), [2])
        self.sm_neg = at("sm_neg", region(64), [2])
        self.sm_sum = at("sm_sum", region(64), [2])
        self.sm_sink = at("sm_sink", region(64), [2])
        self.sm_den = at("sm_den", region(64), [2])
        self.sm_rd = at("sm_rd", region(64), [2])
        self.sinkg = at("sinkg", region(64), [2, 4])
        self.nsinks = at("nsinks", region(24 * 4), [24])
        self.cend = at("cend", region(48 * 4), [4, 3, 4])
        self.gn = at("gn", region(6 * 6 * 4), [6, 6])
        self.mod_rows_at = region(4 * 256 * 4)
        self.mod_rows = at("mod_rows", self.mod_rows_at, [4 * 256])
        r_s = region(8 * TOK * 4)
        self.r_s = r_s
        assert self.top <= nc.sbuf_usable_end, (self.top, nc.sbuf_usable_end)
        self.left = nc.sbuf_usable_end - self.top

        ln = TOK * 4
        self.n_sq = at("n_sq", r_s, [2, TOK])
        self.n_t = at("n_t", r_s + 2 * ln, [2, TOK])
        self.n_y = at("n_y", r_s + 4 * ln, [2, TOK])
        self.f_a = at("f_a", r_s, [2, TOK])
        self.f_b = at("f_b", r_s + 2 * ln, [2, TOK])
        self.gate = at("gate", r_s + 6 * ln, [2, TOK])
        self.mod_t = at("mod_t", r_s + 6 * ln, [2, P])

        self.x_rows = at("x_rows", r_g, [6, D])
        self.p_rows = at("p_rows", r_g + 6 * D * 4, [PT, P])
        self.m_rows = at("m_rows", r_g, [2, D])
        self.vw = SEQ + CTX + 4 * PAD
        r_tail = r_g + KD * (self.vw + TOK) * 4
        ada_tail = at("ada_tail", r_tail, [2, KD, 256])
        assert r_tail + 2 * KD * 256 * 4 <= r_g + 2 * HALF * TOK * 4
        ada_x = at("ada_x", r_x, [6, KD, 256])
        ada_s = at("ada_s", r_s, [2, KD, 256])
        self.ada_first = [ada_x[:, i, :, :] for i in range(6)] + [ada_tail[:, i, :, :] for i in range(2)]
        self.ada_ring = [ada_tail[:, i, :, :] for i in range(2)] + [ada_s[:, i, :, :] for i in range(2)]
        self.vp = at("vp", r_g, [KD, self.vw])
        self.cv = at("cv", r_g + KD * self.vw * 4, [KD, TOK])
        o = r_g
        def nxt(name, shape, dt=F32):
            nonlocal o
            t = at(name, o, shape, dt)
            o += int(np.prod(shape)) * 4
            return t
        self.kf = nxt("kf", [3 * P + 2 * SEQ + 2 * P])
        self.q_ = nxt("q_", [8, SEQ])
        self.k_ = nxt("k_", [2, TOK])
        self.v_ = nxt("v_", [2, TOK])
        self.vt = nxt("vt", [6, 256])
        self.kd = nxt("kd", [4, TOK])
        assert o <= r_g + 2 * HALF * TOK * 4, o - r_g
        o = r_s
        self.qg = nxt("qg", [2, SEQ])
        self.p_sb = nxt("p_sb", [2, 640])
        self.pt_sb = nxt("pt_sb", [2, 640])
        self.o_t = nxt("o_t", [4, 256])
        self.kg = nxt("kg", [TOK])
        self.vg = nxt("vg", [6, HD])
        assert o <= r_s + 8 * ln
        o = r_g + 2 * 640 * 4
        self.pj = nxt("pj", [17, SEQ])
        r_mkv = o
        self.mkv = nxt("mkv", [4, CTX])
        self.ks = nxt("ks", [3 * P + 2 * P + 4 * P + 7 * P])
        r_b = o
        self.bias = nxt("bias", [6, 2 * P])
        self.lw = nxt("lw", [384])
        self.w0b = nxt("w0b", [384])
        r_av = o
        self.av = nxt("av", [3, SEQ])
        assert o <= r_g + 2 * HALF * TOK * 4, o - r_g
        o = r_av
        self.hot = nxt("hot", [384])
        self.rr = nxt("rr", [384])
        self.relb = nxt("relb", [8])
        self.tz = at("tz", r_s + 4096, [6, 2 * P])
        o = r_s
        self.sig = nxt("sig", [4, 384])
        self.ex = nxt("ex", [3, SEQ])
        self.dd = nxt("dd", [2, SEQ])
        self.hq = nxt("hq", [2, SEQ])
        o = r_s
        self.m4 = nxt("m4", [2, 6, 512])
        assert o <= r_s + 8 * ln
        behind = [at(f"behind{i}", r_x + i * KD * TOK * 4, [KD, TOK]) for i in (0, 1)]
        self.lv, self.mt = (behind[0][:, 0:6, SEQ + i * P:SEQ + (i + 1) * P] for i in (0, 1))
        self.inv_t = [behind[1][:, 0:6, SEQ + i * P:SEQ + (i + 1) * P] for i in (0, 1)]
        o = r_b
        self.tok = nxt("tok", [3, 384])
        self.y = nxt("y", [384])
        o = r_mkv
        self.x0 = nxt("x0", [384])
        self.u = nxt("u", [384])
        self.z = nxt("z", [3, HD])
        o = r_g
        self.inv = nxt("inv", [6, P])
        self.y1 = nxt("y1", [3, P])
        self.ysq = at("ysq", self.mod_rows_at, [384])
        self.at = at

        self.ps = ctx.enter_context(nc.psum_tensor("ps", [P, 4096], F32))
        self.counting = []

    def sem(self, name, counting=True):
        s = self.ctx.enter_context(self.nc.semaphore(name))
        if counting:
            self.counting.append(s)
        return s

    def pair(self, n, lo=0, hi=TOK):
        return self.ps[:, n * 1024 + lo:n * 1024 + hi]

    def col(self, name, r=0):
        c = COL[name] + r
        return self.prm[:, c:c + 1]

    def col_at(self, name, r):
        return self.prm[:, bass.ds(r + COL[name], 1)]


def chunks(eng, n):
    full = (n - 2) // 4
    if full >= 2:
        with eng.Fori(0, full) as it:
            for u in range(4):
                yield it, u
    else:
        full = 0
    for i in range(4 * full, n):
        yield i // 4, i % 4


def build(nc, A, out, stop=None, dump=None):
    with ExitStack() as ctx:
        build_in(nc, ctx, A, out, stop, dump)


def build_in(nc, ctx, A, out, stop, dump):
    M = Program(nc, ctx, A)
    sem = M.sem
    ident, ones, head1 = M.kb[:, 0:P], M.kb[:, P:2 * P], M.kb[:, 2 * P:3 * P]

    s_cst = sem("s_cst", False)
    s_rows = sem("s_rows", False)
    s_raw = [sem(f"s_raw{i}", False) for i in range(2)]
    s_ada = [sem(f"s_ada{i}", False) for i in range(ADA_FIRST)]
    s_mod = sem("s_mod", False)
    s_modt = sem("s_modt", False)
    s_ring = [sem(f"s_ring{i}", False) for i in range(4)]
    s_kf = sem("s_kf", False)
    s_mem = sem("s_mem", False)
    s_out = sem("s_out", False)
    hi_ready = sem("hi_ready")
    lo_ready = sem("lo_ready")
    tile_done = sem("tile_done")
    evac = sem("evac")
    ada_used = sem("ada_used")
    start_t = sem("start_t")
    start_c = sem("start_c")
    zero_ready = sem("zero_ready")
    sc_ready = sem("sc_ready")
    mod_rows = sem("mod_rows")
    mod_t = sem("mod_t")
    mod_ready = sem("mod_ready")
    sq_ready = sem("sq_ready")
    sq_used = sem("sq_used")
    rms_ready = sem("rms_ready")
    rstd_ready = sem("rstd_ready")
    t_ready = sem("t_ready")
    y_ready = sem("y_ready")
    x_ready = sem("x_ready")
    h_ready = sem("h_ready")
    gate_ready = sem("gate_ready")
    v_ready = sem("v_ready")
    tap_done = sem("tap_done")
    cv_ready = sem("cv_ready")
    cv_cent = sem("cv_cent")
    mu_ready = sem("mu_ready")
    mid_ready = sem("mid_ready")
    taps_ready = sem("taps_ready")
    silu_ready = sem("silu_ready")
    prod_ready = sem("prod_ready")
    ghi_ready = sem("ghi_ready")
    g_ready = sem("g_ready")
    f_res = sem("f_res")

    rope_r = sem("rope_r")
    rope_c = sem("rope_c")
    turn_t = sem("turn_t")
    turn_c = sem("turn_c")
    grp_ready = sem("grp_ready")
    att_s = sem("att_s")
    att_m = sem("att_m")
    att_p = sem("att_p")
    att_r = sem("att_r")
    att_t = sem("att_t")
    att_c = sem("att_c")
    att_o = sem("att_o")
    att_e = sem("att_e")
    otr_t = sem("otr_t")
    otr_h = sem("otr_h")
    xa_ready = sem("xa_ready")

    H_STAGE = ["start", "pw2", "down00", "down01", "wo", "down10", "down11", "final", "w_out",
               "down20", "down21"]
    H = {s: 8 * (i + 1) for i, s in enumerate(H_STAGE)}

    order = ["start", "ada", "n10", "pw1", "ln", "pw2", "n20", "ffn0", "n11", "qkv", "attn", "wo",
             "n21", "ffn1", "final", "mix", "w_in", "mixers", "w_out", "ffn2_norm", "ffn2"]
    if stop:
        order = order[:order.index(stop) + 1]
    streams_of = {"pw1": ["pw1"], "pw2": ["pw2"], "qkv": ["qkv"], "wo": ["wo"],
                  "w_in": ["w_in", "mem_kv"], "w_out": ["w_out"]}
    for b in range(3):
        streams_of[f"ffn{b}"] = [f"{d}{b}{hf}" for hf in (0, 1) for d in ("up", "down")]
    used_streams = [s for st in order for s in streams_of.get(st, [])]
    q_end = sum(N_CHUNKS[s] for s in used_streams)

    def rows(ap, kt):
        return ap.rearrange("(kt p) c -> p kt c", p=P)

    w_src = {"pw1": rows(A["conv_w_pw1"][0], 8), "pw2": rows(A["conv_w_pw2"][0], 8),
             "qkv": rows(A["attn_w_qkv"][0], 8), "wo": rows(A["attn_w_o"][0], 8),
             "w_in": rows(A["w_in_2"][0], 8), "mem_kv": rows(A["w_mem_kv_2"][0], 8),
             "w_out": rows(A["w_out_2"][0], 8)}
    for b in range(3):
        up = A["w_up_2"][0] if b == 2 else A["ffn_w_up"][b]
        down = A["w_down_2"][0] if b == 2 else A["ffn_w_down"][b]
        for hf in (0, 1):
            w_src[f"up{b}{hf}"] = rows(up, 8)
            w_src[f"down{b}{hf}"] = rows(down[hf * HALF * P:(hf + 1) * HALF * P, :], HALF)

    def column(name, it, u):
        if name == "pw1":
            return it * 256 + ((u % 2) * 8 + u // 2) * P
        if name.startswith("up"):
            return it * 256 + ((u % 2) * FT + int(name[3]) * HALF + u // 2) * P
        return it * 512 + u * P

    def load_stream(sp, name):
        K, q0 = ROWS_OF[name], Q0[name]
        n, full = N_CHUNKS[name], N_CHUNKS[name] // 4
        def one(it, u):
            slot = (q0 + u) % 2
            c = column(name, it, u)
            if not isinstance(c, int):
                c = sp.snap(c)
            sp.wait_ge(lo_ready, done(q0 + 4 * it + u - 1))
            sp.dma_start(M.raw[:, slot, 0:K * P].rearrange("p (k c) -> p k c", c=P),
                         w_src[name][:, :, bass.ds(c, P)]).then_inc(s_raw[slot], 16)
        if full >= 2:
            with sp.Fori(0, full) as it:
                for u in range(4):
                    one(it, u)
        else:
            full = 0
        for i in range(4 * full, n):
            one(i // 4, i % 4)

    def raw_count(q0, it, u):
        return 16 * (2 * it + (q0 + u) // 2 + 1)

    def low_stream(pool, name):
        K, q0 = ROWS_OF[name], Q0[name]
        n, full = N_CHUNKS[name], N_CHUNKS[name] // 4
        def one(it, u):
            slot = (q0 + u) % 2
            pool.wait_ge(hi_ready, done(q0 + 4 * it + u + 1))
            pool.tensor_tensor(M.w_lo[:, slot, 0:K * P], M.raw[:, slot, 0:K * P],
                               M.w_hi[:, slot, 0:K * P].bitcast(F32), ALU.subtract).then_inc(lo_ready, 1)
        if full >= 2:
            with pool.Fori(0, full) as it:
                for u in range(4):
                    one(it, u)
        else:
            full = 0
        for i in range(4 * full, n):
            one(i // 4, i % 4)

    def high(act, name, it, u):
        q0 = Q0[name]
        if isinstance(it, int):
            q = q0 + 4 * it + u + 2
            if q >= q_end:
                return
            K = ROWS_AT[q]
        else:
            K = ROWS_OF[name]
        slot = (q0 + u) % 2
        act.wait_ge(s_raw[slot], raw_count(q0, it, u + 2))
        act.wait_ge(tile_done, done(q0 + 4 * it + u + 1))
        act.activation(M.w_hi[:, slot, 0:K * P], M.raw[:, slot, 0:K * P], ACT.Copy).then_inc(hi_ready, 1)

    def high_first(act):
        for q in range(min(2, q_end)):
            act.wait_ge(s_raw[q], 16)
            act.activation(M.w_hi[:, q, 0:ROWS_AT[q] * P], M.raw[:, q, 0:ROWS_AT[q] * P], ACT.Copy)\
                .then_inc(hi_ready, 1)

    LAT, BOTH, MEM = [(0, SEQ)], [(0, SEQ), (SEQ, CTX)], [(SEQ, CTX)]

    PW1_PAIR = (0, 2, 1, 2)

    def products(pe, name, it, u, segs, from_g=0):
        K, q0 = ROWS_OF[name], Q0[name]
        slot, pair = (q0 + u) % 2, PW1_PAIR[u] if name == "pw1" else (q0 + u) % 4
        hi, lo = (M.g_hi, M.g_lo) if from_g else (M.x_hi, M.x_lo)
        pe.wait_ge(lo_ready, done(q0 + 4 * it + u + 1))
        pe.wait_ge(evac, done(q0 + 4 * it + u - 3))
        for n, (t0, tn) in enumerate(segs):
            for k in range(K):
                if from_g and n == 0 and u == 0 and isinstance(it, int) and it == 0:
                    pe.wait_ge(g_ready, done(from_g - HALF + k + 1))
                wh = M.w_hi[:, slot, k * P:(k + 1) * P]
                wl = M.w_lo[:, slot, k * P:(k + 1) * P]
                o = M.pair(pair, t0, t0 + tn)
                for i, (w_, x_) in enumerate(((wh, hi), (wh, lo), (wl, hi))):
                    mm = pe.matmul(o, w_, x_[:, k, t0:t0 + tn], start=(k == 0 and i == 0),
                                   stop=(k == K - 1 and i == 2))
        mm.then_inc(tile_done, 1)

    def stream_pe(pe, name, segs_of, from_g=0):
        for it, u in chunks(pe, N_CHUNKS[name]):
            products(pe, name, it, u, segs_of(it, u), from_g)


    def start_sp(sp):
        sp.dma_start(M.kb[:, :], A["k_base"]).then_inc(s_cst, 16)
        sp.wait_ge(zero_ready, done(1))
        for name, r in PARAM_ROWS:
            src = A[name]
            if name.endswith("norm_2") and r == 1:
                c = COL[name]
                for half in (0, 1):
                    sp.dma_start(M.p_rows[c % P:c % P + 1, c // P, half * HD:(half + 1) * HD], src)\
                        .then_inc(s_cst, 16)
                continue
            dims = " ".join(f"d{i}" for i in range(len(src.shape)))
            flat = src.rearrange(f"{dims} -> ({dims})") if len(src.shape) > 1 else src
            flat = flat.rearrange("(r c) -> r c", c=P)
            r0 = 0
            while r0 < r:
                c = COL[name] + r0
                n = min(r - r0, P - c % P)
                sp.dma_start(M.p_rows[c % P:c % P + n, c // P, :], flat[r0:r0 + n, :]).then_inc(s_cst, 16)
                r0 += n
        sp.dma_start(M.sinks[:, 0:16], A["attn_sink"][0:1, :].to_broadcast([P, 16])).then_inc(s_cst, 16)
        sp.dma_start(M.sinks[:, 16:22], A["attn_sinks_2"][0:1, :].to_broadcast([P, 6])).then_inc(s_cst, 16)
        sp.dma_start(M.x_rows[:, 0:4, :], A["x"][0].rearrange("(t p) d -> p t d", p=P)).then_inc(s_rows, 16)
        sp.dma_start(M.x_rows[:, 4:6, :], A["ctx"][0].rearrange("(t p) d -> p t d", p=P)).then_inc(s_rows, 16)

    cond = M.sc[:, :].rearrange("p (s k) -> p k s", s=2)
    ada_src = A["ada_w"].rearrange("l (kt p) c -> p l kt c", p=P)

    def ada_first_load(act):
        for n in range(ADA_FIRST):
            act.dma_start(M.ada_first[n], ada_src[:, 0, :, n * 256:(n + 1) * 256]).then_inc(s_ada[n], 16)

    def ada_load(sp, it, n, layer, column):
        sp.wait_ge(ada_used, done(12 * it + (ADA_FIRST + n - 3)))
        sp.dma_start(M.ada_ring[n % 4], ada_src[:, layer, :, bass.ds(column, 256)]).then_inc(s_ring[n % 4], 16)

    def pw1_sp(sp):
        def w(it, u):
            q0 = Q0["pw1"]
            if 4 * it + u >= 2 if isinstance(it, int) else True:
                sp.wait_ge(lo_ready, done(q0 + 4 * it + u - 1))
            c = column("pw1", it, u)
            if not isinstance(c, int):
                c = sp.snap(c)
            sp.dma_start(M.raw[:, (q0 + u) % 2, 0:KD * P].rearrange("p (k c) -> p k c", c=P),
                         w_src["pw1"][:, :, bass.ds(c, P)]).then_inc(s_raw[(q0 + u) % 2], 16)

        def first(n):
            ada_load(sp, 0, n, 0, (ADA_FIRST + n) * 256)
        w(0, 0)
        w(0, 1)
        w(0, 2)
        sp.wait_ge(ada_used, done(ADA_FIRST))
        first(0)
        first(1)
        sp.wait_ge(x_ready, done(8))
        for n in range(2, 6):
            first(n)
        w(0, 3)
        for n in range(6, 12):
            first(n)
        with sp.Fori(0, 2) as it:
            for u in range(4):
                w(it + 1, u)
                for n in range(3 * u - 3, 3 * u + 3) if u % 2 else ():
                    ada_load(sp, it + 1, n, 1, sp.snap(it * (12 * 256) + n * 256))
        w(3, 0)
        w(3, 1)
        for n in range(4):
            ada_load(sp, 3, n, 0, (ADA_FIRST + 12 + n) * 256)
        for u in (2, 3):
            w(3, u)

    def start_pe(pe):
        pe.wait_ge(s_cst, 16 * M.n_param_dma)
        for t in range(PT):
            bank = t // 4
            mm = pe.transpose(M.ps[:, bank * 512 + (t % 4) * P:bank * 512 + (t % 4 + 1) * P],
                              M.p_rows[:, t, :], ident)
            if t % 4 == 3 or t == PT - 1:
                mm.then_inc(start_t, 1)
        pe.wait_ge(s_rows, 32)
        for k in range(KD):
            pair = (k + 2) % 3
            if k >= 1:
                pe.wait_ge(start_c, done(k + 1))
            for t in range(6):
                mm = pe.transpose(M.pair(pair, t * P, (t + 1) * P), M.x_rows[:, t, k * P:(k + 1) * P], ident)
            mm.then_inc(start_t, 1)

    def start_act(act):
        act.wait_ge(start_t, done(1))
        act.activation(M.prm[:, 0:512], M.ps[:, 0:512], ACT.Copy).then_inc(start_c, 1)
        act.wait_ge(start_t, done(2))
        act.activation(M.prm[:, 512:1024], M.ps[:, 512:1024], ACT.Copy).then_inc(start_c, 1)
        act.wait_ge(start_t, done(3))
        act.activation(M.prm[:, 1024:PT * P], M.ps[:, 1024:PT * P], ACT.Copy).then_inc(start_c, 1)
        act.wait_ge(start_c, done(3))
        act.activation(M.sc[:, :], M.prm[:, COL["c"]:COL["c"] + 16], ACT.Silu).then_inc(sc_ready, 1)
        for k in range(KD):
            act.wait_ge(start_t, done(4 + k))
            act.activation(M.h[:, k, :], M.pair((k + 2) % 3), ACT.Copy).then_inc(start_c, 1)

    mod_dram = nc.dram_tensor("mod_scratch", (2, 2 * 6 * D), F32, kind="Internal").ap()
    MOD_GROUPS = 2 + 10

    def ada_products(pe, weights, n):
        c = n // 4
        for k in range(KD):
            mm = pe.matmul(M.ps[32 * c:32 * c + 2, 3 * 1024 + (n % 4) * 256:3 * 1024 + (n % 4 + 1) * 256],
                           cond[:, k, :], weights[:, k, :], start=(k == 0), stop=(k == KD - 1),
                           tile_position=(0, 32 * c))
        mm.then_inc(ada_used, 1)

    def ada_pe(pe):
        pe.wait_ge(sc_ready, done(1))
        for n in range(ADA_FIRST):
            pe.wait_ge(s_ada[n], 16)
            ada_products(pe, M.ada_first[n], n)
        turn_mods_pe(pe, 0)

    def turn_mods_pe(pe, second):
        n = 96 if second else 16
        pe.wait_ge(mod_rows, done(MOD_GROUPS if second else 2))
        pe.wait_ge(s_modt, 32 if not second else 64)
        for s in (0, 1):
            mm = pe.transpose(M.pair(3, s * n, (s + 1) * n), M.mod_t[0:n, s, :], ident[0:n, 0:n])
        mm.then_inc(mod_t, 1)

    def group_act(act, g, layer, column):
        c = g if g < 2 else (g - 2) % 3
        act.wait_ge(ada_used, done(4 * g + 4))
        if g >= 2:
            act.wait_ge(s_mod, 16 * g)
        r = slice(32 * c, 32 * c + 2)
        act.activation(M.mod_rows[r, :], M.ps[r, 3 * 1024:4 * 1024], ACT.Copy).then_inc(mod_rows, 1)
        act.wait_ge(mod_rows, done(g + 1))
        at = layer * 6 * D + column
        act.dma_start(mod_dram[:, at:at + 1024], M.mod_rows[r, :]).then_inc(s_mod, 16)

    def mods_back_act(act, second):
        n = 96 if second else 16
        act.wait_ge(s_mod, 16 * (MOD_GROUPS if second else 2))
        if second:
            act.wait_ge(v_ready, done(7))
        for s in (0, 1):
            act.dma_start(M.mod_t[0:n, s, :], mod_dram[s:s + 1, 0:n * P].rearrange("o (m p) -> (o m) p", p=P))\
                .then_inc(s_modt, 16)

    def pw1_pe(pe):
        pe.wait_ge(x_ready, done(8 * (NN["n10"] + 1)))
        for it, u in chunks(pe, 16):
            if u % 2:
                pe.wait_ge(gate_ready, done(2 * it + u // 2))
            products(pe, "pw1", it, u, BOTH)
            if u % 2 == 0:
                continue
            for n in range(3 * u - 3, 3 * u + 3) if not isinstance(it, int) else range(4 if u == 1 else 0):
                if n % 4 == 0:
                    pe.wait_ge(mod_rows, done(3 * it + n // 4))
                pe.wait_ge(s_ring[n % 4], 16 * (3 * it + n // 4 + 1))
                ada_products(pe, M.ada_ring[n % 4], n)
        turn_mods_pe(pe, 1)

    def add_mods(dve, lo, hi, n):
        for s in (0, 1):
            dve.tensor_tensor(M.mods[:, lo:hi, s], M.pair(3, s * n + lo, s * n + hi),
                              M.prm[:, COL["ada_b"] + lo:COL["ada_b"] + hi], ALU.add)

    def norm_gains(dve, l, w):
        m0 = 48 * l + 8 * (1 + 3 * w)
        for s in (0, 1):
            c = COL[("norm1_g", "norm2_g")[w]] + 8 * l
            dve.scalar_tensor_tensor(out=M.scg[:, l, w, s, :], in0=M.mods[:, m0:m0 + 8, s], scalar=1.0,
                                     in1=M.prm[:, c:c + 8], op0=ALU.add, op1=ALU.mult)

    def ada_dve(dve):
        dve.wait_ge(mod_t, done(1))
        dve.wait_ge(start_c, done(3))
        add_mods(dve, 0, 16, 16)
        dve.tensor_scalar(M.nsinks[:, 0:22], M.sinks[:, 0:22], -1.0, None, ALU.mult)
        dve.drain()
        norm_gains(dve, 0, 0)
        dve.drain().then_inc(mod_ready, 1)

    def ada_rest_dve(dve):
        dve.wait_ge(mod_t, done(2))
        add_mods(dve, 16, 96, 96)
        dve.drain()
        for l, w in ((0, 1), (1, 0), (1, 1)):
            norm_gains(dve, l, w)
        for s in (0, 1):
            c = COL["conv_b_pw2"]
            dve.tensor_tensor(M.b2g1[:, s, :], M.mods[:, 16:24, s], M.prm[:, c:c + 8], ALU.mult)
        dve.drain().then_inc(mod_ready, 1)


    def scale_of(name, k, s):
        if name in ("n10", "n20", "n11", "n21"):
            l, w = int(name[2]), int(name[1]) - 1
            return M.scg[:, l, w, s, k:k + 1], M.mods[:, 48 * l + 24 * w + k, s:s + 1]
        if name == "ln":
            return M.col("conv_ln_g", k), M.col("conv_ln_b", k)
        if name == "final":
            return M.col("final_g", k), 0.0
        if name == "mix":
            return M.col("mem_norm_g_2" if s else "mix_norm_g_2", k), 0.0
        return M.col("ffn_norm_g_2", k), 0.0

    NORM_W = {"n10": TOK, "ln": TOK, "n20": TOK, "n11": TOK, "n21": SEQ, "final": SEQ, "mix": TOK,
              "ffn2_norm": SEQ}
    NORM_Q = {"n10": 0, "ln": Q0["pw2"], "n20": Q0["up00"], "n11": Q0["qkv"], "n21": Q0["up10"],
              "final": Q0["w_in"], "mix": Q0["w_in"] + 1, "ffn2_norm": Q0["up20"]}
    NORM_H = {"n10": "start", "n20": "pw2", "n11": "down01", "n21": "wo", "final": "down11",
              "mix": "final", "ffn2_norm": "w_out"}

    def norm_segs(name):
        w = NORM_W[name]
        if name == "ln":
            return [(0, 0, w)]
        return [(0, 0, SEQ)] + ([(1, SEQ, TOK)] if w == TOK else [])

    def norm_source(eng, name, k):
        if name == "ln":
            eng.wait_ge(cv_cent, done(k + 1))
            return M.cv[:, k, 0:TOK]
        if name == "n10":
            eng.wait_ge(start_c, done(3 + k + 1))
        else:
            eng.wait_ge(h_ready, done(H[NORM_H[name]] - 8 + k + 1))
            if name == "mix":
                eng.wait_ge(mem_ready, done(k + 1))
        return M.h[:, k, 0:NORM_W[name]]

    mem_ready = sem("mem_ready")
    mem_t = sem("mem_t")

    def norm_pe(pe, name):
        i, pair, w = NN[name], NORM_Q[name] % 4, NORM_W[name]
        if name == "mix":
            pe.wait_ge(mem_ready, done(KD))
        pe.wait_ge(evac, done(min(NORM_Q[name], {"final": Q0["w_in"], "mix": Q0["w_in"]}.get(name, 10**6))))
        if name == "ln":
            pair = (pair + 1) % 4
        for k in range(KD):
            pe.wait_ge(sq_ready, done(8 * i + k + 1))
            for t0, tn in ([(0, SEQ), (SEQ, CTX)] if w == TOK else [(0, SEQ)]):
                mm = pe.matmul(M.pair(pair, t0, t0 + tn), ones, M.n_sq[:, k % 2, t0:t0 + tn],
                               start=(k == 0), stop=(k == KD - 1))
            mm.then_inc(sq_used, 1)

    def norm_act(act, name):
        i, pair, w = NN[name], NORM_Q[name] % 4, NORM_W[name]
        if name == "ln":
            pair = (pair + 1) % 4
        for k in range(KD):
            src = norm_source(act, name, k)
            act.wait_ge(sq_used, done(8 * i + k - 1))
            if k < 2:
                act.wait_ge(x_ready, done(8 * i if i else 0))
                if name in ("n11", "final", "n21", "ffn2_norm"):
                    act.wait_ge(evac, done(min(NORM_Q[name], Q0["w_in"])))
            act.activation(M.n_sq[:, k % 2, 0:w], src, ACT.Square).then_inc(sq_ready, 1)
        act.wait_ge(sq_used, done(8 * i + KD))
        act.activation(M.n_y[:, 0, 0:w], M.pair(pair, 0, w), ACT.Sqrt, scale=1.0 / D, bias=eps_col)\
            .then_inc(rms_ready, 1)
        if name == "n10":
            for g in (0, 1):
                group_act(act, g, 0, g * 1024)
            mods_back_act(act, 0)
            act.wait_ge(mod_ready, done(1))
        for k in range(KD):
            act.wait_ge(t_ready, done(8 * i + k + 1))
            if k >= 2:
                act.wait_ge(x_ready, done(8 * i + k - 1))
            else:
                act.wait_ge(rstd_ready, done(i + 1))
            fn = ACT.Silu if name == "ln" else ACT.Identity
            dst = M.h[:, k, :] if name == "final" else M.n_y[:, k % 2, :]
            for s, t0, t1 in norm_segs(name):
                scale, shift = scale_of(name, k, s)
                ins = act.activation(dst[:, t0:t1], M.n_t[:, k % 2, t0:t1], fn, scale=scale, bias=shift)
            if name == "final":
                ins.then_inc(y_ready, 1)
                continue
            act.drain()
            act.activation(M.x_hi[:, k, 0:w], M.n_y[:, k % 2, 0:w], ACT.Copy).then_inc(y_ready, 1)

    def norm_dve(dve, name):
        i, pair, w = NN[name], NORM_Q[name] % 4, NORM_W[name]
        if name == "ln":
            pair = (pair + 1) % 4
        dve.wait_ge(rms_ready, done(i + 1))
        dve.reciprocal(M.pair(pair, 0, w), M.n_y[:, 0, 0:w]).then_inc(rstd_ready, 1)
        dve.wait_ge(rstd_ready, done(i + 1))
        if name == "n10":
            ada_dve(dve)

        def low(k):
            dve.wait_ge(y_ready, done(8 * i + k + 1))
            if name == "final":
                dve.drain().then_inc(x_ready, 1)
                dve.drain().then_inc(h_ready, 1)
                return
            dve.tensor_tensor(M.x_lo[:, k, 0:w], M.n_y[:, k % 2, 0:w], M.x_hi[:, k, 0:w].bitcast(F32),
                              ALU.subtract).then_inc(x_ready, 1)
        for k in range(KD):
            src = norm_source(dve, name, k)
            dve.tensor_tensor(M.n_t[:, k % 2, 0:w], M.pair(pair, 0, w), src, ALU.mult).then_inc(t_ready, 1)
            if k:
                low(k - 1)
        low(KD - 1)

    def prime(eng, sems):
        for s_ in sems:
            eng.drain().then_inc(s_, LEAD)

    def count_param_dmas():
        n = 1 + 2
        for name, r in PARAM_ROWS:
            if name.endswith("norm_2") and r == 1:
                n += 2
                continue
            c = COL[name]
            n += (c + r - 1) // P - c // P + 1
        return n

    rows_out = M.at("rows_out", M.r_g, [4, D])
    out_t = sem("out_t")
    out_c = sem("out_c")
    h_count = {"start": "start", "ada": "start", "n10": "start", "pw1": "start", "ln": "start", "pw2": "pw2",
               "n20": "pw2", "ffn0": "down01", "n11": "down01", "qkv": "down01", "attn": "down01", "wo": "wo",
               "n21": "wo", "ffn1": "down11", "final": "final", "mix": "final", "w_in": "final",
               "mixers": "final", "w_out": "w_out", "ffn2_norm": "w_out", "ffn2": "down21"}

    def finish_pe(pe):
        pe.wait_ge(h_ready, done(H[h_count[order[-1]]]))
        pe.wait_ge(evac, done(q_end))
        pe.wait_ge(x_ready, done(8 * sum(st in NN for st in order)))
        for t in range(SEQ // P):
            for k in range(KD):
                mm = pe.transpose(M.pair(t, k * P, (k + 1) * P), M.h[:, k, t * P:(t + 1) * P], ident)
            mm.then_inc(out_t, 1)

    def finish_dve(dve):
        for t in range(SEQ // P):
            dve.wait_ge(out_t, done(t + 1))
            dve.tensor_copy(M.rows_out_t[:, t, :], M.pair(t, 0, D)).then_inc(out_c, 1)

    def finish_sp(sp):
        for t in range(SEQ // P):
            sp.wait_ge(out_c, done(t + 1))
            sp.dma_start(out[0, t * P:(t + 1) * P, :], M.rows_out_t[:, t, :]).then_inc(s_out, 16)
        sp.wait_ge(s_out, 16 * (SEQ // P))

    M.rows_out_t = rows_out
    eps_col = M.one[:, 0:1]
    gn_eps_col = M.one[:, 1:2]
    zero_col = M.one[:, 2:3]

    VLAT, VCTX = PAD, SEQ + 3 * PAD

    def pw1_dve(dve):
        q0 = Q0["pw1"]
        cw = COL["conv_w_dw"]
        for j in range(8):
            pair = j % 2
            dve.wait_ge(tile_done, done(q0 + 2 * j + 2))
            dve.wait_ge(gate_ready, done(j + 1))
            dve.wait_ge(zero_ready, done(2))
            for t0, t1, at in ((0, SEQ, VLAT), (SEQ, TOK, VCTX)):
                ins = dve.scalar_tensor_tensor(out=M.vp[:, j, at:at + t1 - t0], in0=M.pair(pair, t0, t1),
                                               scalar=M.col("conv_b_pw1", j), in1=M.gate[:, j % 2, t0:t1],
                                               op0=ALU.add, op1=ALU.mult)
            ins.then_inc(v_ready, 1)
            dve.wait_ge(v_ready, done(j + 1))
            for tap in range(TAPS):
                for n, (t0, t1, at) in enumerate(((0, SEQ, VLAT), (SEQ, TOK, VCTX))):
                    src = M.vp[:, j, at - PAD + tap:at - PAD + tap + t1 - t0]
                    w = M.prm[:, cw + tap * 8 + j:cw + tap * 8 + j + 1]
                    o = M.pair(pair, t0, t1)
                    step = 2 * (TAPS * j + tap) + n
                    if tap == 0:
                        ins = dve.tensor_scalar(o, src, w, M.col("conv_b_dw", j), ALU.mult, ALU.add)
                    else:
                        dve.wait_ge(tap_done, done(step - 1))
                        ins = dve.scalar_tensor_tensor(out=o, in0=src, scalar=w, in1=o, op0=ALU.mult, op1=ALU.add)
                    ins.then_inc(tap_done, 1)

    def pw1_act(act):
        for i in range(16):
            it, u = i // 4, i % 4
            high(act, "pw1", it, u)
            for g in range(10):
                if group_step(g) == i:
                    layer, column = ((0, 2048 + g * 1024) if g < 3 else (1, (g - 3) * 1024) if g < 9 else (0, 5 * D))
                    group_act(act, g + 2, layer, column)
            if u % 2 == 0:
                continue
            j, slot, pair_g = i // 2, (i // 2) % 2, PW1_PAIR[u]
            act.wait_ge(tile_done, done(Q0["pw1"] + i + 1))
            if j >= 2:
                act.wait_ge(v_ready, done(j - 1))
            act.activation(M.gate[:, slot, :], M.pair(pair_g), ACT.Sigmoid,
                           bias=M.col("conv_b_pw1", j + 8)).then_inc(gate_ready, 1)
            if j:
                copy_conv(act, j - 1)
        mods_back_act(act, 1)
        copy_conv(act, 7)

    def group_step(g):
        it, c = g // 3, g % 3
        return 4 * it + (2, 4, 5)[c]

    def copy_conv(act, j):
        pair = j % 2
        act.wait_ge(tap_done, done(2 * TAPS * (j + 1)))
        act.activation(M.cv[:, j, :], M.pair(pair), ACT.Copy).then_inc(cv_ready, 1)
        act.wait_ge(cv_ready, done(j + 1))
        act.drain().then_inc(evac, 2)

    def mean_pe(pe):
        pair = Q0["pw2"] % 4
        pe.wait_ge(evac, done(Q0["pw2"]))
        for k in range(KD):
            pe.wait_ge(cv_ready, done(k + 1))
            for t0, tn in BOTH:
                mm = pe.matmul(M.pair(pair, t0, t0 + tn), ones, M.cv[:, k, t0:t0 + tn],
                               start=(k == 0), stop=(k == KD - 1))
        mm.then_inc(mu_ready, 1)

    def mean_dve(dve):
        pair = Q0["pw2"] % 4
        dve.wait_ge(mu_ready, done(1))
        for k in range(KD):
            dve.scalar_tensor_tensor(out=M.cv[:, k, :], in0=M.pair(pair), scalar=-1.0 / D, in1=M.cv[:, k, :],
                                     op0=ALU.mult, op1=ALU.add).then_inc(cv_cent, 1)

    def pw2_act(act):
        q0 = Q0["pw2"]
        for m in range(8):
            high(act, "pw2", m // 4, m % 4)
            act.wait_ge(tile_done, done(q0 + m + 1))
            for s, (t0, tn) in enumerate(BOTH):
                o = M.pair((q0 + m) % 4, t0, t0 + tn)
                ins = act.activation(o, o, ACT.Identity, scale=M.mods[:, 16 + m, s:s + 1],
                                     bias=M.b2g1[:, s, m:m + 1])
            ins.then_inc(f_res, 1)

    def pw2_dve(dve):
        q0 = Q0["pw2"]
        for m in range(8):
            dve.wait_ge(f_res, done(m + 1))
            dve.tensor_tensor(M.h[:, m, :], M.pair((q0 + m) % 4), M.h[:, m, :], ALU.add).then_inc(evac, 1)
            dve.drain().then_inc(h_ready, 1)

    def ffn_cols(b, tap, t, hf, j):
        r = t * FT + HALF * hf
        if b == 2:
            return M.col_at("conv_b_2" if tap is None else "conv_w_2", j + ((tap or 0) * 2 * FT + r))
        if tap is None:
            return M.col_at("ffn_b_dw", j + (b * 2 * FT + r))
        return M.col_at("ffn_w_dw", j + ((b * 3 + tap) * 2 * FT + r))

    SHIFTS = {0: (-1, 0, 1), 1: (-1, 0, 1), 2: (-2, -1, 0)}

    def up_act(act, b, hf, w):
        name = f"up{b}{hf}"
        q0, g0 = Q0[name], HALF * (2 * b + hf)
        zero_tap = SHIFTS[b].index(0)
        for it, u in chunks(act, 2 * HALF):
            high(act, name, it, u)
            if u % 2 == 0:
                continue
            j, slot = 2 * it + u // 2, u // 2
            pa, pb = (q0 + u - 1) % 4, (q0 + u) % 4
            g = 2 * it + (g0 + u // 2)
            act.wait_ge(tile_done, done(q0 + 4 * it + u + 1))
            for t, pr, dst in ((0, pa, M.f_a), (1, pb, M.f_b)):
                ins = act.activation(dst[:, slot, 0:w], M.pair(pr, 0, w), ACT.Identity,
                                     scale=ffn_cols(b, zero_tap, t, hf, j), bias=ffn_cols(b, None, t, hf, j))
            ins.then_inc(mid_ready, 1)
            act.wait_ge(taps_ready, done(g + 1))
            act.activation(M.pair(pa, 0, w), M.f_a[:, slot, 0:w], ACT.Silu).then_inc(silu_ready, 1)
            act.wait_ge(prod_ready, done(g + 1))
            act.activation(M.g_hi[:, bass.ds(j, 1), 0:w], M.pair(pb, 0, w), ACT.Copy).then_inc(ghi_ready, 1)

    def up_dve(dve, b, hf, w):
        name = f"up{b}{hf}"
        q0, g0 = Q0[name], HALF * (2 * b + hf)
        segs = [(0, SEQ)] + ([(SEQ, TOK)] if w == TOK else [])
        for it, u in chunks(dve, 2 * HALF):
            if u % 2 == 0:
                continue
            j, slot = 2 * it + u // 2, u // 2
            pa, pb = (q0 + u - 1) % 4, (q0 + u) % 4
            g = 2 * it + (g0 + u // 2)
            dve.wait_ge(mid_ready, done(g + 1))
            for n, tap in enumerate(t for t in range(3) if SHIFTS[b][t]):
                sh = SHIFTS[b][tap]
                if n:
                    dve.drain()
                for t, pr, dst in ((0, pa, M.f_a), (1, pb, M.f_b)):
                    for t0, t1 in segs:
                        o0, o1 = (t0 - sh, t1) if sh < 0 else (t0, t1 - sh)
                        ins = dve.scalar_tensor_tensor(
                            out=dst[:, slot, o0:o1], in0=M.pair(pr, o0 + sh, o1 + sh),
                            scalar=ffn_cols(b, tap, t, hf, j), in1=dst[:, slot, o0:o1],
                            op0=ALU.mult, op1=ALU.add)
            ins.then_inc(taps_ready, 1)
            dve.wait_ge(silu_ready, done(g + 1))
            dve.tensor_tensor(M.pair(pb, 0, w), M.pair(pa, 0, w), M.f_b[:, slot, 0:w], ALU.mult)\
                .then_inc(prod_ready, 1)
            dve.wait_ge(ghi_ready, done(g + 1))
            dve.tensor_tensor(M.g_lo[:, bass.ds(j, 1), 0:w], M.pair(pb, 0, w),
                              M.g_hi[:, bass.ds(j, 1), 0:w].bitcast(F32), ALU.subtract).then_inc(g_ready, 1)
            dve.drain().then_inc(evac, 2)

    def plain_high(act, name):
        for it, u in chunks(act, N_CHUNKS[name]):
            high(act, name, it, u)

    def down_dve(dve, b, hf, w):
        name = f"down{b}{hf}"
        q0 = Q0[name]
        for m in range(8):
            dve.wait_ge(tile_done, done(q0 + m + 1))
            for s, (t0, tn) in enumerate(BOTH if w == TOK else LAT):
                o = M.h[:, m, t0:t0 + tn]
                src = M.pair((q0 + m) % 4, t0, t0 + tn)
                if b == 2:
                    dve.tensor_tensor(o, src, o, ALU.add)
                else:
                    dve.scalar_tensor_tensor(out=o, in0=src, scalar=M.mods[:, 48 * b + 40 + m, s:s + 1],
                                             in1=o, op0=ALU.mult, op1=ALU.add)
            dve.drain().then_inc(evac, 1)
            dve.drain().then_inc(h_ready, 1)

    class Unit:

        def __init__(self, q, keys, sink, neg_sink, values, out):
            self.q, self.keys, self.sink, self.neg_sink, self.values, self.out = q, keys, sink, neg_sink, values, out
            self.nk = sum(n for _, n, _, _ in keys)

    SCALE = HD ** -0.5

    def att_pe(pe, units, n0):
        def scores(u):
            x = units[u]
            pe.wait_ge(att_p, done(n0 + max(u - 1, 0)))
            for off, n, rhs, masks in x.keys:
                mm = pe.matmul(M.pair(u % 2, off, off + n), x.q, rhs, start=True, stop=True)
                for at, width, mask in masks:
                    mm = pe.matmul(M.pair(u % 2, at, at + width), ident, mask, start=False, stop=True,
                                   skip_group_check=True)
            mm.then_inc(att_s, 1)

        def turn(u):
            x = units[u]
            pe.wait_ge(att_p, done(n0 + u + 1))
            pe.wait_ge(att_c, done(n0 + max(u - 1, 0)))
            pe.wait_ge(att_e, done(n0 + max(u - 1, 0)))
            for k in range(x.nk // P):
                mm = pe.transpose(M.pair(2 + u % 2, k * P, (k + 1) * P), M.p_sb[:, u % 2, k * P:(k + 1) * P], ident)
            mm.then_inc(att_t, 1)

        def values(u):
            x = units[u]
            pe.wait_ge(att_c, done(n0 + u + 1))
            for k, v in enumerate(x.values):
                mm = pe.matmul(M.pair(2 + u % 2, 640, 640 + HD), M.pt_sb[:, u % 2, k * P:(k + 1) * P], v,
                               start=(k == 0), stop=(k == len(x.values) - 1))
            mm.then_inc(att_o, 1)

        scores(0)
        for u in range(len(units)):
            if u + 1 < len(units):
                scores(u + 1)
            turn(u)
            if u:
                values(u - 1)
        values(len(units) - 1)

    def att_dve(dve, units, n0):
        def negated(u):
            x, b = units[u], u % 2
            dve.wait_ge(att_s, done(n0 + u + 1))
            dve.wait_ge(att_p, done(n0 + max(u - 1, 0)))
            dve.tensor_reduce(M.sm_max[:, b:b + 1], M.pair(u % 2, 0, x.nk), AX.X, ALU.max)
            dve.drain()
            if x.sink is None:
                dve.tensor_scalar(M.sm_neg[:, b:b + 1], M.sm_max[:, b:b + 1], -SCALE, None, ALU.mult)\
                    .then_inc(att_m, 1)
            else:
                dve.tensor_scalar(M.sm_neg[:, b:b + 1], M.sm_max[:, b:b + 1], -SCALE, x.neg_sink, ALU.mult,
                                  ALU.min).then_inc(att_m, 1)

        def copied(u):
            x, b = units[u], u % 2
            dve.wait_ge(att_t, done(n0 + u + 1))
            dve.wait_ge(att_o, done(n0 + max(u - 1, 0)))
            dve.tensor_copy(M.pt_sb[:, b, 0:x.nk], M.pair(2 + u % 2, 0, x.nk)).then_inc(att_c, 1)

        def denominator(u):
            x, b = units[u], u % 2
            dve.wait_ge(att_p, done(n0 + u + 1))
            dve.wait_ge(att_e, done(n0 + max(u - 1, 0)))
            den = M.sm_sum
            if x.sink is not None:
                den = M.sm_den
                dve.tensor_tensor(den[:, b:b + 1], M.sm_sum[:, b:b + 1], M.sm_sink[:, b:b + 1], ALU.add)
                dve.drain()
            dve.reciprocal(M.sm_rd[:, b:b + 1], den[:, b:b + 1]).then_inc(att_r, 1)

        negated(0)
        for u in range(len(units)):
            if u + 1 < len(units):
                negated(u + 1)
            denominator(u)
            copied(u)

    def att_act(act, units, n0):
        def exps(u):
            x, b = units[u], u % 2
            act.wait_ge(att_m, done(n0 + u + 1))
            act.wait_ge(att_t, done(n0 + max(u - 1, 0)))
            act.wait_ge(att_r, done(n0 + max(u - 1, 0)))
            act.activation(M.p_sb[:, b, 0:x.nk], M.pair(u % 2, 0, x.nk), ACT.Exp, scale=SCALE,
                           bias=M.sm_neg[:, b:b + 1], accum_out=M.sm_sum[:, b:b + 1])
            if x.sink is not None:
                act.activation(M.sm_sink[:, b:b + 1], x.sink, ACT.Exp, bias=M.sm_neg[:, b:b + 1])
            act.drain().then_inc(att_p, 1)

        def divided(u):
            x, b = units[u], u % 2
            act.wait_ge(att_o, done(n0 + u + 1))
            act.wait_ge(att_r, done(n0 + u + 1))
            act.activation(x.out, M.pair(2 + u % 2, 640, 640 + HD), ACT.Copy, scale=M.sm_rd[:, b:b + 1])\
                .then_inc(att_e, 1)

        exps(0)
        for u in range(len(units)):
            if u + 1 < len(units):
                exps(u + 1)
            if u:
                divided(u - 1)
        divided(len(units) - 1)

    kf_rot, kf_low, kf_high = (M.kf[:, i * P:(i + 1) * P] for i in range(3))
    kf_cos, kf_sin = M.kf[:, 3 * P:3 * P + SEQ], M.kf[:, 3 * P + SEQ:3 * P + 2 * SEQ]
    kf_mask = 3 * P + 2 * SEQ

    def qkv_segs(it, u):
        return LAT if not isinstance(it, int) or 4 * it + u < 8 else BOTH

    def qkv_act(act):
        q0 = Q0["qkv"]
        for it, u in chunks(act, 12):
            high(act, "qkv", it, u)
            act.wait_ge(tile_done, done(q0 + 4 * it + u + 1))
            i = 4 * it + u
            pr = (q0 + u) % 4
            if not isinstance(it, int) or i < 8:
                act.activation(M.q_[:, bass.ds(i, 1), :].rearrange("p a t -> p (a t)"), M.pair(pr, 0, SEQ),
                               ACT.Copy).then_inc(evac, 1)
            else:
                dst = (M.k_ if i < 10 else M.v_)[:, i % 2, :]
                act.activation(dst, M.pair(pr), ACT.Copy).then_inc(evac, 1)

    def rope_tiles():
        return [M.q_[:, i, :] for i in range(8)] + [M.k_[:, i, 0:SEQ] for i in range(2)]

    def prep_pe(pe):
        pe.wait_ge(s_kf, 16)
        pe.wait_ge(evac, done(Q0["wo"]))
        for n, x in enumerate(rope_tiles()):
            pe.wait_ge(rope_c, done(n - 3))
            pe.matmul(M.pair(n % 4, 0, SEQ), kf_rot, x, start=True, stop=True).then_inc(rope_r, 1)
        for g in range(4):
            pe.wait_ge(rope_c, done(10))
            for t0, tn in BOTH:
                mm = pe.matmul(M.pair(g, t0, t0 + tn), (kf_low, kf_high)[g % 2], M.k_[:, g // 2, t0:t0 + tn],
                               start=True, stop=True)
            mm.then_inc(turn_t, 1)
        pe.wait_ge(turn_c, done(2))
        for t in range(6):
            for c in range(2):
                at = t * 256 + c * P
                mm = pe.transpose(M.ps[:, at:at + P], M.v_[:, c, t * P:(t + 1) * P], ident)
        mm.then_inc(turn_t, 1)

    def prep_dve(dve):
        dve.wait_ge(s_kf, 16)
        dve.wait_ge(evac, done(Q0["wo"]))
        for n, x in enumerate(rope_tiles()):
            dve.tensor_tensor(M.gate[:, n % 2, 0:SEQ], x, kf_cos, ALU.mult)
            dve.wait_ge(rope_r, done(n + 1))
            dve.tensor_tensor(M.pair(n % 4, 0, SEQ), M.pair(n % 4, 0, SEQ), kf_sin, ALU.mult)
            dve.drain()
            dve.tensor_tensor(x, M.pair(n % 4, 0, SEQ), M.gate[:, n % 2, 0:SEQ], ALU.add).then_inc(rope_c, 1)

    def prep_act(act):
        for g in range(4):
            act.wait_ge(turn_t, done(g + 1))
            act.activation(M.kd[:, g, :], M.pair(g), ACT.Copy).then_inc(turn_c, 1)
        act.wait_ge(turn_t, done(5))
        act.activation(M.vt[:, :, :].rearrange("p t c -> p (t c)"), M.ps[:, 0:1536], ACT.Copy).then_inc(turn_c, 1)

    def units1():
        out_ = []
        for i in range(4):
            lo, hi = max(i - 1, 0), min(i + 1, 3)
            nb = (hi - lo + 1) * P
            for r in range(4):
                half = HD * (r % 2)
                q = M.qg[half:half + HD, r // 2, i * P:(i + 1) * P]
                k = M.kg[half:half + HD, :]
                masks = []
                if lo < i:
                    masks.append((0, P, M.kf[:, kf_mask:kf_mask + P]))
                if hi > i:
                    masks.append((nb - P, P, M.kf[:, kf_mask + P:kf_mask + 2 * P]))
                keys = [(0, nb, k[:, lo * P:(hi + 1) * P], masks)]
                for at in range(0, CTX, P):
                    keys.append((nb + at, P, k[:, SEQ + at:SEQ + at + P], []))
                out_.append(Unit(q, keys, M.sinkg[:, 0, r:r + 1], M.sinkg[:, 1, r:r + 1],
                                 [M.vg[:, t, :] for t in list(range(lo, hi + 1)) + [4, 5]],
                                 M.o_t[:, i, r * HD:(r + 1) * HD]))
        return out_

    def attn_pe(pe):
        pe.wait_ge(turn_c, done(5))
        with pe.Fori(0, 4) as g:
            pe.wait_ge(grp_ready, done(g + 1))
            att_pe(pe, units1(), 16 * g)
            pe.wait_ge(att_e, done(16 * g + 16))
            for c in range(2):
                for i in range(4):
                    mm = pe.transpose(M.pair(0, c * SEQ + i * P, c * SEQ + (i + 1) * P),
                                      M.o_t[:, i, c * P:(c + 1) * P], ident)
            mm.then_inc(otr_t, 1)

    def attn_dve(dve):
        dve.wait_ge(turn_c, done(5))
        with dve.Fori(0, 4) as g:
            dve.wait_ge(otr_t, done(g))
            dve.tensor_copy(M.qg[:, :, :], M.q_[:, bass.ds(2 * g, 2), :])
            dve.tensor_copy(M.kg[:, :], M.kd[:, bass.ds(g, 1), :].rearrange("p a t -> p (a t)"))
            dve.tensor_copy(M.vg[:, :, :], M.vt[:, :, bass.ds(HD * g, HD)])
            dve.tensor_copy(M.sinkg[:, 0, :], M.sinks[:, bass.ds(4 * g, 4)])
            dve.tensor_copy(M.sinkg[:, 1, :], M.nsinks[:, bass.ds(4 * g, 4)])
            dve.drain().then_inc(grp_ready, 1)
            att_dve(dve, units1(), 16 * g)
            dve.wait_ge(otr_h, done(g + 1))
            dve.tensor_tensor(M.x_lo[:, bass.ds(2 * g, 2), 0:SEQ], M.pair(0, 0, 1024).rearrange("p (c t) -> p c t", c=2),
                              M.x_hi[:, bass.ds(2 * g, 2), 0:SEQ].bitcast(F32), ALU.subtract)
            dve.drain().then_inc(xa_ready, 2)

    def attn_act(act):
        with act.Fori(0, 4) as g:
            att_act(act, units1(), 16 * g)
            act.wait_ge(otr_t, done(g + 1))
            act.activation(M.x_hi[:, bass.ds(2 * g, 2), 0:SEQ], M.pair(0, 0, 1024).rearrange("p (c t) -> p c t", c=2),
                           ACT.Copy).then_inc(otr_h, 1)

    def wo_dve(dve):
        q0 = Q0["wo"]
        for m in range(8):
            dve.wait_ge(tile_done, done(q0 + m + 1))
            o = M.h[:, m, 0:SEQ]
            dve.scalar_tensor_tensor(out=o, in0=M.pair((q0 + m) % 4, 0, SEQ), scalar=M.mods[:, 48 + 16 + m, 0:1],
                                     in1=o, op0=ALU.mult, op1=ALU.add).then_inc(evac, 1)
            dve.drain().then_inc(h_ready, 1)

    class Steps:

        def __init__(self, name, names):
            self.sem, self.names, self.next = sem(name), names, 0

        def after(self, eng, name):
            eng.wait_ge(self.sem, done(self.names.index(name) + 1))

        def mark(self, ins, name):
            assert self.names[self.next] == name, (self.names[self.next], name)
            self.next += 1
            ins.then_inc(self.sem, 1)

    N4, C3 = range(4), range(3)

    def tensor_steps(n):
        last = {e: [f"{s}{n - 1}" for s in x] if n else [] for e, x in
                {-1: ["x0"], 0: ["u"], 1: ["s", "y"], 3: ["yt"]}.items()}
        own = {3: [f"tok0{n}"], 5: [f"tok1{n}", f"tok2{n}"]}
        out_ = [f"mat0{n}", f"mat1{n}"] + last[-1] + [f"m00{n}", f"m01{n}"] + last[0]
        for e in range(1, 7):
            out_ += [f"mt{e}0{n}", f"mt{e}1{n}"] + last.get(e, []) + own.get(e, [])
            out_ += [f"inv{e}0{n}", f"inv{e}1{n}"]
        return out_

    def scalar_steps(n):
        last = {e: [f"{x}{n - 1}"] if n else [] for e, x in {-1: "x0", 0: "u", 2: "sd", 3: "yt", 4: "hi"}.items()}
        own = {3: [f"tok0{n}"], 5: [f"tok1{n}", f"tok2{n}"]}
        out_ = last[-1] + last[0]
        for e in range(1, 7):
            out_ += [f"mt{e}0{n}", f"mt{e}1{n}"] + last.get(e, []) + own.get(e, [])
        return out_

    def vector_steps(n):
        last = {e: [f"{s}{n - 1}" for s in x] if n else [] for e, x in
                {1: ["st", "var"], 2: ["yn"], 3: ["y3"], 4: ["lo"]}.items()}
        out_ = [f"mask0{n}", f"lv00{n}", f"mask1{n}", f"lv01{n}"]
        out_ += [f"inv00{n}", f"lv10{n}", f"inv01{n}", f"lv11{n}"]
        for e in range(1, 7):
            for gr in (0, 1):
                out_ += [f"inv{e}{gr}{n}"] + ([f"lv{e + 1}{gr}{n}"] if e < 6 else [])
            out_ += last.get(e, [])
        return out_

    T_S = Steps("step_t", [f"head{i}" for i in range(8)] + ["kd", "vt", "mv", "rr", "bias", "out"]
                + [f"z{n}" for n in N4] + [f"a{c}" for c in C3] + [f"g{c}" for c in C3]
                + [x for c in C3 for x in (f"kk{c}", f"bonus{c}")]
                + [f"cum{c}" for c in C3]
                + [x for n in N4 for x in tensor_steps(n)] + ["x03", "u3", "y3", "yt3"])
    S_S = Steps("step_s", [x for i in range(8) for x in (f"sq{i}", f"rms{i}")]
                + ["kd", "vt", "mv", "rr", "bias", "out", "low"]
                + [f"sig{n}" for n in N4] + [f"a{c}" for c in C3] + [f"g{c}" for c in C3]
                + [f"kk{c}" for c in C3]
                + [x for c in C3 for x in (f"cend{c}", f"exp{c}")] + ["ez"]
                + [x for n in N4 for x in scalar_steps(n)] + ["x03", "u3", "sd3", "yt3", "hi3"])
    V_S = Steps("step_v", [f"head{i}" for i in range(8)] + ["out"] + ["shift"] + [f"z{n}" for n in N4]
                + [x for c in C3 for x in (f"kk{c}", f"rk{c}", f"kn{c}", f"bonus{c}")]
                + [x for c in C3 for x in (f"cend{c}", f"abc{c}")] + ["ezs"]
                + [x for n in N4 for x in vector_steps(n)] + ["var3", "yn3", "y33", "lo3"])
    s_k2 = sem("s_k2", False)
    s_rr = sem("s_rr", False)
    s_tz = sem("s_tz", False)

    k_low, k_high, k_anti = (M.ks[:, i * P:(i + 1) * P] for i in range(3))
    k_tri = M.ks[:, 3 * P:5 * P]
    k_mask4 = M.ks[:, 5 * P:9 * P]

    def k_level(e):
        return M.ks[:, (9 + e) * P:(10 + e) * P]

    rr_dram = nc.dram_tensor("rr_scratch", (6, 384), F32, kind="Internal").ap()

    def tables_act(act):
        act.wait_ge(tile_done, done(Q0["w_in"]))
        act.wait_ge(g_ready, done(4 * HALF))
        act.dma_start(M.m_rows[:, :, :], A["mem_2"][0].rearrange("(t p) d -> p t d", p=P)).then_inc(s_mem, 16)
        act.dma_start(M.ks[:, :], A["k_second"]).then_inc(s_k2, 16)
        act.dma_start(M.lw[0:32, :], A["rwkv_w2_2"][0]).then_inc(s_k2, 16)
        act.dma_start(M.lw[32:64, :], A["rwkv_a2_2"][0]).then_inc(s_k2, 16)
        act.dma_start(M.lw[64:128, :], A["rwkv_g2_2"][0]).then_inc(s_k2, 16)
        act.dma_start(M.w0b[:, :], A["rwkv_w0_2"][0:1, :].to_broadcast([P, 384])).then_inc(s_k2, 16)
        act.dma_start(M.hot[:, :], A["k_hot"]).then_inc(s_k2, 16)
        act.activation(M.relb[:, :], M.kb[:, P:P + 8], ACT.Copy)
        act.drain()
        act.dma_start(M.relb[0:32, 0:6], A["rel_bias_2"]).then_inc(s_k2, 16)

    def mem_pe(pe):
        pe.wait_ge(s_mem, 16)
        pe.wait_ge(x_ready, done(8 * (NN["final"] + 1)))
        for k in range(KD):
            pe.wait_ge(mem_ready, done(k - 3))
            for t in range(2):
                mm = pe.transpose(M.pair(k % 4, t * P, (t + 1) * P), M.m_rows[:, t, k * P:(k + 1) * P], ident)
            mm.then_inc(mem_t, 1)

    def mem_act(act):
        for k in range(KD):
            act.wait_ge(mem_t, done(k + 1))
            act.activation(M.h[:, k, SEQ:TOK], M.pair(k % 4, 0, CTX), ACT.Copy).then_inc(mem_ready, 1)

    def w_in_act(act):
        for name, n, w0_, w1_ in (("w_in", 17, 0, SEQ), ("mem_kv", 4, SEQ, TOK)):
            for it, u in chunks(act, n):
                high(act, name, it, u)
                act.wait_ge(tile_done, done(Q0[name] + 4 * it + u + 1))
                if name == "w_in":
                    dst = M.pj[:, bass.ds(4 * it + u, 1), :].rearrange("p a t -> p (a t)")
                else:
                    dst = M.mkv[:, 4 * it + u, :]
                act.activation(dst, M.pair((Q0[name] + u) % 4, w0_, w1_), ACT.Copy).then_inc(evac, 1)

    def head_tiles():
        return ([(M.pj[:, i, :], SEQ, "attn_q_norm_2") for i in range(3)] + [(M.pj[:, 3, :], SEQ, "attn_k_norm_2")]
                + [(M.pj[:, i, :], SEQ, "mem_q_norm_2") for i in (15, 16)]
                + [(M.mkv[:, i, :], CTX, "mem_k_norm_2") for i in (0, 1)])

    def mix_prep_pe(pe):
        pe.wait_ge(evac, done(Q0["w_out"]))
        pe.wait_ge(s_k2, 16 * 7)
        for i, (x, w, _) in enumerate(head_tiles()):
            S_S.after(pe, f"sq{i}")
            if i >= 4:
                V_S.after(pe, f"head{i - 4}")
            T_S.mark(pe.matmul(M.pair(i % 4, 0, w), head1, M.n_sq[:, i % 2, 0:w], start=True, stop=True), f"head{i}")
        V_S.after(pe, "head7")
        for g in (0, 1):
            mm = pe.matmul(M.ps[:, g * SEQ:(g + 1) * SEQ], (k_low, k_high)[g], M.pj[:, 3, :], start=True, stop=True)
        T_S.mark(mm, "kd")
        for t in range(4):
            mm = pe.transpose(M.pair(1, t * P, (t + 1) * P), M.pj[:, 4, t * P:(t + 1) * P], ident)
        T_S.mark(mm, "vt")
        for t in range(2):
            for c in range(2):
                at = t * 256 + c * P
                mm = pe.transpose(M.pair(2, at, at + P), M.mkv[:, 2 + c, t * P:(t + 1) * P], ident)
        T_S.mark(mm, "mv")
        T_S.mark(pe.matmul(M.ps[0:6, 3072:3072 + 384], M.relb[0:33, 0:6], M.hot[0:33, :], start=True, stop=True), "rr")
        pe.wait_ge(s_tz, 16)
        S_S.after(pe, "rr")
        for n in range(3):
            mm = pe.matmul(M.ps[:, 2048 + n * 512:2560 + n * 512], k_anti,
                           M.tz[:, 2 * n:2 * n + 2, :].rearrange("p h k -> p (h k)"), start=True, stop=True)
        T_S.mark(mm, "bias")

    def mix_prep_act(act):
        act.wait_ge(evac, done(Q0["w_out"]))
        tiles = head_tiles()
        def square(i):
            x, w, _ = tiles[i]
            if i >= 2:
                T_S.after(act, f"head{i - 2}")
            S_S.mark(act.activation(M.n_sq[:, i % 2, 0:w], x, ACT.Square), f"sq{i}")
        for i, (x, w, _) in enumerate(tiles):
            square(i)
            T_S.after(act, f"head{i}")
            if i >= 2:
                V_S.after(act, f"head{i - 2}")
            S_S.mark(act.activation(M.n_t[:, i % 2, 0:w], M.pair(i % 4, 0, w), ACT.Sqrt, scale=1.0 / HD,
                                    bias=eps_col), f"rms{i}")
        T_S.after(act, "kd")
        V_S.after(act, "head7")
        S_S.mark(act.activation(M.qg[:, :, :].rearrange("p g t -> p (g t)"), M.ps[:, 0:1024], ACT.Copy), "kd")
        T_S.after(act, "vt")
        S_S.mark(act.activation(M.kg[:, 0:SEQ], M.pair(1, 0, SEQ), ACT.Copy), "vt")
        T_S.after(act, "mv")
        S_S.mark(act.activation(M.pj[:, 3, :], M.pair(2, 0, SEQ), ACT.Copy), "mv")
        T_S.after(act, "rr")
        S_S.mark(act.activation(M.rr[0:6, :], M.ps[0:6, 3072:3072 + 384], ACT.Copy), "rr")
        S_S.after(act, "rr")
        act.dma_start(rr_dram, M.rr[0:6, :]).then_inc(s_rr, 16)
        act.wait_ge(s_rr, 16)
        skew = bass.AP(rr_dram.tensor, 0, [[1, P], [384, 6], [1, 2 * P]])
        act.dma_start(M.tz[:, :, :], skew).then_inc(s_tz, 16)
        T_S.after(act, "bias")
        S_S.mark(act.activation(M.bias[:, :, :].rearrange("p h k -> p (h k)"), M.ps[:, 2048:2048 + 1536], ACT.Copy,
                                scale=1.0 / SCALE), "bias")

    def mix_prep_dve(dve):
        dve.wait_ge(evac, done(Q0["w_out"]))
        for i, (x, w, gain) in enumerate(head_tiles()):
            S_S.after(dve, f"rms{i}")
            dve.reciprocal(M.pair(i % 4, 0, w), M.n_t[:, i % 2, 0:w])
            dve.drain()
            V_S.mark(dve.scalar_tensor_tensor(out=x, in0=x, scalar=M.col(gain), in1=M.pair(i % 4, 0, w),
                                              op0=ALU.mult, op1=ALU.mult), f"head{i}")

    def units2():
        out_ = []
        for i in range(4):
            lo = max(i - 1, 0)
            nb = (i - lo + 1) * P
            for hh in range(6):
                half, g = HD * (hh % 2), hh // 3
                out_.append(Unit(M.pj[half:half + HD, hh // 2, i * P:(i + 1) * P],
                                 [(0, nb, M.qg[half:half + HD, g, lo * P:(i + 1) * P],
                                   [(0, nb, M.bias[:, hh, 2 * P - nb:2 * P])])],
                                 M.sinks[:, 16 + hh:17 + hh], M.nsinks[:, 16 + hh:17 + hh],
                                 [M.kg[:, t * P + g * HD:t * P + (g + 1) * HD] for t in range(lo, i + 1)],
                                 M.h[:, 2 * i + hh // 4, SEQ + (hh % 4) * HD:SEQ + (hh % 4 + 1) * HD]))
        for i in range(4):
            for hh in range(4):
                half = HD * (hh % 2)
                out_.append(Unit(M.pj[half:half + HD, 15 + hh // 2, i * P:(i + 1) * P],
                                 [(0, CTX, M.mkv[half:half + HD, hh // 2, :], [])], None, None,
                                 [M.pj[:, 3, t * 256 + hh * HD:t * 256 + (hh + 1) * HD] for t in range(2)],
                                 M.o_t[:, i, hh * HD:(hh + 1) * HD]))
        return out_

    OUT_TILES = [0, 1, 2, 6, 7]

    def mix_out_pe(pe):
        pe.wait_ge(att_e, done(64 + 40))
        for n in range(5):
            for i in range(4):
                src = M.h[:, 2 * i + n // 2, SEQ + (n % 2) * P:SEQ + (n % 2 + 1) * P] if n < 3 \
                    else M.o_t[:, i, (n - 3) * P:(n - 2) * P]
                mm = pe.transpose(M.ps[:, n * 512 + i * P:n * 512 + (i + 1) * P], src, ident)
        T_S.mark(mm, "out")

    def mix_out_act(act):
        T_S.after(act, "out")
        for n, c in enumerate(OUT_TILES):
            ins = act.activation(M.x_hi[:, c, 0:SEQ], M.ps[:, n * 512:(n + 1) * 512], ACT.Copy)
        S_S.mark(ins, "out")

    def mix_out_dve(dve):
        S_S.after(dve, "out")
        for n, c in enumerate(OUT_TILES):
            ins = dve.tensor_tensor(M.x_lo[:, c, 0:SEQ], M.ps[:, n * 512:(n + 1) * 512],
                                    M.x_hi[:, c, 0:SEQ].bitcast(F32), ALU.subtract)
        V_S.mark(ins, "out")

    r_t = [M.pj[:, 5 + c, :] for c in C3]
    k_t = [M.pj[:, 8 + c, :] for c in C3]
    v_t = [M.pj[:, 11 + c, :] for c in C3]
    lor = M.pj[:, 14, :]
    g_t = [M.pj[:, c, :] for c in C3]
    kk_t = [M.pj[:, 3, :], M.pj[:, 4, :], M.pj[:, 15, :]]
    a_t = [M.av[:, c, :] for c in C3]
    bonus_t = [M.h[:, 2 * c:2 * c + 2, SEQ:TOK] for c in C3]
    H6 = range(6)

    def two(ap):
        return ap.rearrange("p (a b) -> p a b", a=2)

    def rw_pre_dve(dve):
        for i in range(10):
            x, d = M.pj[:, 5 + i, :], M.dd[:, i % 2, :]
            dve.tensor_tensor(d[:, 1:SEQ], x[:, 0:SEQ - 1], x[:, 1:SEQ], ALU.subtract)
            dve.tensor_scalar(d[:, 0:1], x[:, 0:1], -1.0, None, ALU.mult)
            dve.drain()
            ins = dve.scalar_tensor_tensor(out=x, in0=d, scalar=M.col("rwkv_mu_2", i), in1=x, op0=ALU.mult, op1=ALU.add)
        V_S.mark(ins, "shift")
        for n in N4:
            T_S.after(dve, f"z{n}")
            V_S.mark(dve.tensor_tensor(M.sig[:, n, :], M.pair(n, 0, 384), M.w0b[:, :], ALU.add), f"z{n}")
        for c in C3:
            dve.tensor_scalar(kk_t[c], k_t[c], M.col("rwkv_k_k_2", c), None, ALU.mult)
            dve.drain()
            V_S.mark(dve.tensor_tensor(M.hq[:, 0, :], kk_t[c], kk_t[c], ALU.mult), f"kk{c}")
            S_S.after(dve, f"a{c}")
            dve.tensor_scalar(M.dd[:, 0, :], a_t[c], 1.0, M.col("rwkv_k_a_2", c), ALU.subtract, ALU.mult)
            dve.drain()
            dve.scalar_tensor_tensor(out=k_t[c], in0=M.dd[:, 0, :], scalar=1.0, in1=k_t[c], op0=ALU.add, op1=ALU.mult)
            dve.drain()
            V_S.mark(dve.scalar_tensor_tensor(out=M.hq[:, 1, :], in0=r_t[c], scalar=M.col("rwkv_r_k_2", c),
                                              in1=k_t[c], op0=ALU.mult, op1=ALU.mult), f"rk{c}")
            S_S.after(dve, f"kk{c}")
            dve.tensor_scalar(M.dd[:, 1, :], M.dd[:, 1, :], L2_EPS, None, ALU.max)
            dve.drain()
            dve.reciprocal(M.dd[:, 1, :], M.dd[:, 1, :])
            dve.drain()
            V_S.mark(dve.tensor_tensor(kk_t[c], kk_t[c], M.dd[:, 1, :], ALU.mult), f"kn{c}")
            T_S.after(dve, f"bonus{c}")
            V_S.mark(dve.tensor_tensor(bonus_t[c], two(M.pair(1, 0, SEQ)), two(v_t[c]), ALU.mult), f"bonus{c}")
        for c in C3:
            S_S.after(dve, f"cend{c}")
            V_S.mark(dve.tensor_scalar(M.cend[:, 1, c, :], M.cend[:, 0, c, :], -1.0, None, ALU.mult), f"cend{c}")
            S_S.after(dve, f"exp{c}")
            dve.tensor_tensor(a_t[c], a_t[c], kk_t[c], ALU.mult)
            dve.tensor_tensor(r_t[c], r_t[c], M.ex[:, 0, :], ALU.mult)
            dve.tensor_tensor(k_t[c], k_t[c], M.ex[:, 2, :], ALU.mult)
            dve.drain()
            dve.scalar_tensor_tensor(out=kk_t[c], in0=kk_t[c], scalar=-1.0, in1=M.ex[:, 1, :],
                                     op0=ALU.mult, op1=ALU.mult)
            dve.tensor_tensor(a_t[c], a_t[c], M.ex[:, 2, :], ALU.mult)
            V_S.mark(dve.drain(), f"abc{c}")
        V_S.mark(dve.tensor_tensor(M.cend[:, 2, :, 0:3], M.cend[:, 0, :, 0:3], M.cend[:, 0, :, 1:4], ALU.add), "ezs")

    def rw_pre_act(act):
        V_S.after(act, "shift")
        act.activation(lor[0:32, :], lor[0:32, :], ACT.Tanh)
        S_S.mark(act.activation(lor[64:128, :], lor[64:128, :], ACT.Sigmoid), "low")
        for n in N4:
            V_S.after(act, f"z{n}")
            S_S.mark(act.activation(M.sig[:, n, :], M.sig[:, n, :], ACT.Sigmoid), f"sig{n}")
        for c in C3:
            T_S.after(act, f"a{c}")
            S_S.mark(act.activation(a_t[c], M.pair(c, 0, SEQ), ACT.Sigmoid, bias=M.col("rwkv_a0_2", c)), f"a{c}")
        for c in C3:
            T_S.after(act, f"g{c}")
            S_S.mark(act.activation(g_t[c], M.pair(c, SEQ, 2 * SEQ), ACT.Copy), f"g{c}")
        for c in C3:
            T_S.after(act, f"kk{c}")
            if c:
                V_S.after(act, f"kn{c - 1}")
            V_S.after(act, f"rk{c}")
            S_S.mark(act.activation(M.dd[:, 1, :], M.pair(0, 0, SEQ), ACT.Sqrt), f"kk{c}")
        for c in C3:
            T_S.after(act, f"cum{c}")
            if c:
                V_S.after(act, f"abc{c - 1}")
            ps = M.pair(2 * (c % 2) if c < 2 else 0, 0, 1024).rearrange("p (n s t) -> p n s t", n=4, s=2)
            S_S.mark(act.activation(M.cend[:, 0, c, :], ps[:, :, 0, P - 1], ACT.Copy, scale=KAPPA / 2), f"cend{c}")
            V_S.after(act, f"cend{c}")
            for n in N4:
                t = slice(n * P, (n + 1) * P)
                plus, minus = M.cend[:, 0, c, n:n + 1], M.cend[:, 1, c, n:n + 1]
                act.activation(M.ex[:, 0, t], ps[:, n, 0, :], ACT.Exp, scale=-KAPPA, bias=plus)
                act.activation(M.ex[:, 1, t], ps[:, n, 1, :], ACT.Exp, scale=-KAPPA, bias=plus)
                ins = act.activation(M.ex[:, 2, t], ps[:, n, 0, :], ACT.Exp, scale=KAPPA, bias=minus)
            S_S.mark(ins, f"exp{c}")
        V_S.after(act, "ezs")
        S_S.mark(act.activation(M.cend[:, 3, :, 0:3], M.cend[:, 2, :, 0:3], ACT.Exp, scale=-1.0), "ez")

    def rw_pre_pe(pe):
        S_S.after(pe, "low")
        V_S.after(pe, "out")
        for n in N4:
            T_S.mark(pe.matmul(M.pair(n, 0, 384), lor[0:32, n * P:(n + 1) * P], M.lw[0:32, :], start=True, stop=True),
                     f"z{n}")
        for c in C3:
            V_S.after(pe, f"z{c}")
            T_S.mark(pe.matmul(M.pair(c, 0, SEQ), M.lw[32:64, c * P:(c + 1) * P], lor[32:64, :], start=True, stop=True),
                     f"a{c}")
        for c in C3:
            T_S.mark(pe.matmul(M.pair(c, SEQ, 2 * SEQ), M.lw[64:128, c * P:(c + 1) * P], lor[64:128, :],
                               start=True, stop=True), f"g{c}")
        for c in C3:
            V_S.after(pe, f"kk{c}")
            S_S.after(pe, f"a0" if c == 0 else f"kk{c - 1}")
            T_S.mark(pe.matmul(M.pair(0, 0, SEQ), head1, M.hq[:, 0, :], start=True, stop=True), f"kk{c}")
            V_S.after(pe, f"rk{c}")
            S_S.after(pe, "a1")
            if c:
                V_S.after(pe, f"bonus{c - 1}")
            T_S.mark(pe.matmul(M.pair(1, 0, SEQ), head1, M.hq[:, 1, :], start=True, stop=True), f"bonus{c}")
        for c in C3:
            V_S.after(pe, "bonus2")
            S_S.after(pe, "g2" if c < 2 else "exp0")
            pr = 2 * (c % 2) if c < 2 else 0
            if c == 0:
                S_S.after(pe, "kk2")
            for n in N4:
                mm = pe.matmul(M.pair(pr, n * 256, (n + 1) * 256), M.sig[:, n, c * P:(c + 1) * P], k_tri,
                               start=True, stop=True)
            T_S.mark(mm, f"cum{c}")

    def head_rows(hh):
        return slice(HD * (hh % 2), HD * (hh % 2) + HD)

    def by_parity(hh):
        at = (6 + hh % 2) * 512 + (hh // 2) * HD
        return M.ps[:, at:at + HD]

    def bank(b, n=384, at=0):
        return M.ps[:, b * 512 + at:b * 512 + at + n]

    def heads(ap, h=3):
        return ap.rearrange("p (h x) -> p h x", h=h)

    def of_parity(ap, p):
        return ap.rearrange("p (c a x) -> p a c x", c=3, a=2)[:, p, :, :]

    STATE_AT = 256
    GROUPS = ((0, range(0, 3)), (1, range(3, 6)))

    def rw_pe(pe):
        def mats(n, gr, hs):
            if n:
                V_S.after(pe, f"inv6{gr}{n - 1}")
            t = slice(n * P, (n + 1) * P)
            for hh in hs:
                r, c = head_rows(hh), hh // 2
                for q_, (lhs, rhs) in enumerate(((a_t, kk_t), (a_t, r_t), (k_t, kk_t), (k_t, r_t))):
                    mm = pe.matmul(bank(hh, P, q_ * P), lhs[c][r, t], rhs[c][r, t], start=True, stop=True)
            T_S.mark(mm, f"mat{gr}{n}")

        def first_level(n, gr, hs):
            V_S.after(pe, f"lv0{gr}{n}")
            for i, hh in enumerate(hs):
                mm = pe.transpose(bank(3 * gr, P, i * P), M.lv[:, hh, :], ident)
            T_S.mark(mm, f"m0{gr}{n}")

        def level_times_inv(n, e, gr, hs):
            V_S.after(pe, f"lv{e}{gr}{n}")
            for i, hh in enumerate(hs):
                mm = pe.matmul(bank(3 * gr, P, i * P), M.lv[:, hh, :], M.inv[:, hh, :], start=True, stop=True)
            T_S.mark(mm, f"mt{e}{gr}{n}")

        def inv_step(n, e, gr, hs):
            S_S.after(pe, f"mt{e}{gr}{n}")
            inv_t = M.inv_t[n % 2]
            if e < 6:
                for i, hh in enumerate(hs):
                    pe.matmul(bank(3 * gr + 1, P, i * P), inv_t[:, hh, :], M.mt[:, hh, :], start=True, stop=True)
            for i, hh in enumerate(hs):
                mm = pe.matmul(bank(3 * gr + 2, P, i * P), M.mt[:, hh, :], inv_t[:, hh, :], start=True, stop=True)
            T_S.mark(mm, f"inv{e}{gr}{n}")

        def tokens(n, q_):
            t = slice(n * P, (n + 1) * P)
            if q_ == 0:
                if n:
                    V_S.after(pe, f"yn{n - 1}")
            else:
                S_S.after(pe, f"tok{q_ - 2}{n}" if q_ == 2 else f"yt{n - 1}") if q_ == 2 or n else None
            for c in C3:
                mm = pe.transpose(bank((7, 6, 7)[q_], P, c * P), (a_t, k_t, v_t)[q_][c][:, t], ident)
            T_S.mark(mm, f"tok{q_}{n}")

        def x0(n):
            S_S.after(pe, f"tok2{n}")
            if n:
                V_S.after(pe, f"st{n - 1}")
            t = slice(n * P, (n + 1) * P)
            for hh in H6:
                r, c = head_rows(hh), hh // 2
                mm = pe.matmul(by_parity(hh), M.m4[:, n % 2, hh, 2 * P:3 * P], M.tok[:, 2, hh * HD:(hh + 1) * HD],
                               start=True, stop=(n == 0))
                if n:
                    mm = pe.matmul(by_parity(hh), kk_t[c][r, t], M.z[r, c, :], start=False, stop=True)
            T_S.mark(mm, f"x0{n}")

        def u(n):
            S_S.after(pe, f"x0{n}")
            for hh in H6:
                mm = pe.matmul(bank(6, HD, hh * HD), M.inv_t[n % 2][:, hh, :], M.x0[:, hh * HD:(hh + 1) * HD],
                               start=True, stop=True)
            T_S.mark(mm, f"u{n}")

        def state(n):
            S_S.after(pe, f"u{n}")
            for hh in H6:
                r, c = head_rows(hh), hh // 2
                at = 7 * 512 + STATE_AT + c * HD
                o = M.ps[r, at:at + HD]
                pe.matmul(o, M.tok[:, 0, hh * HD:(hh + 1) * HD], M.u[:, hh * HD:(hh + 1) * HD],
                          start=True, stop=False)
                mm = pe.matmul(o, M.tok[:, 1, hh * HD:(hh + 1) * HD], M.tok[:, 2, hh * HD:(hh + 1) * HD],
                               start=False, stop=True)
            T_S.mark(mm, f"s{n}")

        def y(n):
            S_S.after(pe, f"u{n}")
            t = slice(n * P, (n + 1) * P)
            for hh in H6:
                r, c = head_rows(hh), hh // 2
                o = by_parity(hh)
                pe.matmul(o, M.m4[:, n % 2, hh, 3 * P:4 * P], M.tok[:, 2, hh * HD:(hh + 1) * HD],
                          start=True, stop=False)
                mm = pe.matmul(o, M.m4[:, n % 2, hh, P:2 * P], M.u[:, hh * HD:(hh + 1) * HD],
                               start=False, stop=(n == 0))
                if n:
                    mm = pe.matmul(o, r_t[c][r, t], M.z[r, c, :], start=False, stop=True)
            T_S.mark(mm, f"y{n}")

        def turned(n):
            V_S.after(pe, f"yn{n}")
            for c in C3:
                mm = pe.transpose(bank(6, P, c * P), M.y[:, c * P:(c + 1) * P], ident)
            T_S.mark(mm, f"yt{n}")

        V_S.after(pe, "ezs")
        for n in N4:
            for gr, hs in GROUPS:
                mats(n, gr, hs)
            if n:
                x0(n - 1)
            for gr, hs in GROUPS:
                first_level(n, gr, hs)
            if n:
                u(n - 1)
            for e in range(1, 7):
                for gr, hs in GROUPS:
                    level_times_inv(n, e, gr, hs)
                if n and e == 1:
                    state(n - 1)
                    y(n - 1)
                if e == 3:
                    if n:
                        turned(n - 1)
                    tokens(n, 0)
                if e == 5:
                    tokens(n, 1)
                    tokens(n, 2)
                for gr, hs in GROUPS:
                    inv_step(n, e, gr, hs)
        V_S.after(pe, "inv613")
        x0(3)
        u(3)
        y(3)
        turned(3)

    def rw_act(act):
        def x0(n):
            T_S.after(act, f"x0{n}")
            for p in (0, 1):
                ins = act.activation(of_parity(M.x0[:, :], p), heads(bank(6 + p, 192)), ACT.Copy)
            S_S.mark(ins, f"x0{n}")

        def u(n):
            T_S.after(act, f"u{n}")
            S_S.mark(act.activation(M.u[:, :], bank(6), ACT.Copy), f"u{n}")

        def deviation(n):
            V_S.after(act, f"var{n}")
            S_S.mark(act.activation(M.gn[:, 2, :], M.gn[:, 1, :], ACT.Sqrt, scale=1.0 / HD, bias=gn_eps_col), f"sd{n}")

        def turned(n):
            T_S.after(act, f"yt{n}")
            for c in C3:
                ins = act.activation(M.y1[:, c, :], bank(6, P, c * P), ACT.Identity,
                                     scale=M.col("rwkv_ln_w_2", c), bias=M.col("rwkv_ln_b_2", c))
            S_S.mark(ins, f"yt{n}")

        def high_part(n):
            V_S.after(act, f"y3{n}")
            S_S.mark(act.activation(M.x_hi[:, 3:6, n * P:(n + 1) * P], M.y1[:, :, :], ACT.Copy), f"hi{n}")

        def tokens(n, q_):
            T_S.after(act, f"tok{q_}{n}")
            S_S.mark(act.activation(M.tok[:, q_, :], bank((7, 6, 7)[q_]), ACT.Copy), f"tok{q_}{n}")

        for n in N4:
            if n:
                x0(n - 1)
                u(n - 1)
            for e in range(1, 7):
                for gr in (0, 1):
                    T_S.after(act, f"mt{e}{gr}{n}")
                    S_S.mark(act.activation(M.mt[:, 3 * gr:3 * gr + 3, :], heads(bank(3 * gr)), ACT.Copy),
                             f"mt{e}{gr}{n}")
                if n and e == 2:
                    deviation(n - 1)
                if n and e == 3:
                    turned(n - 1)
                if n and e == 4:
                    high_part(n - 1)
                for q_ in {3: (0,), 5: (1, 2)}.get(e, ()):
                    tokens(n, q_)
        for step in (x0, u, deviation, turned, high_part):
            step(3)

    def rw_dve(dve):
        eye3 = ident.unsqueeze(1).to_broadcast([P, 3, P])

        def level(n, e, gr):
            hs = slice(3 * gr, 3 * gr + 3)
            V_S.mark(dve.tensor_tensor(M.lv[:, hs, :], M.m4[:, n % 2, hs, 0:P],
                                       k_level(e).unsqueeze(1).to_broadcast([P, 3, P]), ALU.mult), f"lv{e}{gr}{n}")

        def masked(n, gr):
            hs = slice(3 * gr, 3 * gr + 3)
            T_S.after(dve, f"mat{gr}{n}")
            V_S.mark(dve.copy_predicated(M.m4[:, n % 2, hs, :],
                                         k_mask4.bitcast(U32).unsqueeze(1).to_broadcast([P, 3, 512]),
                                         heads(M.ps[:, 1536 * gr:1536 * (gr + 1)])), f"mask{gr}{n}")
            V_S.after(dve, f"mask{gr}{n}")
            level(n, 0, gr)

        def inv_start(n, gr):
            hs = slice(3 * gr, 3 * gr + 3)
            V_S.after(dve, f"lv0{gr}{n}")
            dve.tensor_tensor(M.inv_t[n % 2][:, hs, :], M.lv[:, hs, :], eye3, ALU.add)
            T_S.after(dve, f"m0{gr}{n}")
            dve.tensor_tensor(M.inv[:, hs, :], heads(bank(3 * gr)), eye3, ALU.add)
            V_S.mark(dve.drain(), f"inv0{gr}{n}")
            level(n, 1, gr)

        def inv_sums(n, e, gr):
            hs = slice(3 * gr, 3 * gr + 3)
            inv, inv_t = M.inv[:, hs, :], M.inv_t[n % 2][:, hs, :]
            T_S.after(dve, f"inv{e}{gr}{n}")
            if e < 6:
                dve.tensor_tensor(inv, heads(bank(3 * gr + 1)), inv, ALU.add)
            dve.tensor_tensor(inv_t, heads(bank(3 * gr + 2)), inv_t, ALU.add)
            V_S.mark(dve.drain(), f"inv{e}{gr}{n}")
            if e < 6:
                level(n, e + 1, gr)

        y6, q6 = heads(M.y[:, :], 6), heads(M.ysq[:, :], 6)

        def over_head(i):
            return M.gn[:, i, :].unsqueeze(2).to_broadcast([P, 6, HD])

        def state_and_variance(n):
            T_S.after(dve, f"y{n}")
            if n < 3:
                ps_s = M.ps[:, 7 * 512 + STATE_AT:7 * 512 + STATE_AT + 192].rearrange("p (c x) -> p c x", c=3)
                if n:
                    dve.tensor_tensor(M.z[:, :, :], ps_s, M.z[:, :, :], ALU.add)
                    dve.drain()
                for c in C3:
                    src = M.z[:, c, :] if n else ps_s[:, c, :]
                    ins = dve.tensor_scalar(M.z[:, c, :], src, M.cend[:, 3, c, n:n + 1], None, ALU.mult)
                V_S.mark(ins, f"st{n}")
            y_ps = [heads(bank(6 + p, 192)) for p in (0, 1)]
            for p in (0, 1):
                dve.tensor_reduce(M.gn[:, 0, p:6:2], y_ps[p], AX.X, ALU.add)
            dve.drain()
            dve.tensor_scalar(M.gn[:, 0, :], M.gn[:, 0, :], -1.0 / HD, None, ALU.mult)
            dve.drain()
            for p in (0, 1):
                dve.tensor_tensor(of_parity(M.y[:, :], p), y_ps[p],
                                  M.gn[:, 0, p:6:2].unsqueeze(2).to_broadcast([P, 3, HD]), ALU.add)
            dve.drain()
            dve.tensor_tensor(q6, y6, y6, ALU.mult)
            dve.drain()
            V_S.mark(dve.tensor_reduce(M.gn[:, 1, :], q6, AX.X, ALU.add), f"var{n}")

        def normed(n):
            S_S.after(dve, f"sd{n}")
            dve.reciprocal(M.gn[:, 3, :], M.gn[:, 2, :])
            dve.drain()
            V_S.mark(dve.tensor_tensor(y6, y6, over_head(3), ALU.mult), f"yn{n}")

        def gated(n):
            S_S.after(dve, f"yt{n}")
            for c in C3:
                b = M.h[:, 2 * c + n // 2, SEQ + (n % 2) * P:SEQ + (n % 2 + 1) * P]
                dve.tensor_tensor(M.y1[:, c, :], M.y1[:, c, :], b, ALU.add)
            dve.drain()
            V_S.mark(dve.tensor_tensor(M.y1[:, :, :], M.y1[:, :, :], M.pj[:, 0:3, n * P:(n + 1) * P], ALU.mult), f"y3{n}")

        def low_part(n):
            S_S.after(dve, f"hi{n}")
            V_S.mark(dve.tensor_tensor(M.x_lo[:, 3:6, n * P:(n + 1) * P], M.y1[:, :, :],
                                       M.x_hi[:, 3:6, n * P:(n + 1) * P].bitcast(F32), ALU.subtract), f"lo{n}")

        of_last = {1: state_and_variance, 2: normed, 3: gated, 4: low_part}
        dve.wait_ge(zero_ready, done(3))
        for n in N4:
            for gr in (0, 1):
                masked(n, gr)
            for gr in (0, 1):
                inv_start(n, gr)
            for e in range(1, 7):
                for gr in (0, 1):
                    inv_sums(n, e, gr)
                if n and e in of_last:
                    of_last[e](n - 1)
        for step in (state_and_variance, normed, gated, low_part):
            step(3)

    def w_out_dve(dve):
        q0 = Q0["w_out"]
        for m in range(8):
            dve.wait_ge(tile_done, done(q0 + m + 1))
            o = M.h[:, m, 0:SEQ]
            dve.tensor_tensor(o, M.pair((q0 + m) % 4, 0, SEQ), o, ALU.add).then_inc(evac, 1)
            dve.drain().then_inc(h_ready, 1)

    M.n_param_dma = count_param_dmas()
    block = ctx.enter_context(nc.Block())

    if True:
        @block.sync
        def _(sp):
            prime(sp, [])
            start_sp(sp)
            for name in used_streams:
                if name == "pw1":
                    pw1_sp(sp)
                else:
                    load_stream(sp, name)
                if name == "qkv":
                    sp.wait_ge(tile_done, done(Q0["qkv"] + 1))
                    sp.dma_start(M.kf[:, :], A["k_first"]).then_inc(s_kf, 16)
            finish_sp(sp)

        @block.gpsimd
        def _(pool):
            prime(pool, [lo_ready, zero_ready])
            pool.memset(M.p_rows[:, PT - 1, :], 0.0)
            pool.memset(M.one[:, 0:1], EPS)
            pool.memset(M.one[:, 1:2], GN_EPS)
            pool.memset(M.one[:, 2:8], 0.0)
            pool.drain().then_inc(zero_ready, 1)
            if "pw1" in order:
                pool.wait_ge(start_c, done(3 + KD))
                pool.memset(M.vp[:, :, :], 0.0).then_inc(zero_ready, 1)
            for name in used_streams:
                if name == "w_out":
                    V_S.after(pool, "abc2")
                    pool.memset(M.m4[:, :, :, :], 0.0).then_inc(zero_ready, 1)
                low_stream(pool, name)

        @block.scalar
        def _(act):
            prime(act, [mod_rows, hi_ready, start_c, sc_ready, sq_ready, rms_ready, y_ready, gate_ready, cv_ready,
                        mid_ready, silu_ready, ghi_ready, f_res, mem_ready, turn_c, att_p, att_c, att_e, otr_h, S_S.sem])
            ada_first_load(act)
            act.wait_ge(zero_ready, done(1))
            start_act(act)
            if q_end:
                high_first(act)
            for st in order:
                if st == "final":
                    tables_act(act)
                if st == "mix":
                    mem_act(act)
                if st in NN:
                    norm_act(act, st)
                if st == "w_in":
                    w_in_act(act)
                if st == "mixers":
                    mix_prep_act(act)
                    att_act(act, units2(), 64)
                    mix_out_act(act)
                    rw_pre_act(act)
                    rw_act(act)
                if st == "w_out":
                    plain_high(act, "w_out")
                if st == "pw1":
                    pw1_act(act)
                    act.wait_ge(mod_ready, done(2))
                if st == "pw2":
                    pw2_act(act)
                if st == "qkv":
                    qkv_act(act)
                if st == "attn":
                    prep_act(act)
                    attn_act(act)
                if st == "wo":
                    plain_high(act, "wo")
                if st in ("ffn0", "ffn1", "ffn2"):
                    b, w = int(st[3]), TOK if st == "ffn0" else SEQ
                    for hf in (0, 1):
                        up_act(act, b, hf, w)
                        plain_high(act, f"down{b}{hf}")

        @block.tensor
        def _(pe):
            prime(pe, [mod_t, tile_done, ada_used, start_t, sq_used, mu_ready, mem_t, out_t, rope_r, turn_t, att_s, att_t, att_o, otr_t, T_S.sem])
            start_pe(pe)
            for st in order:
                if st == "ln":
                    mean_pe(pe)
                if st == "mix":
                    mem_pe(pe)
                if st in NN:
                    norm_pe(pe, st)
                if st == "n10":
                    ada_pe(pe)
                if st == "w_in":
                    pe.wait_ge(x_ready, done(8 * (NN["mix"] + 1)))
                    stream_pe(pe, "w_in", lambda it, u: LAT)
                    stream_pe(pe, "mem_kv", lambda it, u: MEM)
                if st == "mixers":
                    mix_prep_pe(pe)
                    S_S.after(pe, "bias")
                    att_pe(pe, units2(), 64)
                    mix_out_pe(pe)
                    rw_pre_pe(pe)
                    rw_pe(pe)
                if st == "w_out":
                    V_S.after(pe, "lo3")
                    stream_pe(pe, "w_out", lambda it, u: LAT)
                if st == "pw1":
                    pw1_pe(pe)
                if st == "pw2":
                    pe.wait_ge(x_ready, done(8 * (NN["ln"] + 1)))
                    stream_pe(pe, "pw2", lambda it, u: BOTH)
                if st == "qkv":
                    pe.wait_ge(x_ready, done(8 * (NN["n11"] + 1)))
                    stream_pe(pe, "qkv", qkv_segs)
                if st == "attn":
                    prep_pe(pe)
                    attn_pe(pe)
                if st == "wo":
                    pe.wait_ge(xa_ready, done(8))
                    stream_pe(pe, "wo", lambda it, u: LAT)
                if st in ("ffn0", "ffn1", "ffn2"):
                    b, segs = int(st[3]), BOTH if st == "ffn0" else LAT
                    pe.wait_ge(x_ready, done(8 * (NN[["n20", "n21", "ffn2_norm"][b]] + 1)))
                    for hf in (0, 1):
                        stream_pe(pe, f"up{b}{hf}", lambda it, u: segs)
                        stream_pe(pe, f"down{b}{hf}", lambda it, u: segs, from_g=HALF * (2 * b + hf + 1))
            finish_pe(pe)

        @block.vector
        def _(dve):
            prime(dve, [evac, mod_ready, rstd_ready, t_ready, x_ready, h_ready, v_ready, tap_done, cv_cent,
                        taps_ready, prod_ready, g_ready, out_c, rope_c, grp_ready, att_m, att_r, xa_ready, V_S.sem])
            dve.wait_ge(start_c, done(3 + KD))
            dve.drain().then_inc(h_ready, 8)
            for st in order:
                if st == "ln":
                    mean_dve(dve)
                if st in NN:
                    norm_dve(dve, st)
                if st == "mixers":
                    mix_prep_dve(dve)
                    S_S.after(dve, "bias")
                    att_dve(dve, units2(), 64)
                    mix_out_dve(dve)
                    rw_pre_dve(dve)
                    rw_dve(dve)
                if st == "w_out":
                    w_out_dve(dve)
                if st == "pw1":
                    pw1_dve(dve)
                    ada_rest_dve(dve)
                if st == "pw2":
                    pw2_dve(dve)
                if st == "attn":
                    prep_dve(dve)
                    attn_dve(dve)
                if st == "wo":
                    wo_dve(dve)
                if st in ("ffn0", "ffn1", "ffn2"):
                    b, w = int(st[3]), TOK if st == "ffn0" else SEQ
                    for hf in (0, 1):
                        up_dve(dve, b, hf, w)
                        down_dve(dve, b, hf, w)
            finish_dve(dve)


_INS = ["x", "c", "ctx", "c_ctx", "ada_w", "ada_b", "norm1_g", "norm2_g", "final_g", "conv_w_pw1", "conv_b_pw1",
        "conv_w_dw", "conv_b_dw", "conv_ln_g", "conv_ln_b", "conv_w_pw2", "conv_b_pw2", "attn_w_qkv", "attn_w_o",
        "attn_sink", "ffn_w_up", "ffn_w_dw", "ffn_b_dw", "ffn_w_down", "mem_2", "rel_bias_2", "mix_norm_g_2",
        "w_in_2", "attn_q_norm_2", "attn_k_norm_2", "attn_sinks_2", "rwkv_mu_2", "rwkv_w0_2", "rwkv_w2_2",
        "rwkv_a0_2", "rwkv_a2_2", "rwkv_g2_2", "rwkv_k_k_2", "rwkv_k_a_2", "rwkv_r_k_2", "rwkv_ln_w_2",
        "rwkv_ln_b_2", "mem_norm_g_2", "w_mem_kv_2", "mem_q_norm_2", "mem_k_norm_2", "w_out_2", "ffn_norm_g_2",
        "w_up_2", "conv_w_2", "conv_b_2", "w_down_2"]
_OUT_SHAPE = (1, SEQ, D)


def kernel(**inputs):
    import numpy as _np
    import concourse.bacc as _bacc
    from concourse import mybir as _mybir
    from concourse.bass_utils import run_bass_kernel_spmd as _run

    nc = _bacc.Bacc("TRN2", target_bir_lowering=False, num_devices=1)
    arrays, aps = {}, {}
    given = {name: _np.ascontiguousarray(inputs[name]) for name in _INS}
    for name, a in list(given.items()) + list(constants().items()):
        arrays[f"in_{name}"] = a
        aps[name] = nc.dram_tensor(f"in_{name}", a.shape, _mybir.dt.from_np(a.dtype), kind="ExternalInput").ap()
    out = nc.dram_tensor("out_0", _OUT_SHAPE, F32, kind="ExternalOutput").ap()
    build(nc, aps, out)
    r = _run(nc, [arrays], core_ids=[0])
    return r.results[0]["out_0"]
```

```python
from contextlib import ExitStack

import concourse.bass as bass
from concourse import mybir
import numpy as np

P = 128
D = 1024
KD = D // P
SEQ = 512
CTX = 256
TOK = SEQ + CTX
DFF = 2816
FT = DFF // P
HALF = FT // 2
HD = 64
TAPS = 31
PAD = TAPS // 2
EPS = 1e-6
GN_EPS = 64e-5
L2_EPS = 1e-12
KAPPA = float(np.exp(-0.5))
NEG = -1e30

F32 = mybir.dt.float32
F32R = mybir.dt.float32r
U32 = mybir.dt.uint32
ALU = mybir.AluOpType
ACT = mybir.ActivationFunctionType
AX = mybir.AxisListType

LEAD = 8


def done(n):
    return n + LEAD


PARAM_ROWS = [
    ("c", 8), ("c_ctx", 8), ("ada_b", 96), ("norm1_g", 16), ("norm2_g", 16), ("final_g", 8),
    ("conv_b_pw1", 16), ("conv_w_dw", 8 * TAPS), ("conv_b_dw", 8), ("conv_ln_g", 8), ("conv_ln_b", 8),
    ("conv_b_pw2", 8), ("ffn_w_dw", 2 * 3 * 2 * FT), ("ffn_b_dw", 2 * 2 * FT),
    ("mix_norm_g_2", 8), ("mem_norm_g_2", 8), ("ffn_norm_g_2", 8), ("conv_w_2", 3 * 2 * FT),
    ("conv_b_2", 2 * FT), ("rwkv_mu_2", 10), ("rwkv_a0_2", 3), ("rwkv_k_k_2", 3), ("rwkv_k_a_2", 3),
    ("rwkv_r_k_2", 3), ("rwkv_ln_w_2", 3), ("rwkv_ln_b_2", 3),
    ("attn_q_norm_2", 1), ("attn_k_norm_2", 1), ("mem_q_norm_2", 1), ("mem_k_norm_2", 1),
]
COL, _n = {}, 0
for _name, _rows in PARAM_ROWS:
    COL[_name] = _n
    _n += _rows
N_ROWS = _n
PT = -(-N_ROWS // P)

STREAMS = [("pw1", 16, 8), ("pw2", 8, 8)]
for _h in (0, 1):
    STREAMS += [(f"up0{_h}", 2 * HALF, 8), (f"down0{_h}", 8, HALF)]
STREAMS += [("qkv", 12, 8), ("wo", 8, 8)]
for _h in (0, 1):
    STREAMS += [(f"up1{_h}", 2 * HALF, 8), (f"down1{_h}", 8, HALF)]
STREAMS += [("w_in", 17, 8), ("mem_kv", 4, 8), ("w_out", 8, 8)]
for _h in (0, 1):
    STREAMS += [(f"up2{_h}", 2 * HALF, 8), (f"down2{_h}", 8, HALF)]
Q0, ROWS_OF, _q = {}, {}, 0
ROWS_AT = []
for _name, _chunks, _rows in STREAMS:
    Q0[_name], ROWS_OF[_name] = _q, _rows
    ROWS_AT += [_rows] * _chunks
    _q += _chunks
N_CHUNKS = dict((s[0], s[1]) for s in STREAMS)
Q_ALL = _q

ADA_FIRST = 2 * D // 256

NORMS = ["n10", "ln", "n20", "n11", "n21", "final", "mix", "ffn2_norm"]
NN = {s: i for i, s in enumerate(NORMS)}


def constants():
    eye = np.eye(P, dtype=np.float32)
    ones = np.ones((P, P), np.float32)
    head = np.kron(np.eye(2, dtype=np.float32), np.ones((HD, HD), np.float32))
    base = np.concatenate([eye, ones, head], 1)

    rot = np.zeros((P, P), np.float32)
    for h in (0, HD):
        for d in range(HD // 2):
            rot[h + d + HD // 2, h + d] = -1.0
            rot[h + d, h + d + HD // 2] = 1.0
    low = np.zeros((P, P), np.float32)
    high = np.zeros((P, P), np.float32)
    for d in range(HD):
        low[d, d] = low[d, d + HD] = 1.0
        high[d + HD, d] = high[d + HD, d + HD] = 1.0
    n_freq = HD // 4
    inv = np.float32(10000.0) ** (-np.arange(n_freq, dtype=np.float32) / np.float32(n_freq))
    pos = np.arange(SEQ)
    row, col = (pos // 64).astype(np.float32), (pos % 64).astype(np.float32)
    ang = np.concatenate([row[None] * inv[:, None], col[None] * inv[:, None]], 0).astype(np.float32)
    cos, sin = np.tile(np.cos(ang), (4, 1)), np.tile(np.sin(ang), (4, 1))
    q, k = np.arange(P)[:, None], np.arange(P)[None]
    before = np.where(k >= q, 0.0, NEG).astype(np.float32)
    after = np.where(k <= q, 0.0, NEG).astype(np.float32)
    first = np.concatenate([rot, low, high, cos, sin, before, after], 1)

    anti = eye[:, ::-1].copy()
    s, t = q, k
    strict, upto = (s < t).astype(np.float32), (s <= t).astype(np.float32)
    tri = np.concatenate([upto, strict], 1)
    mask = np.concatenate([strict, upto, strict, upto], 1)
    levels = []
    for e in range(7):
        b = 1 << e
        levels.append(((s // (2 * b) == t // (2 * b)) & (s // b % 2 == 0) & (t // b % 2 == 1)).astype(np.float32))
    second = np.concatenate([low, high, anti, tri, mask] + levels, 1)

    j = np.arange(384)
    dist = 255 - j
    inside = (dist >= 0) & (dist < 128)
    dd = np.clip(dist, 0, 127)
    large = 16 + (np.log(np.maximum(dd, 1).astype(np.float32) / np.float32(16)) / np.float32(np.log(128 / 16))
                  * np.float32(16)).astype(np.int32)
    bucket = np.where(dd < 16, dd, np.minimum(large, 31))
    hot = np.zeros((P, 384), np.float32)
    hot[bucket[inside], j[inside]] = 1.0
    hot[32, ~inside] = NEG
    return {"k_base": base.astype(np.float32), "k_first": first.astype(np.float32),
            "k_second": second.astype(np.float32), "k_hot": hot}


class Program:

    def __init__(self, nc, ctx, A):
        self.nc, self.A, self.ctx = nc, A, ctx
        base = -(-nc.sbuf_base // 64) * 64
        self.top = base

        def region(nbytes):
            at = self.top
            self.top += -(-nbytes // 64) * 64
            return at

        def at(name, offset, shape, dt=F32):
            return nc.alloc_sbuf_tensor_at(name, [P] + shape, dt, offset=offset)

        self.h = at("h", region(KD * TOK * 4), [KD, TOK])
        r_x = region(2 * KD * TOK * 4)
        self.x_hi = at("x_hi", r_x, [KD, TOK], F32R)
        self.x_lo = at("x_lo", r_x + KD * TOK * 4, [KD, TOK], F32R)
        r_g = region(2 * HALF * TOK * 4)
        self.r_x, self.r_g = r_x, r_g
        self.g_hi = at("g_hi", r_g, [HALF, TOK], F32R)
        self.g_lo = at("g_lo", r_g + HALF * TOK * 4, [HALF, TOK], F32R)
        w = HALF * P * 4
        self.raw = at("raw", region(2 * w), [2, HALF * P])
        self.w_hi = at("w_hi", region(2 * w), [2, HALF * P], F32R)
        self.w_lo = at("w_lo", region(2 * w), [2, HALF * P], F32R)
        self.prm = at("prm", region(PT * P * 4), [PT * P])
        self.kb = at("kb", region(3 * P * 4), [3 * P])
        self.mods = at("mods", region(96 * 2 * 4), [96, 2])
        self.scg = at("scg", region(64 * 4), [2, 2, 2, KD])
        self.b2g1 = at("b2g1", region(16 * 4), [2, KD])
        self.sc = at("sc", region(16 * 4), [2 * KD])
        self.sinks = at("sinks", region(24 * 4), [24])
        self.one = at("one", region(32), [8])
        self.sm_max = at("sm_max", region(64), [2])
        self.sm_neg = at("sm_neg", region(64), [2])
        self.sm_sum = at("sm_sum", region(64), [2])
        self.sm_sink = at("sm_sink", region(64), [2])
        self.sm_den = at("sm_den", region(64), [2])
        self.sm_rd = at("sm_rd", region(64), [2])
        self.nsinks = at("nsinks", region(24 * 4), [24])
        self.cend = at("cend", region(48 * 4), [4, 3, 4])
        self.gn = at("gn", region(6 * 6 * 4), [6, 6])
        self.mod_rows_at = region(4 * 256 * 4)
        self.mod_rows = at("mod_rows", self.mod_rows_at, [4 * 256])
        r_s = region(8 * TOK * 4)
        self.r_s = r_s
        assert self.top <= nc.sbuf_usable_end, (self.top, nc.sbuf_usable_end)

        ln = TOK * 4
        self.n_sq = at("n_sq", r_s, [2, TOK])
        self.n_t = at("n_t", r_s + 2 * ln, [2, TOK])
        self.n_y = at("n_y", r_s + 4 * ln, [2, TOK])
        self.f_a = at("f_a", r_s, [2, TOK])
        self.f_b = at("f_b", r_s + 2 * ln, [2, TOK])
        self.gate = at("gate", r_s + 6 * ln, [2, TOK])
        self.mod_t = at("mod_t", r_s + 6 * ln, [2, P])

        self.x_rows = at("x_rows", r_g, [6, D])
        self.p_rows = at("p_rows", r_g + 6 * D * 4, [PT, P])
        self.m_rows = at("m_rows", r_g, [2, D])
        self.vw = SEQ + CTX + 4 * PAD
        r_tail = r_g + KD * (self.vw + TOK) * 4
        ada_tail = at("ada_tail", r_tail, [2, KD, 256])
        assert r_tail + 2 * KD * 256 * 4 <= r_g + 2 * HALF * TOK * 4
        ada_x = at("ada_x", r_x, [6, KD, 256])
        ada_s = at("ada_s", r_s, [2, KD, 256])
        self.ada_first = [ada_x[:, i, :, :] for i in range(6)] + [ada_tail[:, i, :, :] for i in range(2)]
        self.ada_ring = [ada_tail[:, i, :, :] for i in range(2)] + [ada_s[:, i, :, :] for i in range(2)]
        self.vp = at("vp", r_g, [KD, self.vw])
        self.cv = at("cv", r_g + KD * self.vw * 4, [KD, TOK])
        o = r_g
        def nxt(name, shape, dt=F32):
            nonlocal o
            t = at(name, o, shape, dt)
            o += int(np.prod(shape)) * 4
            return t
        self.kf = nxt("kf", [3 * P + 2 * SEQ + 2 * P])
        self.q_ = nxt("q_", [8, SEQ])
        self.k_ = nxt("k_", [2, TOK])
        self.v_ = nxt("v_", [2, TOK])
        self.vt = nxt("vt", [6, 256])
        self.kd = nxt("kd", [4, TOK])
        assert o <= r_g + 2 * HALF * TOK * 4, o - r_g
        o = r_s
        self.p_sb = nxt("p_sb", [2, 640])
        self.pt_sb = nxt("pt_sb", [2, 640])
        self.o_t = nxt("o_t", [4, 256])
        self.o_t2 = nxt("o_t2", [4, 256])
        o -= 2 * 256 * 4
        self.qg = nxt("qg", [2, SEQ])
        self.kg = nxt("kg", [SEQ])
        assert o <= r_s + 8 * ln
        o = r_g + 2 * 640 * 4
        self.pj = nxt("pj", [17, SEQ])
        r_mkv = o
        self.mkv = nxt("mkv", [4, CTX])
        self.ks = nxt("ks", [3 * P + 2 * P + 4 * P + 7 * P])
        r_b = o
        self.bias = nxt("bias", [6, 2 * P])
        self.lw = nxt("lw", [384])
        self.w0b = nxt("w0b", [384])
        r_av = o
        self.av = nxt("av", [3, SEQ])
        assert o <= r_g + 2 * HALF * TOK * 4, o - r_g
        o = r_av
        self.hot = nxt("hot", [384])
        self.rr = nxt("rr", [384])
        self.relb = nxt("relb", [8])
        self.tz = at("tz", r_s + 10240, [6, 2 * P])
        o = r_s
        self.sig = nxt("sig", [4, 384])
        self.ex = nxt("ex", [3, SEQ])
        self.dd = nxt("dd", [2, SEQ])
        self.hq = nxt("hq", [2, SEQ])
        o = r_s
        self.m4 = nxt("m4", [2, 6, 512])
        assert o <= r_s + 8 * ln
        behind = [at(f"behind{i}", r_x + i * KD * TOK * 4, [KD, TOK]) for i in (0, 1)]
        self.lv, self.mt = (behind[0][:, 0:6, SEQ + i * P:SEQ + (i + 1) * P] for i in (0, 1))
        self.inv_t = [behind[1][:, 0:6, SEQ + i * P:SEQ + (i + 1) * P] for i in (0, 1)]
        o = r_b
        self.tok = nxt("tok", [3, 384])
        self.y = nxt("y", [384])
        o = r_mkv
        self.x0 = nxt("x0", [384])
        self.u = nxt("u", [384])
        self.z = nxt("z", [3, HD])
        o = r_g
        self.inv = nxt("inv", [6, P])
        self.y1 = nxt("y1", [3, P])
        self.ysq = at("ysq", self.mod_rows_at, [384])
        self.at = at

        self.ps = ctx.enter_context(nc.psum_tensor("ps", [P, 4096], F32))

    def sem(self, name, counting=True):
        return self.ctx.enter_context(self.nc.semaphore(name))

    def pair(self, n, lo=0, hi=TOK):
        return self.ps[:, n * 1024 + lo:n * 1024 + hi]

    def col(self, name, r=0):
        c = COL[name] + r
        return self.prm[:, c:c + 1]

    def col_at(self, name, r):
        return self.prm[:, bass.ds(r + COL[name], 1)]


def chunks(eng, n):
    full = (n - 2) // 4
    if full >= 2:
        with eng.Fori(0, full) as it:
            for u in range(4):
                yield it, u
    else:
        full = 0
    for i in range(4 * full, n):
        yield i // 4, i % 4


def build(nc, A, out, stop=None):
    with ExitStack() as ctx:
        build_in(nc, ctx, A, out, stop)


def build_in(nc, ctx, A, out, stop):
    M = Program(nc, ctx, A)
    sem = M.sem
    ident, ones, head1 = M.kb[:, 0:P], M.kb[:, P:2 * P], M.kb[:, 2 * P:3 * P]

    s_cst = sem("s_cst", False)
    s_rows = sem("s_rows", False)
    s_raw = [sem(f"s_raw{i}", False) for i in range(2)]
    s_ada = [sem(f"s_ada{i}", False) for i in range(ADA_FIRST)]
    s_mod = sem("s_mod", False)
    s_modt = sem("s_modt", False)
    s_ring = [sem(f"s_ring{i}", False) for i in range(4)]
    s_kf = sem("s_kf", False)
    s_mem = sem("s_mem", False)
    s_out = sem("s_out", False)
    hi_ready = sem("hi_ready")
    lo_ready = sem("lo_ready")
    tile_done = sem("tile_done")
    evac = sem("evac")
    ada_used = sem("ada_used")
    start_t = sem("start_t")
    start_c = sem("start_c")
    zero_ready = sem("zero_ready")
    sc_ready = sem("sc_ready")
    mod_rows = sem("mod_rows")
    mod_t = sem("mod_t")
    mod_ready = sem("mod_ready")
    sq_ready = sem("sq_ready")
    sq_used = sem("sq_used")
    stat_ready = sem("stat_ready")
    rms_ready = sem("rms_ready")
    rstd_ready = sem("rstd_ready")
    t_ready = sem("t_ready")
    y_ready = sem("y_ready")
    x_ready = sem("x_ready")
    h_ready = sem("h_ready")
    gate_ready = sem("gate_ready")
    v_ready = sem("v_ready")
    tap_done = sem("tap_done")
    cv_ready = sem("cv_ready")
    cv_cent = sem("cv_cent")
    mu_ready = sem("mu_ready")
    mid_ready = sem("mid_ready")
    taps_ready = sem("taps_ready")
    silu_ready = sem("silu_ready")
    prod_ready = sem("prod_ready")
    ghi_ready = sem("ghi_ready")
    g_ready = sem("g_ready")
    f_res = sem("f_res")

    rope_r = sem("rope_r")
    rope_c = sem("rope_c")
    turn_t = sem("turn_t")
    turn_c = sem("turn_c")
    att_s = sem("att_s")
    att_m = sem("att_m")
    att_p = sem("att_p")
    att_r = sem("att_r")
    att_t = sem("att_t")
    att_c = sem("att_c")
    att_o = sem("att_o")
    att_e = sem("att_e")
    otr_t = sem("otr_t")
    otr_h = sem("otr_h")
    xa_ready = sem("xa_ready")

    H_STAGE = ["start", "pw2", "down00", "down01", "wo", "down10", "down11", "final", "w_out",
               "down20", "down21"]
    H = {s: 8 * (i + 1) for i, s in enumerate(H_STAGE)}

    order = ["start", "ada", "n10", "pw1", "ln", "pw2", "n20", "ffn0", "n11", "qkv", "attn", "wo",
             "n21", "ffn1", "final", "mix", "w_in", "mixers", "w_out", "ffn2_norm", "ffn2"]
    if stop:
        order = order[:order.index(stop) + 1]
    streams_of = {"pw1": ["pw1"], "pw2": ["pw2"], "qkv": ["qkv"], "wo": ["wo"],
                  "w_in": ["w_in", "mem_kv"], "w_out": ["w_out"]}
    for b in range(3):
        streams_of[f"ffn{b}"] = [f"{d}{b}{hf}" for hf in (0, 1) for d in ("up", "down")]
    used_streams = [s for st in order for s in streams_of.get(st, [])]
    q_end = sum(N_CHUNKS[s] for s in used_streams)

    def rows(ap, kt):
        return ap.rearrange("(kt p) c -> p kt c", p=P)

    w_src = {"pw1": rows(A["conv_w_pw1"][0], 8), "pw2": rows(A["conv_w_pw2"][0], 8),
             "qkv": rows(A["attn_w_qkv"][0], 8), "wo": rows(A["attn_w_o"][0], 8),
             "w_in": rows(A["w_in_2"][0], 8), "mem_kv": rows(A["w_mem_kv_2"][0], 8),
             "w_out": rows(A["w_out_2"][0], 8)}
    for b in range(3):
        up = A["w_up_2"][0] if b == 2 else A["ffn_w_up"][b]
        down = A["w_down_2"][0] if b == 2 else A["ffn_w_down"][b]
        for hf in (0, 1):
            w_src[f"up{b}{hf}"] = rows(up, 8)
            w_src[f"down{b}{hf}"] = rows(down[hf * HALF * P:(hf + 1) * HALF * P, :], HALF)

    def column(name, it, u):
        if name == "pw1":
            return it * 256 + ((u % 2) * 8 + u // 2) * P
        if name.startswith("up"):
            return it * 256 + ((u % 2) * FT + int(name[3]) * HALF + u // 2) * P
        return it * 512 + u * P

    def load_stream(sp, name):
        K, q0 = ROWS_OF[name], Q0[name]
        n, full = N_CHUNKS[name], N_CHUNKS[name] // 4
        def one(it, u):
            slot = (q0 + u) % 2
            c = column(name, it, u)
            if not isinstance(c, int):
                c = sp.snap(c)
            sp.wait_ge(lo_ready, done(q0 + 4 * it + u - 1))
            sp.dma_start(M.raw[:, slot, 0:K * P].rearrange("p (k c) -> p k c", c=P),
                         w_src[name][:, :, bass.ds(c, P)]).then_inc(s_raw[slot], 16)
        if full >= 2 and name != "qkv":
            with sp.Fori(0, full) as it:
                for u in range(4):
                    one(it, u)
        else:
            full = 0
        for i in range(4 * full, n):
            if name == "qkv" and i == 2:
                sp.wait_ge(tile_done, done(Q0["qkv"]))
                sp.dma_start(M.kf[:, :], A["k_first"]).then_inc(s_kf, 16)
            one(i // 4, i % 4)

    def raw_count(q0, it, u):
        return 16 * (2 * it + (q0 + u) // 2 + 1)

    def low_stream(pool, name, first=0, last=None):
        K, q0 = ROWS_OF[name], Q0[name]
        n, full = N_CHUNKS[name], N_CHUNKS[name] // 4
        def one(it, u):
            slot = (q0 + u) % 2
            pool.wait_ge(hi_ready, done(q0 + 4 * it + u + 1))
            pool.tensor_tensor(M.w_lo[:, slot, 0:K * P], M.raw[:, slot, 0:K * P],
                               M.w_hi[:, slot, 0:K * P].bitcast(F32), ALU.subtract).then_inc(lo_ready, 1)
        if last is not None:
            for i in range(first, last):
                one(i // 4, i % 4)
            return
        if full >= 2:
            with pool.Fori(0, full) as it:
                for u in range(4):
                    one(it, u)
        else:
            full = 0
        for i in range(4 * full, n):
            one(i // 4, i % 4)

    def high(act, name, it, u):
        q0 = Q0[name]
        if isinstance(it, int):
            q = q0 + 4 * it + u + 2
            if q >= q_end:
                return
            K = ROWS_AT[q]
        else:
            K = ROWS_OF[name]
        slot = (q0 + u) % 2
        act.wait_ge(s_raw[slot], raw_count(q0, it, u + 2))
        act.wait_ge(tile_done, done(q0 + 4 * it + u + 1))
        act.activation(M.w_hi[:, slot, 0:K * P], M.raw[:, slot, 0:K * P], ACT.Copy).then_inc(hi_ready, 1)

    def high_first(act):
        for q in range(min(2, q_end)):
            act.wait_ge(s_raw[q], 16)
            act.activation(M.w_hi[:, q, 0:ROWS_AT[q] * P], M.raw[:, q, 0:ROWS_AT[q] * P], ACT.Copy)\
                .then_inc(hi_ready, 1)

    LAT, BOTH, MEM = [(0, SEQ)], [(0, SEQ), (SEQ, CTX)], [(SEQ, CTX)]

    PW1_PAIR = (0, 2, 1, 2)

    def tile_products(pe, name, u, t0, tn, k, from_g):
        K, q0 = ROWS_OF[name], Q0[name]
        slot, pair = (q0 + u) % 2, PW1_PAIR[u] if name == "pw1" else (q0 + u) % 4
        hi, lo = (M.g_hi, M.g_lo) if from_g else (M.x_hi, M.x_lo)
        wh = M.w_hi[:, slot, k * P:(k + 1) * P]
        wl = M.w_lo[:, slot, k * P:(k + 1) * P]
        o = M.pair(pair, t0, t0 + tn)
        pe.matmul(o, wh, hi[:, k, t0:t0 + tn], start=(k == 0), stop=False)
        pe.matmul(o, wh, lo[:, k, t0:t0 + tn], start=False, stop=False)
        return pe.matmul(o, wl, hi[:, k, t0:t0 + tn], start=False, stop=(k == K - 1))

    def chunk_start(pe, name, it, u):
        q0 = Q0[name]
        pe.wait_ge(lo_ready, done(q0 + 4 * it + u + 1))
        pe.wait_ge(evac, done(q0 + 4 * it + u - 3))
        if name == "pw1" and u % 2:
            pe.wait_ge(gate_ready, done(2 * it + u // 2))

    def products(pe, name, it, u, segs, from_g=0):
        chunk_start(pe, name, it, u)
        for n, (t0, tn) in enumerate(segs):
            for k in range(ROWS_OF[name]):
                if from_g and n == 0 and u == 0 and isinstance(it, int) and it == 0:
                    pe.wait_ge(g_ready, done(from_g - HALF + k + 1))
                mm = tile_products(pe, name, u, t0, tn, k, from_g)
        mm.then_inc(tile_done, 1)

    LAG = 3

    def first_two(pe, name, segs, norm):
        for step in range(KD + LAG):
            for u, k in ((0, step), (1, step - LAG)):
                if not 0 <= k < KD:
                    continue
                if k == 0:
                    chunk_start(pe, name, 0, u)
                if u == 0:
                    pe.wait_ge(x_ready, done(8 * NN[norm] + k + 1))
                for t0, tn in segs:
                    mm = tile_products(pe, name, u, t0, tn, k, 0)
                if k == KD - 1:
                    mm.then_inc(tile_done, 1)

    def peeled_chunks(eng, n):
        full = (n - 2) // 4
        for u in range(4):
            yield 0, u
        if full >= 3:
            with eng.Fori(1, full) as it:
                for u in range(4):
                    yield it, u
        else:
            full = 1
        for i in range(4 * full, n):
            yield i // 4, i % 4

    def stream_pe(pe, name, segs_of, from_g=0, norm=None):
        if norm:
            first_two(pe, name, segs_of(0, 0), norm)
        for it, u in peeled_chunks(pe, N_CHUNKS[name]) if norm else chunks(pe, N_CHUNKS[name]):
            if norm and isinstance(it, int) and it == 0 and u < 2:
                continue
            products(pe, name, it, u, segs_of(it, u), from_g)


    def start_sp(sp):
        sp.dma_start(M.kb[:, :], A["k_base"]).then_inc(s_cst, 16)
        sp.wait_ge(zero_ready, done(1))
        for name, r in PARAM_ROWS:
            src = A[name]
            if name.endswith("norm_2") and r == 1:
                c = COL[name]
                for half in (0, 1):
                    sp.dma_start(M.p_rows[c % P:c % P + 1, c // P, half * HD:(half + 1) * HD], src)\
                        .then_inc(s_cst, 16)
                continue
            dims = " ".join(f"d{i}" for i in range(len(src.shape)))
            flat = src.rearrange(f"{dims} -> ({dims})") if len(src.shape) > 1 else src
            flat = flat.rearrange("(r c) -> r c", c=P)
            r0 = 0
            while r0 < r:
                c = COL[name] + r0
                n = min(r - r0, P - c % P)
                sp.dma_start(M.p_rows[c % P:c % P + n, c // P, :], flat[r0:r0 + n, :]).then_inc(s_cst, 16)
                r0 += n
        sp.dma_start(M.sinks[:, 0:16], A["attn_sink"][0:1, :].to_broadcast([P, 16])).then_inc(s_cst, 16)
        sp.dma_start(M.sinks[:, 16:22], A["attn_sinks_2"][0:1, :].to_broadcast([P, 6])).then_inc(s_cst, 16)
        sp.dma_start(M.x_rows[:, 0:4, :], A["x"][0].rearrange("(t p) d -> p t d", p=P)).then_inc(s_rows, 16)
        sp.dma_start(M.x_rows[:, 4:6, :], A["ctx"][0].rearrange("(t p) d -> p t d", p=P)).then_inc(s_rows, 16)

    cond = M.sc[:, :].rearrange("p (s k) -> p k s", s=2)
    ada_src = A["ada_w"].rearrange("l (kt p) c -> p l kt c", p=P)

    def ada_first_load(act):
        for n in range(ADA_FIRST):
            act.dma_start(M.ada_first[n], ada_src[:, 0, :, n * 256:(n + 1) * 256]).then_inc(s_ada[n], 16)

    def ada_load(sp, it, n, layer, column):
        sp.wait_ge(ada_used, done(12 * it + (ADA_FIRST + n - 3)))
        sp.dma_start(M.ada_ring[n % 4], ada_src[:, layer, :, bass.ds(column, 256)]).then_inc(s_ring[n % 4], 16)

    def pw1_sp(sp):
        def w(it, u):
            q0 = Q0["pw1"]
            if 4 * it + u >= 2 if isinstance(it, int) else True:
                sp.wait_ge(lo_ready, done(q0 + 4 * it + u - 1))
            c = column("pw1", it, u)
            if not isinstance(c, int):
                c = sp.snap(c)
            sp.dma_start(M.raw[:, (q0 + u) % 2, 0:KD * P].rearrange("p (k c) -> p k c", c=P),
                         w_src["pw1"][:, :, bass.ds(c, P)]).then_inc(s_raw[(q0 + u) % 2], 16)

        def first(n):
            ada_load(sp, 0, n, 0, (ADA_FIRST + n) * 256)
        w(0, 0)
        w(0, 1)
        w(0, 2)
        sp.wait_ge(ada_used, done(ADA_FIRST))
        first(0)
        first(1)
        sp.wait_ge(x_ready, done(8))
        for n in range(2, 6):
            first(n)
        w(0, 3)
        for n in range(6, 12):
            first(n)
        with sp.Fori(0, 2) as it:
            for u in range(4):
                w(it + 1, u)
                for n in range(3 * u - 3, 3 * u + 3) if u % 2 else ():
                    ada_load(sp, it + 1, n, 1, sp.snap(it * (12 * 256) + n * 256))
        w(3, 0)
        w(3, 1)
        for n in range(4):
            ada_load(sp, 3, n, 0, (ADA_FIRST + 12 + n) * 256)
        for u in (2, 3):
            w(3, u)

    def start_pe(pe):
        pe.wait_ge(s_cst, 16 * M.n_param_dma)
        for t in range(PT):
            bank = t // 4
            mm = pe.transpose(M.ps[:, bank * 512 + (t % 4) * P:bank * 512 + (t % 4 + 1) * P],
                              M.p_rows[:, t, :], ident)
            if t % 4 == 3 or t == PT - 1:
                mm.then_inc(start_t, 1)
        pe.wait_ge(s_rows, 32)
        for k in range(KD):
            pair = (k + 2) % 3
            if k >= 1:
                pe.wait_ge(start_c, done(k + 1))
            for t in range(6):
                mm = pe.transpose(M.pair(pair, t * P, (t + 1) * P), M.x_rows[:, t, k * P:(k + 1) * P], ident)
            mm.then_inc(start_t, 1)

    def start_act(act):
        act.wait_ge(start_t, done(1))
        act.activation(M.prm[:, 0:512], M.ps[:, 0:512], ACT.Copy).then_inc(start_c, 1)
        act.wait_ge(start_t, done(2))
        act.activation(M.prm[:, 512:1024], M.ps[:, 512:1024], ACT.Copy).then_inc(start_c, 1)
        act.wait_ge(start_t, done(3))
        act.activation(M.prm[:, 1024:PT * P], M.ps[:, 1024:PT * P], ACT.Copy).then_inc(start_c, 1)
        act.wait_ge(start_c, done(3))
        act.activation(M.sc[:, :], M.prm[:, COL["c"]:COL["c"] + 16], ACT.Silu).then_inc(sc_ready, 1)
        for k in range(KD):
            act.wait_ge(start_t, done(4 + k))
            act.activation(M.h[:, k, :], M.pair((k + 2) % 3), ACT.Copy).then_inc(start_c, 1)

    mod_dram = nc.dram_tensor("mod_scratch", (2, 2 * 6 * D), F32, kind="Internal").ap()
    MOD_GROUPS = 2 + 10

    def ada_products(pe, weights, n):
        c = n // 4
        for k in range(KD):
            mm = pe.matmul(M.ps[32 * c:32 * c + 2, 3 * 1024 + (n % 4) * 256:3 * 1024 + (n % 4 + 1) * 256],
                           cond[:, k, :], weights[:, k, :], start=(k == 0), stop=(k == KD - 1),
                           tile_position=(0, 32 * c))
        mm.then_inc(ada_used, 1)

    def ada_pe(pe):
        pe.wait_ge(sc_ready, done(1))
        for n in range(ADA_FIRST):
            pe.wait_ge(s_ada[n], 16)
            ada_products(pe, M.ada_first[n], n)
        turn_mods_pe(pe, 0)

    def turn_mods_pe(pe, second):
        n = 96 if second else 16
        pe.wait_ge(mod_rows, done(MOD_GROUPS if second else 2))
        pe.wait_ge(s_modt, 32 if not second else 64)
        for s in (0, 1):
            mm = pe.transpose(M.pair(3, s * n, (s + 1) * n), M.mod_t[0:n, s, :], ident[0:n, 0:n])
        mm.then_inc(mod_t, 1)

    def group_act(act, g, layer, column):
        c = g if g < 2 else (g - 2) % 3
        act.wait_ge(ada_used, done(4 * g + 4))
        if g >= 2:
            act.wait_ge(s_mod, 16 * g)
        r = slice(32 * c, 32 * c + 2)
        act.activation(M.mod_rows[r, :], M.ps[r, 3 * 1024:4 * 1024], ACT.Copy).then_inc(mod_rows, 1)
        act.wait_ge(mod_rows, done(g + 1))
        at = layer * 6 * D + column
        act.dma_start(mod_dram[:, at:at + 1024], M.mod_rows[r, :]).then_inc(s_mod, 16)

    def mods_back_act(act, second):
        n = 96 if second else 16
        act.wait_ge(s_mod, 16 * (MOD_GROUPS if second else 2))
        if second:
            act.wait_ge(v_ready, done(7))
        for s in (0, 1):
            act.dma_start(M.mod_t[0:n, s, :], mod_dram[s:s + 1, 0:n * P].rearrange("o (m p) -> (o m) p", p=P))\
                .then_inc(s_modt, 16)

    def pw1_pe(pe):
        first_two(pe, "pw1", BOTH, "n10")
        for it, u in peeled_chunks(pe, 16):
            peeled = isinstance(it, int)
            if not (peeled and 4 * it + u < 2):
                products(pe, "pw1", it, u, BOTH)
            if u % 2 == 0:
                continue
            for n in range(3 * u - 3, 3 * u + 3) if not peeled or it < 3 else range(4 if u == 1 else 0):
                if n % 4 == 0:
                    pe.wait_ge(mod_rows, done(3 * it + n // 4))
                pe.wait_ge(s_ring[n % 4], 16 * (3 * it + n // 4 + 1))
                ada_products(pe, M.ada_ring[n % 4], n)
        turn_mods_pe(pe, 1)

    def add_mods(dve, lo, hi, n):
        for s in (0, 1):
            dve.tensor_tensor(M.mods[:, lo:hi, s], M.pair(3, s * n + lo, s * n + hi),
                              M.prm[:, COL["ada_b"] + lo:COL["ada_b"] + hi], ALU.add)

    def norm_gains(dve, l, w):
        m0 = 48 * l + 8 * (1 + 3 * w)
        for s in (0, 1):
            c = COL[("norm1_g", "norm2_g")[w]] + 8 * l
            dve.scalar_tensor_tensor(out=M.scg[:, l, w, s, :], in0=M.mods[:, m0:m0 + 8, s], scalar=1.0,
                                     in1=M.prm[:, c:c + 8], op0=ALU.add, op1=ALU.mult)

    def ada_dve(dve):
        dve.wait_ge(mod_t, done(1))
        dve.wait_ge(start_c, done(3))
        add_mods(dve, 0, 16, 16)
        dve.tensor_scalar(M.nsinks[:, 0:22], M.sinks[:, 0:22], -1.0, None, ALU.mult)
        dve.drain()
        norm_gains(dve, 0, 0)
        dve.drain().then_inc(mod_ready, 1)

    def ada_rest_dve(dve):
        dve.wait_ge(mod_t, done(2))
        add_mods(dve, 16, 96, 96)
        dve.drain()
        for l, w in ((0, 1), (1, 0), (1, 1)):
            norm_gains(dve, l, w)
        for s in (0, 1):
            c = COL["conv_b_pw2"]
            dve.tensor_tensor(M.b2g1[:, s, :], M.mods[:, 16:24, s], M.prm[:, c:c + 8], ALU.mult)
        dve.drain().then_inc(mod_ready, 1)


    def scale_of(name, k, s):
        if name in ("n10", "n20", "n11", "n21"):
            l, w = int(name[2]), int(name[1]) - 1
            return M.scg[:, l, w, s, k:k + 1], M.mods[:, 48 * l + 24 * w + k, s:s + 1]
        if name == "ln":
            return M.col("conv_ln_g", k), M.col("conv_ln_b", k)
        if name == "final":
            return M.col("final_g", k), 0.0
        if name == "mix":
            return M.col("mem_norm_g_2" if s else "mix_norm_g_2", k), 0.0
        return M.col("ffn_norm_g_2", k), 0.0

    NORM_W = {"n10": TOK, "ln": TOK, "n20": TOK, "n11": TOK, "n21": SEQ, "final": SEQ, "mix": TOK,
              "ffn2_norm": SEQ}
    NORM_Q = {"n10": 0, "ln": Q0["pw2"], "n20": Q0["up00"], "n11": Q0["qkv"], "n21": Q0["up10"],
              "final": Q0["w_in"], "mix": Q0["w_in"], "ffn2_norm": Q0["up20"]}
    NORM_H = {"n10": "start", "n20": "pw2", "n11": "down01", "n21": "wo", "final": "down11",
              "mix": "final", "ffn2_norm": "w_out"}

    def norm_segs(name):
        w = NORM_W[name]
        if name == "ln":
            return [(0, 0, w)]
        return [(0, 0, SEQ)] + ([(1, SEQ, TOK)] if w == TOK else [])

    def norm_source(eng, name, k):
        if name == "ln":
            eng.wait_ge(cv_cent, done(k + 1))
            return M.cv[:, k, 0:TOK]
        if name == "n10":
            eng.wait_ge(start_c, done(3 + k + 1))
        else:
            eng.wait_ge(h_ready, done(H[NORM_H[name]] - 8 + k + 1))
            if name == "mix":
                eng.wait_ge(mem_ready, done(k + 1))
        return M.h[:, k, 0:NORM_W[name]]

    mem_ready = sem("mem_ready")
    mem_t = sem("mem_t")

    def norm_pair(name):
        return 1 if name == "n10" else (NORM_Q[name] + 2) % 4

    def norm_pe(pe, name):
        i, pair, w = NN[name], norm_pair(name), NORM_W[name]
        if name == "mix":
            pe.wait_ge(mem_ready, done(KD))
        pe.wait_ge(evac, done(NORM_Q[name]))
        pe.wait_ge(sq_used, done(7 * i + 7))
        for t0, tn in (BOTH if w == TOK else LAT):
            mm = pe.matmul(M.pair(pair, t0, t0 + tn), ones, M.n_t[:, 0, t0:t0 + tn], start=True, stop=True)
        mm.then_inc(stat_ready, 1)

    EARLY = {"pw2": "n20", "down01": "n11", "wo": "n21", "down11": "final", "w_out": "ffn2_norm"}

    def square_act(act, name, k):
        i, w = NN[name], NORM_W[name]
        src = norm_source(act, name, k)
        if k == 0:
            act.wait_ge(x_ready, done(8 * i))
            if name in ("n11", "final"):
                act.wait_ge(g_ready, done(HALF * (2 if name == "n11" else 4)))
            if name == "n21":
                act.wait_ge(xa_ready, done(8))
            if name == "ffn2_norm":
                V_S.after(act, "lo3")
        if k >= 3:
            act.wait_ge(sq_used, done(7 * i + k - 2))
        dst = M.n_sq[:, k % 2, 0:w] if k else M.n_t[:, 0, 0:w]
        act.activation(dst, src, ACT.Square).then_inc(sq_ready, 1)

    def add_square_dve(dve, name, k):
        if k == 0:
            return
        i, w = NN[name], NORM_W[name]
        dve.wait_ge(sq_ready, done(8 * i + k + 1))
        if k > 1:
            dve.wait_ge(sq_used, done(7 * i + k - 1))
        dve.tensor_tensor(M.n_t[:, 0, 0:w], M.n_sq[:, k % 2, 0:w], M.n_t[:, 0, 0:w], ALU.add).then_inc(sq_used, 1)

    def early_act(act, stream, m):
        if stream in EARLY and m:
            square_act(act, EARLY[stream], m - 1)

    def early_dve(dve, stream, m):
        if stream in EARLY and m:
            add_square_dve(dve, EARLY[stream], m - 1)

    def norm_act(act, name):
        i, pair, w = NN[name], norm_pair(name), NORM_W[name]
        if name not in EARLY.values():
            for k in range(KD):
                square_act(act, name, k)
        act.wait_ge(stat_ready, done(i + 1))
        act.activation(M.n_y[:, 0, 0:w], M.pair(pair, 0, w), ACT.Sqrt, scale=1.0 / D, bias=eps_col)\
            .then_inc(rms_ready, 1)
        if name == "n10":
            for g in (0, 1):
                group_act(act, g, 0, g * 1024)
            mods_back_act(act, 0)
            act.wait_ge(mod_ready, done(1))
        for k in range(KD):
            act.wait_ge(t_ready, done(8 * i + k + 1))
            if k >= 2:
                act.wait_ge(x_ready, done(8 * i + k - 1))
            else:
                act.wait_ge(rstd_ready, done(i + 1))
            fn = ACT.Silu if name == "ln" else ACT.Identity
            dst = M.h[:, k, :] if name == "final" else M.n_y[:, k % 2, :]
            for s, t0, t1 in norm_segs(name):
                scale, shift = scale_of(name, k, s)
                ins = act.activation(dst[:, t0:t1], M.n_t[:, k % 2, t0:t1], fn, scale=scale, bias=shift)
            if name == "final":
                ins.then_inc(y_ready, 1)
                continue
            act.drain()
            act.activation(M.x_hi[:, k, 0:w], M.n_y[:, k % 2, 0:w], ACT.Copy).then_inc(y_ready, 1)

    def norm_dve(dve, name):
        i, pair, w = NN[name], norm_pair(name), NORM_W[name]
        if name not in EARLY.values():
            for k in range(KD):
                add_square_dve(dve, name, k)
        dve.wait_ge(rms_ready, done(i + 1))
        dve.reciprocal(M.pair(pair, 0, w), M.n_y[:, 0, 0:w]).then_inc(rstd_ready, 1)
        dve.wait_ge(rstd_ready, done(i + 1))
        if name == "n10":
            ada_dve(dve)

        def low(k):
            dve.wait_ge(y_ready, done(8 * i + k + 1))
            if name == "final":
                dve.drain().then_inc(x_ready, 1)
                dve.drain().then_inc(h_ready, 1)
                return
            dve.tensor_tensor(M.x_lo[:, k, 0:w], M.n_y[:, k % 2, 0:w], M.x_hi[:, k, 0:w].bitcast(F32),
                              ALU.subtract).then_inc(x_ready, 1)
        for k in range(KD):
            src = norm_source(dve, name, k)
            dve.tensor_tensor(M.n_t[:, k % 2, 0:w], M.pair(pair, 0, w), src, ALU.mult).then_inc(t_ready, 1)
            if k:
                low(k - 1)
        low(KD - 1)

    def prime(eng, sems):
        for s_ in sems:
            eng.drain().then_inc(s_, LEAD)

    def count_param_dmas():
        n = 1 + 2
        for name, r in PARAM_ROWS:
            if name.endswith("norm_2") and r == 1:
                n += 2
                continue
            c = COL[name]
            n += (c + r - 1) // P - c // P + 1
        return n

    rows_out = M.at("rows_out", M.r_g, [4, D])
    out_t = sem("out_t")
    out_c = sem("out_c")
    h_count = {"start": "start", "ada": "start", "n10": "start", "pw1": "start", "ln": "start", "pw2": "pw2",
               "n20": "pw2", "ffn0": "down01", "n11": "down01", "qkv": "down01", "attn": "down01", "wo": "wo",
               "n21": "wo", "ffn1": "down11", "final": "final", "mix": "final", "w_in": "final",
               "mixers": "final", "w_out": "w_out", "ffn2_norm": "w_out", "ffn2": "down21"}

    def finish_pe(pe):
        pe.wait_ge(h_ready, done(H[h_count[order[-1]]]))
        pe.wait_ge(evac, done(q_end))
        pe.wait_ge(x_ready, done(8 * sum(st in NN for st in order)))
        for t in range(SEQ // P):
            for k in range(KD):
                mm = pe.transpose(M.pair(t, k * P, (k + 1) * P), M.h[:, k, t * P:(t + 1) * P], ident)
            mm.then_inc(out_t, 1)

    def finish_dve(dve):
        for t in range(SEQ // P):
            dve.wait_ge(out_t, done(t + 1))
            dve.tensor_copy(M.rows_out_t[:, t, :], M.pair(t, 0, D)).then_inc(out_c, 1)

    def finish_sp(sp):
        for t in range(SEQ // P):
            sp.wait_ge(out_c, done(t + 1))
            sp.dma_start(out[0, t * P:(t + 1) * P, :], M.rows_out_t[:, t, :]).then_inc(s_out, 16)
        sp.wait_ge(s_out, 16 * (SEQ // P))

    M.rows_out_t = rows_out
    eps_col = M.one[:, 0:1]
    gn_eps_col = M.one[:, 1:2]
    zero_col = M.one[:, 2:3]

    VLAT, VCTX = PAD, SEQ + 3 * PAD

    def pw1_dve(dve):
        q0 = Q0["pw1"]
        cw = COL["conv_w_dw"]
        for j in range(8):
            pair = j % 2
            dve.wait_ge(tile_done, done(q0 + 2 * j + 2))
            dve.wait_ge(gate_ready, done(j + 1))
            dve.wait_ge(zero_ready, done(2))
            for t0, t1, at in ((0, SEQ, VLAT), (SEQ, TOK, VCTX)):
                ins = dve.scalar_tensor_tensor(out=M.vp[:, j, at:at + t1 - t0], in0=M.pair(pair, t0, t1),
                                               scalar=M.col("conv_b_pw1", j), in1=M.gate[:, j % 2, t0:t1],
                                               op0=ALU.add, op1=ALU.mult)
            ins.then_inc(v_ready, 1)
            dve.wait_ge(v_ready, done(j + 1))
            for tap in range(TAPS):
                for n, (t0, t1, at) in enumerate(((0, SEQ, VLAT), (SEQ, TOK, VCTX))):
                    src = M.vp[:, j, at - PAD + tap:at - PAD + tap + t1 - t0]
                    w = M.prm[:, cw + tap * 8 + j:cw + tap * 8 + j + 1]
                    o = M.pair(pair, t0, t1)
                    step = 2 * (TAPS * j + tap) + n
                    if tap == 0:
                        ins = dve.tensor_scalar(o, src, w, M.col("conv_b_dw", j), ALU.mult, ALU.add)
                    else:
                        dve.wait_ge(tap_done, done(step - 1))
                        ins = dve.scalar_tensor_tensor(out=o, in0=src, scalar=w, in1=o, op0=ALU.mult, op1=ALU.add)
                    ins.then_inc(tap_done, 1)

    def pw1_act(act):
        for i in range(16):
            it, u = i // 4, i % 4
            high(act, "pw1", it, u)
            for g in range(10):
                if group_step(g) == i:
                    layer, column = ((0, 2048 + g * 1024) if g < 3 else (1, (g - 3) * 1024) if g < 9 else (0, 5 * D))
                    group_act(act, g + 2, layer, column)
            if u % 2 == 0:
                continue
            j, slot, pair_g = i // 2, (i // 2) % 2, PW1_PAIR[u]
            act.wait_ge(tile_done, done(Q0["pw1"] + i + 1))
            if j >= 2:
                act.wait_ge(v_ready, done(j - 1))
            act.activation(M.gate[:, slot, :], M.pair(pair_g), ACT.Sigmoid,
                           bias=M.col("conv_b_pw1", j + 8)).then_inc(gate_ready, 1)
            if j:
                copy_conv(act, j - 1)
        mods_back_act(act, 1)
        copy_conv(act, 7)

    def group_step(g):
        it, c = g // 3, g % 3
        return 4 * it + (2, 4, 5)[c]

    def copy_conv(act, j):
        pair = j % 2
        act.wait_ge(tap_done, done(2 * TAPS * (j + 1)))
        act.activation(M.cv[:, j, :], M.pair(pair), ACT.Copy).then_inc(cv_ready, 1)
        act.wait_ge(cv_ready, done(j + 1))
        act.drain().then_inc(evac, 2)

    def mean_pe(pe):
        pair = Q0["pw2"] % 4
        pe.wait_ge(evac, done(Q0["pw2"]))
        for k in range(KD):
            pe.wait_ge(cv_ready, done(k + 1))
            for t0, tn in BOTH:
                mm = pe.matmul(M.pair(pair, t0, t0 + tn), ones, M.cv[:, k, t0:t0 + tn],
                               start=(k == 0), stop=(k == KD - 1))
        mm.then_inc(mu_ready, 1)

    def mean_dve(dve):
        pair = Q0["pw2"] % 4
        dve.wait_ge(mu_ready, done(1))
        for k in range(KD):
            dve.scalar_tensor_tensor(out=M.cv[:, k, :], in0=M.pair(pair), scalar=-1.0 / D, in1=M.cv[:, k, :],
                                     op0=ALU.mult, op1=ALU.add).then_inc(cv_cent, 1)

    def pw2_act(act):
        q0 = Q0["pw2"]
        for m in range(8):
            high(act, "pw2", m // 4, m % 4)
            act.wait_ge(tile_done, done(q0 + m + 1))
            for s, (t0, tn) in enumerate(BOTH):
                o = M.pair((q0 + m) % 4, t0, t0 + tn)
                ins = act.activation(o, o, ACT.Identity, scale=M.mods[:, 16 + m, s:s + 1],
                                     bias=M.b2g1[:, s, m:m + 1])
            ins.then_inc(f_res, 1)
            early_act(act, "pw2", m)
        early_act(act, "pw2", 8)

    def pw2_dve(dve):
        q0 = Q0["pw2"]
        for m in range(8):
            dve.wait_ge(f_res, done(m + 1))
            dve.tensor_tensor(M.h[:, m, :], M.pair((q0 + m) % 4), M.h[:, m, :], ALU.add).then_inc(evac, 1)
            dve.drain().then_inc(h_ready, 1)
            early_dve(dve, "pw2", m)
        early_dve(dve, "pw2", 8)

    def ffn_cols(b, tap, t, hf, j):
        r = t * FT + HALF * hf
        if b == 2:
            return M.col_at("conv_b_2" if tap is None else "conv_w_2", j + ((tap or 0) * 2 * FT + r))
        if tap is None:
            return M.col_at("ffn_b_dw", j + (b * 2 * FT + r))
        return M.col_at("ffn_w_dw", j + ((b * 3 + tap) * 2 * FT + r))

    SHIFTS = {0: (-1, 0, 1), 1: (-1, 0, 1), 2: (-2, -1, 0)}

    def up_act(act, b, hf, w):
        name = f"up{b}{hf}"
        q0, g0 = Q0[name], HALF * (2 * b + hf)
        zero_tap = SHIFTS[b].index(0)
        for it, u in chunks(act, 2 * HALF):
            high(act, name, it, u)
            if u % 2 == 0:
                continue
            j, slot = 2 * it + u // 2, u // 2
            pa, pb = (q0 + u - 1) % 4, (q0 + u) % 4
            g = 2 * it + (g0 + u // 2)
            act.wait_ge(tile_done, done(q0 + 4 * it + u + 1))
            for t, pr, dst in ((0, pa, M.f_a), (1, pb, M.f_b)):
                ins = act.activation(dst[:, slot, 0:w], M.pair(pr, 0, w), ACT.Identity,
                                     scale=ffn_cols(b, zero_tap, t, hf, j), bias=ffn_cols(b, None, t, hf, j))
            ins.then_inc(mid_ready, 1)
            act.wait_ge(taps_ready, done(g + 1))
            act.activation(M.pair(pa, 0, w), M.f_a[:, slot, 0:w], ACT.Silu).then_inc(silu_ready, 1)
            act.wait_ge(prod_ready, done(g + 1))
            act.activation(M.g_hi[:, bass.ds(j, 1), 0:w], M.pair(pb, 0, w), ACT.Copy).then_inc(ghi_ready, 1)

    def up_dve(dve, b, hf, w):
        name = f"up{b}{hf}"
        q0, g0 = Q0[name], HALF * (2 * b + hf)
        segs = [(0, SEQ)] + ([(SEQ, TOK)] if w == TOK else [])
        for it, u in chunks(dve, 2 * HALF):
            if u % 2 == 0:
                continue
            j, slot = 2 * it + u // 2, u // 2
            pa, pb = (q0 + u - 1) % 4, (q0 + u) % 4
            g = 2 * it + (g0 + u // 2)
            dve.wait_ge(mid_ready, done(g + 1))
            for n, tap in enumerate(t for t in range(3) if SHIFTS[b][t]):
                sh = SHIFTS[b][tap]
                if n:
                    dve.drain()
                for t, pr, dst in ((0, pa, M.f_a), (1, pb, M.f_b)):
                    for t0, t1 in segs:
                        o0, o1 = (t0 - sh, t1) if sh < 0 else (t0, t1 - sh)
                        ins = dve.scalar_tensor_tensor(
                            out=dst[:, slot, o0:o1], in0=M.pair(pr, o0 + sh, o1 + sh),
                            scalar=ffn_cols(b, tap, t, hf, j), in1=dst[:, slot, o0:o1],
                            op0=ALU.mult, op1=ALU.add)
            ins.then_inc(taps_ready, 1)
            dve.wait_ge(silu_ready, done(g + 1))
            dve.tensor_tensor(M.pair(pb, 0, w), M.pair(pa, 0, w), M.f_b[:, slot, 0:w], ALU.mult)\
                .then_inc(prod_ready, 1)
            dve.wait_ge(ghi_ready, done(g + 1))
            dve.tensor_tensor(M.g_lo[:, bass.ds(j, 1), 0:w], M.pair(pb, 0, w),
                              M.g_hi[:, bass.ds(j, 1), 0:w].bitcast(F32), ALU.subtract).then_inc(g_ready, 1)
            dve.drain().then_inc(evac, 2)

    def plain_high(act, name):
        for it, u in chunks(act, N_CHUNKS[name]):
            high(act, name, it, u)
            if name in EARLY:
                early_act(act, name, 4 * it + u)
        early_act(act, name, 8)

    def down_dve(dve, b, hf, w):
        name = f"down{b}{hf}"
        q0 = Q0[name]
        for m in range(8):
            dve.wait_ge(tile_done, done(q0 + m + 1))
            for s, (t0, tn) in enumerate(BOTH if w == TOK else LAT):
                o = M.h[:, m, t0:t0 + tn]
                src = M.pair((q0 + m) % 4, t0, t0 + tn)
                if b == 2:
                    dve.tensor_tensor(o, src, o, ALU.add)
                else:
                    dve.scalar_tensor_tensor(out=o, in0=src, scalar=M.mods[:, 48 * b + 40 + m, s:s + 1],
                                             in1=o, op0=ALU.mult, op1=ALU.add)
            dve.drain().then_inc(evac, 1)
            dve.drain().then_inc(h_ready, 1)
            early_dve(dve, name, m)
        early_dve(dve, name, 8)

    class Unit:

        def __init__(self, q, keys, sink, neg_sink, values, out):
            self.q, self.keys, self.sink, self.neg_sink, self.values, self.out = q, keys, sink, neg_sink, values, out
            self.nk = sum(n for _, n, _, _ in keys)

    SCALE = HD ** -0.5

    def att_pe(pe, units, n0, after=lambda eng, u: None):
        def scores(u):
            x = units[u]
            pe.wait_ge(att_p, done(n0 + max(u - 1, 0)))
            for off, n, rhs, masks in x.keys:
                mm = pe.matmul(M.pair(u % 2, off, off + n), x.q, rhs, start=True, stop=True)
                for at, width, mask in masks:
                    mm = pe.matmul(M.pair(u % 2, at, at + width), ident, mask, start=False, stop=True,
                                   skip_group_check=True)
            mm.then_inc(att_s, 1)

        def turn(u):
            x = units[u]
            pe.wait_ge(att_p, done(n0 + u + 1))
            pe.wait_ge(att_c, done(n0 + max(u - 1, 0)))
            pe.wait_ge(att_e, done(n0 + max(u - 1, 0)))
            for k in range(x.nk // P):
                mm = pe.transpose(M.pair(2 + u % 2, k * P, (k + 1) * P), M.p_sb[:, u % 2, k * P:(k + 1) * P], ident)
            mm.then_inc(att_t, 1)

        def values(u):
            x = units[u]
            pe.wait_ge(att_c, done(n0 + u + 1))
            for k, v in enumerate(x.values):
                mm = pe.matmul(M.pair(2 + u % 2, 640, 640 + HD), M.pt_sb[:, u % 2, k * P:(k + 1) * P], v,
                               start=(k == 0), stop=(k == len(x.values) - 1))
            mm.then_inc(att_o, 1)

        scores(0)
        for u in range(len(units)):
            if u + 1 < len(units):
                scores(u + 1)
            turn(u)
            if u:
                values(u - 1)
            after(pe, u)
        values(len(units) - 1)

    def att_dve(dve, units, n0, after=lambda eng, u: None):
        def negated(u):
            x, b = units[u], u % 2
            dve.wait_ge(att_s, done(n0 + u + 1))
            dve.wait_ge(att_p, done(n0 + max(u - 1, 0)))
            dve.tensor_reduce(M.sm_max[:, b:b + 1], M.pair(u % 2, 0, x.nk), AX.X, ALU.max)
            dve.drain()
            if x.sink is None:
                dve.tensor_scalar(M.sm_neg[:, b:b + 1], M.sm_max[:, b:b + 1], -SCALE, None, ALU.mult)\
                    .then_inc(att_m, 1)
            else:
                dve.tensor_scalar(M.sm_neg[:, b:b + 1], M.sm_max[:, b:b + 1], -SCALE, x.neg_sink, ALU.mult,
                                  ALU.min).then_inc(att_m, 1)

        def copied(u):
            x, b = units[u], u % 2
            dve.wait_ge(att_t, done(n0 + u + 1))
            dve.wait_ge(att_o, done(n0 + max(u - 1, 0)))
            dve.tensor_copy(M.pt_sb[:, b, 0:x.nk], M.pair(2 + u % 2, 0, x.nk)).then_inc(att_c, 1)

        def denominator(u):
            x, b = units[u], u % 2
            dve.wait_ge(att_p, done(n0 + u + 1))
            dve.wait_ge(att_e, done(n0 + max(u - 1, 0)))
            den = M.sm_sum
            if x.sink is not None:
                den = M.sm_den
                dve.tensor_tensor(den[:, b:b + 1], M.sm_sum[:, b:b + 1], M.sm_sink[:, b:b + 1], ALU.add)
                dve.drain()
            dve.reciprocal(M.sm_rd[:, b:b + 1], den[:, b:b + 1]).then_inc(att_r, 1)

        negated(0)
        for u in range(len(units)):
            if u + 1 < len(units):
                negated(u + 1)
            denominator(u)
            copied(u)
            after(dve, u)

    def att_act(act, units, n0, after=lambda eng, u: None):
        def exps(u):
            x, b = units[u], u % 2
            act.wait_ge(att_m, done(n0 + u + 1))
            act.wait_ge(att_t, done(n0 + max(u - 1, 0)))
            act.wait_ge(att_r, done(n0 + max(u - 1, 0)))
            act.activation(M.p_sb[:, b, 0:x.nk], M.pair(u % 2, 0, x.nk), ACT.Exp, scale=SCALE,
                           bias=M.sm_neg[:, b:b + 1], accum_out=M.sm_sum[:, b:b + 1])
            if x.sink is not None:
                act.activation(M.sm_sink[:, b:b + 1], x.sink, ACT.Exp, bias=M.sm_neg[:, b:b + 1])
            act.drain().then_inc(att_p, 1)

        def divided(u):
            x, b = units[u], u % 2
            act.wait_ge(att_o, done(n0 + u + 1))
            act.wait_ge(att_r, done(n0 + u + 1))
            act.activation(x.out, M.pair(2 + u % 2, 640, 640 + HD), ACT.Copy, scale=M.sm_rd[:, b:b + 1])\
                .then_inc(att_e, 1)

        exps(0)
        for u in range(len(units)):
            if u + 1 < len(units):
                exps(u + 1)
            if u:
                divided(u - 1)
            after(act, u)
        divided(len(units) - 1)

    kf_rot, kf_low, kf_high = (M.kf[:, i * P:(i + 1) * P] for i in range(3))
    kf_cos, kf_sin = M.kf[:, 3 * P:3 * P + SEQ], M.kf[:, 3 * P + SEQ:3 * P + 2 * SEQ]
    kf_mask = 3 * P + 2 * SEQ

    def qkv_segs(it, u):
        return LAT if not isinstance(it, int) or 4 * it + u < 8 else BOTH

    def qkv_act(act):
        q0 = Q0["qkv"]
        for it, u in chunks(act, 12):
            high(act, "qkv", it, u)
            act.wait_ge(tile_done, done(q0 + 4 * it + u + 1))
            i = 4 * it + u
            pr = (q0 + u) % 4
            if not isinstance(it, int) or i < 8:
                act.activation(M.q_[:, bass.ds(i, 1), :].rearrange("p a t -> p (a t)"), M.pair(pr, 0, SEQ),
                               ACT.Copy).then_inc(evac, 1)
            else:
                dst = (M.k_ if i < 10 else M.v_)[:, i % 2, :]
                act.activation(dst, M.pair(pr), ACT.Copy).then_inc(evac, 1)

    def rope_tiles():
        return [M.q_[:, i, :] for i in range(8)] + [M.k_[:, i, 0:SEQ] for i in range(2)]

    def rope_ps(n):
        return M.pair((Q0["qkv"] + n) % 4, SEQ, 2 * SEQ)

    def qkv_pe(pe):
        q0 = Q0["qkv"]
        def rotate(n):
            pe.wait_ge(evac, done(q0 + n + 1))
            if n >= 4:
                pe.wait_ge(rope_c, done(n - 3))
            pe.matmul(rope_ps(n), kf_rot, rope_tiles()[n], start=True, stop=True).then_inc(rope_r, 1)
        first_two(pe, "qkv", LAT, "n11")
        pe.wait_ge(s_kf, 16)
        for n in range(12):
            if n >= 8:
                pe.wait_ge(rope_c, done(n - 3))
            if n >= 2:
                products(pe, "qkv", n // 4, n % 4, qkv_segs(n // 4, n % 4))
            if 1 <= n <= 10:
                rotate(n - 1)

    def qkv_dve(dve):
        dve.wait_ge(s_kf, 16)
        for n, x in enumerate(rope_tiles()):
            dve.wait_ge(evac, done(Q0["qkv"] + n + 1))
            dve.tensor_tensor(M.gate[:, n % 2, 0:SEQ], x, kf_cos, ALU.mult)
            dve.wait_ge(rope_r, done(n + 1))
            dve.tensor_tensor(rope_ps(n), rope_ps(n), kf_sin, ALU.mult)
            dve.drain()
            dve.tensor_tensor(x, rope_ps(n), M.gate[:, n % 2, 0:SEQ], ALU.add).then_inc(rope_c, 1)

    def prep_pe(pe):
        pe.wait_ge(evac, done(Q0["wo"]))
        for g in range(4):
            pe.wait_ge(rope_c, done(10))
            for t0, tn in BOTH:
                mm = pe.matmul(M.pair(g, t0, t0 + tn), (kf_low, kf_high)[g % 2], M.k_[:, g // 2, t0:t0 + tn],
                               start=True, stop=True)
            mm.then_inc(turn_t, 1)
        pe.wait_ge(turn_c, done(2))
        for t in range(6):
            for c in range(2):
                at = t * 256 + c * P
                mm = pe.transpose(M.ps[:, at:at + P], M.v_[:, c, t * P:(t + 1) * P], ident)
        mm.then_inc(turn_t, 1)

    def prep_act(act):
        for g in range(4):
            act.wait_ge(turn_t, done(g + 1))
            act.activation(M.kd[:, g, :], M.pair(g), ACT.Copy).then_inc(turn_c, 1)
        act.wait_ge(turn_t, done(5))
        act.activation(M.vt[:, :, :].rearrange("p t c -> p (t c)"), M.ps[:, 0:1536], ACT.Copy).then_inc(turn_c, 1)

    def units1():
        out_ = []
        for g in range(4):
            for i in range(4):
                lo, hi = max(i - 1, 0), min(i + 1, 3)
                nb = (hi - lo + 1) * P
                for r in range(4):
                    half = HD * (r % 2)
                    q = M.q_[half:half + HD, 2 * g + r // 2, i * P:(i + 1) * P]
                    k = M.kd[half:half + HD, g, :]
                    masks = []
                    if lo < i:
                        masks.append((0, P, M.kf[:, kf_mask:kf_mask + P]))
                    if hi > i:
                        masks.append((nb - P, P, M.kf[:, kf_mask + P:kf_mask + 2 * P]))
                    keys = [(0, nb, k[:, lo * P:(hi + 1) * P], masks)]
                    for at in range(0, CTX, P):
                        keys.append((nb + at, P, k[:, SEQ + at:SEQ + at + P], []))
                    h = 4 * g + r
                    out_.append(Unit(q, keys, M.sinks[:, h:h + 1], M.nsinks[:, h:h + 1],
                                     [M.vt[:, t, g * HD:(g + 1) * HD] for t in list(range(lo, hi + 1)) + [4, 5]],
                                     (M.o_t, M.o_t2)[g % 2][:, i, r * HD:(r + 1) * HD]))
        return out_

    def group_after(u):
        return ((u - 17) // 16, u % 2) if u >= 17 and u % 16 == 1 else None

    def outputs_pe(pe, u, group=None):
        g, pair = group or group_after(u) or (None, None)
        if g is None:
            return
        pe.wait_ge(att_e, done(16 * g + 16))
        pe.wait_ge(att_p, done(min(u + 1, 64)))
        for c in range(2):
            for i in range(4):
                mm = pe.transpose(M.pair(pair, c * SEQ + i * P, c * SEQ + (i + 1) * P),
                                  (M.o_t, M.o_t2)[g % 2][:, i, c * P:(c + 1) * P], ident)
        mm.then_inc(otr_t, 1)
        pe.wait_ge(xa_ready, done(2 * g + 2))

    def outputs_act(act, u, group=None):
        g, pair = group or group_after(u) or (None, None)
        if g is None:
            return
        act.wait_ge(otr_t, done(g + 1))
        act.activation(M.x_hi[:, 2 * g:2 * g + 2, 0:SEQ], M.pair(pair, 0, 1024).rearrange("p (c t) -> p c t", c=2),
                       ACT.Copy).then_inc(otr_h, 1)

    def outputs_dve(dve, u, group=None):
        g, pair = group or group_after(u) or (None, None)
        if g is None:
            return
        dve.wait_ge(otr_h, done(g + 1))
        dve.tensor_tensor(M.x_lo[:, 2 * g:2 * g + 2, 0:SEQ], M.pair(pair, 0, 1024).rearrange("p (c t) -> p c t", c=2),
                          M.x_hi[:, 2 * g:2 * g + 2, 0:SEQ].bitcast(F32), ALU.subtract)
        dve.drain().then_inc(xa_ready, 2)

    def attn_pe(pe):
        pe.wait_ge(turn_c, done(5))
        att_pe(pe, units1(), 0, outputs_pe)
        outputs_pe(pe, 64, (3, 0))

    def attn_dve(dve):
        dve.wait_ge(turn_c, done(5))
        att_dve(dve, units1(), 0, outputs_dve)
        outputs_dve(dve, 64, (3, 0))

    def attn_act(act):
        att_act(act, units1(), 0, outputs_act)
        outputs_act(act, 64, (3, 0))

    def wo_dve(dve):
        q0 = Q0["wo"]
        for m in range(8):
            dve.wait_ge(tile_done, done(q0 + m + 1))
            o = M.h[:, m, 0:SEQ]
            dve.scalar_tensor_tensor(out=o, in0=M.pair((q0 + m) % 4, 0, SEQ), scalar=M.mods[:, 48 + 16 + m, 0:1],
                                     in1=o, op0=ALU.mult, op1=ALU.add).then_inc(evac, 1)
            dve.drain().then_inc(h_ready, 1)
            early_dve(dve, "wo", m)
        early_dve(dve, "wo", 8)

    class Steps:

        def __init__(self, name, names):
            self.sem, self.names, self.next = sem(name), names, 0

        def after(self, eng, name):
            eng.wait_ge(self.sem, done(self.names.index(name) + 1))

        def mark(self, ins, name):
            assert self.names[self.next] == name, (self.names[self.next], name)
            self.next += 1
            ins.then_inc(self.sem, 1)

    N4, C3 = range(4), range(3)

    def tensor_steps(n):
        last = {e: [f"{s}{n - 1}" for s in x] if n else [] for e, x in
                {-1: ["x0"], 0: ["u"], 1: ["s", "y"], 3: ["yt"]}.items()}
        own = {3: [f"tok0{n}"], 5: [f"tok1{n}", f"tok2{n}"]}
        out_ = [f"mat0{n}", f"mat1{n}"] + last[-1] + [f"m00{n}", f"m01{n}"] + last[0]
        for e in range(1, 7):
            out_ += [f"mt{e}0{n}", f"mt{e}1{n}"] + last.get(e, []) + own.get(e, [])
            out_ += [f"inv{e}0{n}", f"inv{e}1{n}"]
        return out_

    def scalar_steps(n):
        last = {e: [f"{x}{n - 1}"] if n else [] for e, x in {-1: "x0", 0: "u", 2: "sd", 3: "yt", 4: "hi"}.items()}
        own = {3: [f"tok0{n}"], 5: [f"tok1{n}", f"tok2{n}"]}
        out_ = last[-1] + last[0]
        for e in range(1, 7):
            out_ += [f"mt{e}0{n}", f"mt{e}1{n}"] + last.get(e, []) + own.get(e, [])
        return out_

    def vector_steps(n):
        last = {e: [f"{s}{n - 1}" for s in x] if n else [] for e, x in
                {1: ["st", "var"], 2: ["yn"], 3: ["y3"], 4: ["lo"]}.items()}
        out_ = [f"mask0{n}", f"lv00{n}", f"mask1{n}", f"lv01{n}"]
        for e in range(7):
            out_ += [f"inv{e}0{n}", f"inv{e}1{n}"] + last.get(e, [])
        return out_

    T_S = Steps("step_t", [f"head{i}" for i in range(6)] + ["rr", "head6", "head7", "kd", "vt", "mv", "bias", "out"]
                + [f"z{n}" for n in N4] + [f"a{c}" for c in C3] + ["kk0", "bonus0"] + [f"g{c}" for c in C3]
                + ["cum0", "cum1", "cum2", "kk1", "bonus1", "kk2", "bonus2"]
                + [x for n in N4 for x in tensor_steps(n)] + ["x03", "u3", "y3", "yt3"])
    S_S = Steps("step_s", ["sq0", "sq1", "sq2", "rms0", "sq3", "rms1", "rms2", "rms3", "sq4", "sq5", "rms4", "rms5",
                           "rr", "sq6", "sq7", "rms6", "rms7"]
                + ["kd", "vt", "mv", "bias", "out", "low"]
                + [f"sig{n}" for n in N4] + [f"a{c}" for c in C3] + ["kk0"] + [f"g{c}" for c in C3]
                + ["cend0", "exp0", "cend1", "kk1", "exp1", "cend2", "kk2", "exp2", "ez"]
                + [x for n in N4 for x in scalar_steps(n)] + ["x03", "u3", "sd3", "yt3", "hi3"])
    V_S = Steps("step_v", [f"head{i}" for i in range(8)] + ["out"] + ["shift"] + [f"z{n}" for n in N4]
                + ["kk0", "rk0", "kn0", "bonus0", "cend0", "abc0"]
                + [x for c in (1, 2) for x in (f"cend{c}", f"kk{c}", f"rk{c}", f"kn{c}", f"bonus{c}", f"abc{c}")]
                + ["ezs"]
                + [x for n in N4 for x in vector_steps(n)] + ["var3", "yn3", "y33", "lo3"])
    P_S = Steps("step_p", [f"lv{e}{gr}{n}" for n in N4 for e in range(1, 7) for gr in (0, 1)])
    s_k2 = sem("s_k2", False)
    s_rr = sem("s_rr", False)
    s_tz = sem("s_tz", False)

    k_low, k_high, k_anti = (M.ks[:, i * P:(i + 1) * P] for i in range(3))
    k_tri = M.ks[:, 3 * P:5 * P]
    k_mask4 = M.ks[:, 5 * P:9 * P]

    def k_level(e):
        return M.ks[:, (9 + e) * P:(10 + e) * P]

    rr_dram = nc.dram_tensor("rr_scratch", (6, 384), F32, kind="Internal").ap()

    def tables_act(act):
        act.wait_ge(tile_done, done(Q0["w_in"]))
        act.wait_ge(g_ready, done(4 * HALF))
        act.dma_start(M.m_rows[:, :, :], A["mem_2"][0].rearrange("(t p) d -> p t d", p=P)).then_inc(s_mem, 16)
        act.dma_start(M.ks[:, :], A["k_second"]).then_inc(s_k2, 16)
        act.dma_start(M.lw[0:32, :], A["rwkv_w2_2"][0]).then_inc(s_k2, 16)
        act.dma_start(M.lw[32:64, :], A["rwkv_a2_2"][0]).then_inc(s_k2, 16)
        act.dma_start(M.lw[64:128, :], A["rwkv_g2_2"][0]).then_inc(s_k2, 16)
        act.dma_start(M.w0b[:, :], A["rwkv_w0_2"][0:1, :].to_broadcast([P, 384])).then_inc(s_k2, 16)
        act.dma_start(M.hot[:, :], A["k_hot"]).then_inc(s_k2, 16)
        act.activation(M.relb[:, :], M.kb[:, P:P + 8], ACT.Copy)
        act.drain()
        act.dma_start(M.relb[0:32, 0:6], A["rel_bias_2"]).then_inc(s_k2, 16)

    def mem_pe(pe):
        pe.wait_ge(s_mem, 16)
        pe.wait_ge(x_ready, done(8 * (NN["final"] + 1)))
        for k in range(KD):
            pe.wait_ge(mem_ready, done(k - 3))
            for t in range(2):
                mm = pe.transpose(M.pair(k % 4, t * P, (t + 1) * P), M.m_rows[:, t, k * P:(k + 1) * P], ident)
            mm.then_inc(mem_t, 1)

    def mem_act(act):
        for k in range(KD):
            act.wait_ge(mem_t, done(k + 1))
            act.activation(M.h[:, k, SEQ:TOK], M.pair(k % 4, 0, CTX), ACT.Copy).then_inc(mem_ready, 1)

    SQUARE_AT = {("w_in", 0): 0, ("w_in", 1): 1, ("w_in", 2): 2, ("w_in", 3): 3, ("w_in", 15): 4, ("w_in", 16): 5}
    RMS_AT = {("w_in", 2): (0,), ("w_in", 3): (1, 2, 3), ("mem_kv", 0): (4,), ("mem_kv", 1): (5,)}

    def w_in_act(act):
        for name, n, w0_, w1_ in (("w_in", 17, 0, SEQ), ("mem_kv", 4, SEQ, TOK)):
            for it, u in peeled_chunks(act, n) if name == "w_in" else chunks(act, n):
                high(act, name, it, u)
                act.wait_ge(tile_done, done(Q0[name] + 4 * it + u + 1))
                if name == "w_in":
                    dst = M.pj[:, bass.ds(4 * it + u, 1), :].rearrange("p a t -> p (a t)")
                else:
                    dst = M.mkv[:, 4 * it + u, :]
                act.activation(dst, M.pair((Q0[name] + u) % 4, w0_, w1_), ACT.Copy).then_inc(evac, 1)
                if not isinstance(it, int):
                    continue
                at = (name, 4 * it + u)
                if at in SQUARE_AT:
                    act.wait_ge(evac, done(Q0[name] + 4 * it + u + 1))
                    head_square(act, SQUARE_AT[at])
                for i in RMS_AT.get(at, ()):
                    head_rms(act, i)

    def head_ps(i):
        x, w, _ = head_tiles()[i]
        return M.pair((Q0["w_in"] + (0, 1, 2, 3, 15, 16)[i]) % 4 if i < 6 else i - 6, SEQ, SEQ + w)

    def head_square(act, i):
        x, w, _ = head_tiles()[i]
        if i >= 2:
            T_S.after(act, f"head{i - 2}")
        S_S.mark(act.activation(M.n_sq[:, i % 2, 0:w], x, ACT.Square), f"sq{i}")

    def head_sum(pe, i):
        x, w, _ = head_tiles()[i]
        S_S.after(pe, f"sq{i}")
        T_S.mark(pe.matmul(head_ps(i), head1, M.n_sq[:, i % 2, 0:w], start=True, stop=True), f"head{i}")

    def head_rms(act, i):
        x, w, _ = head_tiles()[i]
        T_S.after(act, f"head{i}")
        if i >= 2:
            V_S.after(act, f"head{i - 2}")
        S_S.mark(act.activation(M.n_t[:, i % 2, 0:w], head_ps(i), ACT.Sqrt, scale=1.0 / HD, bias=eps_col), f"rms{i}")

    def head_norm(dve, i):
        x, w, gain = head_tiles()[i]
        S_S.after(dve, f"rms{i}")
        dve.reciprocal(head_ps(i), M.n_t[:, i % 2, 0:w])
        dve.drain()
        V_S.mark(dve.scalar_tensor_tensor(out=x, in0=x, scalar=M.col(gain), in1=head_ps(i),
                                          op0=ALU.mult, op1=ALU.mult), f"head{i}")

    def w_in_pe(pe):
        first_two(pe, "w_in", LAT, "mix")
        for it, u in peeled_chunks(pe, 17):
            peeled = isinstance(it, int)
            if not (peeled and 4 * it + u < 2):
                products(pe, "w_in", it, u, LAT)
            if peeled and 4 * it + u in (2, 3):
                head_sum(pe, u - 2)
                if u == 3:
                    head_sum(pe, 2)
                    head_sum(pe, 3)
        for u in range(4):
            V_S.after(pe, f"head{max(u + 2, 3)}")
            products(pe, "mem_kv", 0, u, MEM)
            if u < 2:
                head_sum(pe, 4 + u)

    def head_tiles():
        return ([(M.pj[:, i, :], SEQ, "attn_q_norm_2") for i in range(3)] + [(M.pj[:, 3, :], SEQ, "attn_k_norm_2")]
                + [(M.pj[:, i, :], SEQ, "mem_q_norm_2") for i in (15, 16)]
                + [(M.mkv[:, i, :], CTX, "mem_k_norm_2") for i in (0, 1)])

    def mix_prep_pe(pe):
        pe.wait_ge(evac, done(Q0["w_out"]))
        pe.wait_ge(s_k2, 16 * 7)
        T_S.mark(pe.matmul(M.ps[0:6, 3072:3072 + 384], M.relb[0:33, 0:6], M.hot[0:33, :], start=True, stop=True), "rr")
        for i in (6, 7):
            head_sum(pe, i)
        V_S.after(pe, "head7")
        for g in (0, 1):
            mm = pe.matmul(M.ps[:, g * SEQ:(g + 1) * SEQ], (k_low, k_high)[g], M.pj[:, 3, :], start=True, stop=True)
        T_S.mark(mm, "kd")
        for t in range(4):
            mm = pe.transpose(M.pair(1, t * P, (t + 1) * P), M.pj[:, 4, t * P:(t + 1) * P], ident)
        T_S.mark(mm, "vt")
        for t in range(2):
            for c in range(2):
                at = t * 256 + c * P
                mm = pe.transpose(M.pair(2, at, at + P), M.mkv[:, 2 + c, t * P:(t + 1) * P], ident)
        T_S.mark(mm, "mv")
        pe.wait_ge(s_tz, 16)
        S_S.after(pe, "mv")
        for n in range(3):
            mm = pe.matmul(M.ps[:, 2048 + n * 512:2560 + n * 512], k_anti,
                           M.tz[:, 2 * n:2 * n + 2, :].rearrange("p h k -> p (h k)"), start=True, stop=True)
        T_S.mark(mm, "bias")

    def mix_prep_act(act):
        act.wait_ge(evac, done(Q0["w_out"]))
        T_S.after(act, "rr")
        S_S.mark(act.activation(M.rr[0:6, :], M.ps[0:6, 3072:3072 + 384], ACT.Copy), "rr")
        S_S.after(act, "rr")
        act.dma_start(rr_dram, M.rr[0:6, :]).then_inc(s_rr, 16)
        head_square(act, 6)
        head_square(act, 7)
        head_rms(act, 6)
        head_rms(act, 7)
        act.wait_ge(s_rr, 16)
        V_S.after(act, "head5")
        skew = bass.AP(rr_dram.tensor, 0, [[1, P], [384, 6], [1, 2 * P]])
        act.dma_start(M.tz[:, :, :], skew).then_inc(s_tz, 16)
        T_S.after(act, "kd")
        V_S.after(act, "head7")
        S_S.mark(act.activation(M.qg[:, :, :].rearrange("p g t -> p (g t)"), M.ps[:, 0:1024], ACT.Copy), "kd")
        T_S.after(act, "vt")
        S_S.mark(act.activation(M.kg[:, 0:SEQ], M.pair(1, 0, SEQ), ACT.Copy), "vt")
        T_S.after(act, "mv")
        S_S.mark(act.activation(M.pj[:, 3, :], M.pair(2, 0, SEQ), ACT.Copy), "mv")
        T_S.after(act, "bias")
        S_S.mark(act.activation(M.bias[:, :, :].rearrange("p h k -> p (h k)"), M.ps[:, 2048:2048 + 1536], ACT.Copy,
                                scale=1.0 / SCALE), "bias")

    def w_in_dve(dve):
        for i in range(6):
            head_norm(dve, i)

    def mix_prep_dve(dve):
        for i in (6, 7):
            head_norm(dve, i)

    def units2():
        out_ = []
        for i in range(4):
            lo = max(i - 1, 0)
            nb = (i - lo + 1) * P
            for hh in range(6):
                half, g = HD * (hh % 2), hh // 3
                out_.append(Unit(M.pj[half:half + HD, hh // 2, i * P:(i + 1) * P],
                                 [(0, nb, M.qg[half:half + HD, g, lo * P:(i + 1) * P],
                                   [(0, nb, M.bias[:, hh, 2 * P - nb:2 * P])])],
                                 M.sinks[:, 16 + hh:17 + hh], M.nsinks[:, 16 + hh:17 + hh],
                                 [M.kg[:, t * P + g * HD:t * P + (g + 1) * HD] for t in range(lo, i + 1)],
                                 M.h[:, 2 * i + hh // 4, SEQ + (hh % 4) * HD:SEQ + (hh % 4 + 1) * HD]))
        for i in range(4):
            for hh in range(4):
                half = HD * (hh % 2)
                out_.append(Unit(M.pj[half:half + HD, 15 + hh // 2, i * P:(i + 1) * P],
                                 [(0, CTX, M.mkv[half:half + HD, hh // 2, :], [])], None, None,
                                 [M.pj[:, 3, t * 256 + hh * HD:t * 256 + (hh + 1) * HD] for t in range(2)],
                                 M.o_t[:, i, hh * HD:(hh + 1) * HD]))
        return out_

    OUT_TILES = [0, 1, 2, 6, 7]

    def mix_out_pe(pe):
        pe.wait_ge(att_e, done(64 + 40))
        for n in range(5):
            for i in range(4):
                src = M.h[:, 2 * i + n // 2, SEQ + (n % 2) * P:SEQ + (n % 2 + 1) * P] if n < 3 \
                    else M.o_t[:, i, (n - 3) * P:(n - 2) * P]
                mm = pe.transpose(M.ps[:, n * 512 + i * P:n * 512 + (i + 1) * P], src, ident)
        T_S.mark(mm, "out")

    def mix_out_act(act):
        T_S.after(act, "out")
        for n, c in enumerate(OUT_TILES):
            ins = act.activation(M.x_hi[:, c, 0:SEQ], M.ps[:, n * 512:(n + 1) * 512], ACT.Copy)
        S_S.mark(ins, "out")

    def mix_out_dve(dve):
        S_S.after(dve, "out")
        for n, c in enumerate(OUT_TILES):
            ins = dve.tensor_tensor(M.x_lo[:, c, 0:SEQ], M.ps[:, n * 512:(n + 1) * 512],
                                    M.x_hi[:, c, 0:SEQ].bitcast(F32), ALU.subtract)
        V_S.mark(ins, "out")

    r_t = [M.pj[:, 5 + c, :] for c in C3]
    k_t = [M.pj[:, 8 + c, :] for c in C3]
    v_t = [M.pj[:, 11 + c, :] for c in C3]
    lor = M.pj[:, 14, :]
    g_t = [M.pj[:, c, :] for c in C3]
    kk_t = [M.pj[:, 3, :], M.pj[:, 4, :], M.pj[:, 15, :]]
    a_t = [M.av[:, c, :] for c in C3]
    bonus_t = [M.h[:, 2 * c:2 * c + 2, SEQ:TOK] for c in C3]
    H6 = range(6)
    CUM_PAIRS = (2, 3, 2)

    def two(ap):
        return ap.rearrange("p (a b) -> p a b", a=2)

    def rw_pre_dve(dve):
        for i in range(10):
            x, d = M.pj[:, 5 + i, :], M.dd[:, i % 2, :]
            dve.tensor_tensor(d[:, 1:SEQ], x[:, 0:SEQ - 1], x[:, 1:SEQ], ALU.subtract)
            dve.tensor_scalar(d[:, 0:1], x[:, 0:1], -1.0, None, ALU.mult)
            dve.drain()
            ins = dve.scalar_tensor_tensor(out=x, in0=d, scalar=M.col("rwkv_mu_2", i), in1=x, op0=ALU.mult, op1=ALU.add)
        V_S.mark(ins, "shift")
        for n in N4:
            T_S.after(dve, f"z{n}")
            V_S.mark(dve.tensor_tensor(M.sig[:, n, :], M.pair(n, 0, 384), M.w0b[:, :], ALU.add), f"z{n}")
        for c in C3:
            if c:
                S_S.after(dve, f"cend{c}")
                V_S.mark(dve.tensor_scalar(M.cend[:, 1, c, :], M.cend[:, 0, c, :], -1.0, None, ALU.mult), f"cend{c}")
            dve.tensor_scalar(kk_t[c], k_t[c], M.col("rwkv_k_k_2", c), None, ALU.mult)
            dve.drain()
            V_S.mark(dve.tensor_tensor(M.hq[:, 0, :], kk_t[c], kk_t[c], ALU.mult), f"kk{c}")
            S_S.after(dve, f"a{c}")
            dve.tensor_scalar(M.dd[:, 0, :], a_t[c], 1.0, M.col("rwkv_k_a_2", c), ALU.subtract, ALU.mult)
            dve.drain()
            dve.scalar_tensor_tensor(out=k_t[c], in0=M.dd[:, 0, :], scalar=1.0, in1=k_t[c], op0=ALU.add, op1=ALU.mult)
            dve.drain()
            V_S.mark(dve.scalar_tensor_tensor(out=M.hq[:, 1, :], in0=r_t[c], scalar=M.col("rwkv_r_k_2", c),
                                              in1=k_t[c], op0=ALU.mult, op1=ALU.mult), f"rk{c}")
            S_S.after(dve, f"kk{c}")
            dve.tensor_scalar(M.dd[:, 1, :], M.dd[:, 1, :], L2_EPS, None, ALU.max)
            dve.drain()
            dve.reciprocal(M.dd[:, 1, :], M.dd[:, 1, :])
            dve.drain()
            V_S.mark(dve.tensor_tensor(kk_t[c], kk_t[c], M.dd[:, 1, :], ALU.mult), f"kn{c}")
            T_S.after(dve, f"bonus{c}")
            V_S.mark(dve.tensor_tensor(bonus_t[c], two(M.pair(1, 0, SEQ)), two(v_t[c]), ALU.mult), f"bonus{c}")
            if c == 0:
                S_S.after(dve, "cend0")
                V_S.mark(dve.tensor_scalar(M.cend[:, 1, 0, :], M.cend[:, 0, 0, :], -1.0, None, ALU.mult), "cend0")
            V_S.after(dve, f"bonus{c}")
            S_S.after(dve, f"exp{c}")
            dve.tensor_tensor(a_t[c], a_t[c], kk_t[c], ALU.mult)
            dve.tensor_tensor(r_t[c], r_t[c], M.ex[:, 0, :], ALU.mult)
            dve.tensor_tensor(k_t[c], k_t[c], M.ex[:, 2, :], ALU.mult)
            dve.drain()
            dve.scalar_tensor_tensor(out=kk_t[c], in0=kk_t[c], scalar=-1.0, in1=M.ex[:, 1, :],
                                     op0=ALU.mult, op1=ALU.mult)
            dve.tensor_tensor(a_t[c], a_t[c], M.ex[:, 2, :], ALU.mult)
            V_S.mark(dve.drain(), f"abc{c}")
        V_S.mark(dve.tensor_tensor(M.cend[:, 2, :, 0:3], M.cend[:, 0, :, 0:3], M.cend[:, 0, :, 1:4], ALU.add), "ezs")

    def rw_pre_act(act):
        def kk_norm(c):
            T_S.after(act, f"kk{c}")
            if c:
                V_S.after(act, f"kn{c - 1}")
            V_S.after(act, f"rk{c}")
            S_S.mark(act.activation(M.dd[:, 1, :], M.pair(0, 0, SEQ), ACT.Sqrt), f"kk{c}")

        V_S.after(act, "shift")
        act.activation(lor[0:32, :], lor[0:32, :], ACT.Tanh)
        S_S.mark(act.activation(lor[64:128, :], lor[64:128, :], ACT.Sigmoid), "low")
        for n in N4:
            V_S.after(act, f"z{n}")
            S_S.mark(act.activation(M.sig[:, n, :], M.sig[:, n, :], ACT.Sigmoid), f"sig{n}")
        for c in C3:
            T_S.after(act, f"a{c}")
            S_S.mark(act.activation(a_t[c], M.pair(c, 0, SEQ), ACT.Sigmoid, bias=M.col("rwkv_a0_2", c)), f"a{c}")
        kk_norm(0)
        for c in C3:
            T_S.after(act, f"g{c}")
            S_S.mark(act.activation(g_t[c], M.pair(c, SEQ, 2 * SEQ), ACT.Copy), f"g{c}")
        def sums(c):
            return M.pair(CUM_PAIRS[c], 0, 1024).rearrange("p (n s t) -> p n s t", n=4, s=2)

        def tile_sums(c):
            T_S.after(act, f"cum{c}")
            S_S.mark(act.activation(M.cend[:, 0, c, :], sums(c)[:, :, 0, P - 1], ACT.Copy, scale=KAPPA / 2), f"cend{c}")

        def exps(c):
            V_S.after(act, f"cend{c}")
            if c:
                V_S.after(act, f"abc{c - 1}")
            for n in N4:
                t = slice(n * P, (n + 1) * P)
                plus, minus = M.cend[:, 0, c, n:n + 1], M.cend[:, 1, c, n:n + 1]
                act.activation(M.ex[:, 0, t], sums(c)[:, n, 0, :], ACT.Exp, scale=-KAPPA, bias=plus)
                act.activation(M.ex[:, 1, t], sums(c)[:, n, 1, :], ACT.Exp, scale=-KAPPA, bias=plus)
                ins = act.activation(M.ex[:, 2, t], sums(c)[:, n, 0, :], ACT.Exp, scale=KAPPA, bias=minus)
            S_S.mark(ins, f"exp{c}")

        tile_sums(0)
        exps(0)
        for c in (1, 2):
            tile_sums(c)
            kk_norm(c)
            exps(c)
        V_S.after(act, "ezs")
        S_S.mark(act.activation(M.cend[:, 3, :, 0:3], M.cend[:, 2, :, 0:3], ACT.Exp, scale=-1.0), "ez")

    def rw_pre_pe(pe):
        def kk_sums(c):
            V_S.after(pe, f"kk{c}")
            S_S.after(pe, "a0" if c == 0 else f"kk{c - 1}")
            T_S.mark(pe.matmul(M.pair(0, 0, SEQ), head1, M.hq[:, 0, :], start=True, stop=True), f"kk{c}")
            V_S.after(pe, f"rk{c}")
            if c:
                V_S.after(pe, f"bonus{c - 1}")
            else:
                S_S.after(pe, "a1")
            T_S.mark(pe.matmul(M.pair(1, 0, SEQ), head1, M.hq[:, 1, :], start=True, stop=True), f"bonus{c}")

        S_S.after(pe, "low")
        V_S.after(pe, "out")
        for n in N4:
            T_S.mark(pe.matmul(M.pair(n, 0, 384), lor[0:32, n * P:(n + 1) * P], M.lw[0:32, :], start=True, stop=True),
                     f"z{n}")
        for c in C3:
            V_S.after(pe, f"z{c}")
            T_S.mark(pe.matmul(M.pair(c, 0, SEQ), M.lw[32:64, c * P:(c + 1) * P], lor[32:64, :], start=True, stop=True),
                     f"a{c}")
        kk_sums(0)
        for c in C3:
            T_S.mark(pe.matmul(M.pair(c, SEQ, 2 * SEQ), M.lw[64:128, c * P:(c + 1) * P], lor[64:128, :],
                               start=True, stop=True), f"g{c}")
        def cum(c):
            if c == 2:
                S_S.after(pe, "exp0")
            for n in N4:
                mm = pe.matmul(M.pair(CUM_PAIRS[c], n * 256, (n + 1) * 256), M.sig[:, n, c * P:(c + 1) * P], k_tri,
                               start=True, stop=True)
            T_S.mark(mm, f"cum{c}")

        S_S.after(pe, "g2")
        V_S.after(pe, "z3")
        cum(0)
        cum(1)
        cum(2)
        kk_sums(1)
        kk_sums(2)

    def head_rows(hh):
        return slice(HD * (hh % 2), HD * (hh % 2) + HD)

    def by_parity(hh):
        at = (6 + hh % 2) * 512 + (hh // 2) * HD
        return M.ps[:, at:at + HD]

    def bank(b, n=384, at=0):
        return M.ps[:, b * 512 + at:b * 512 + at + n]

    def heads(ap, h=3):
        return ap.rearrange("p (h x) -> p h x", h=h)

    def of_parity(ap, p):
        return ap.rearrange("p (c a x) -> p a c x", c=3, a=2)[:, p, :, :]

    STATE_AT = 256
    GROUPS = ((0, range(0, 3)), (1, range(3, 6)))

    def level(eng, n, e, gr):
        hs = slice(3 * gr, 3 * gr + 3)
        return eng.tensor_tensor(M.lv[:, hs, :], M.m4[:, n % 2, hs, 0:P],
                                 k_level(e).unsqueeze(1).to_broadcast([P, 3, P]), ALU.mult)

    def rw_pool(pool):
        for n in N4:
            for e in range(1, 7):
                for gr in (0, 1):
                    if e == 1:
                        V_S.after(pool, f"inv0{gr}{n}")
                    else:
                        T_S.after(pool, f"mt{e - 1}{gr}{n}")
                    P_S.mark(level(pool, n, e, gr), f"lv{e}{gr}{n}")

    def rw_pe(pe):
        def mats(n, gr, hs):
            if n:
                V_S.after(pe, f"inv6{gr}{n - 1}")
            t = slice(n * P, (n + 1) * P)
            for hh in hs:
                r, c = head_rows(hh), hh // 2
                for q_, (lhs, rhs) in enumerate(((a_t, kk_t), (a_t, r_t), (k_t, kk_t), (k_t, r_t))):
                    mm = pe.matmul(bank(hh, P, q_ * P), lhs[c][r, t], rhs[c][r, t], start=True, stop=True)
            T_S.mark(mm, f"mat{gr}{n}")

        def first_level(n, gr, hs):
            V_S.after(pe, f"lv0{gr}{n}")
            for i, hh in enumerate(hs):
                mm = pe.transpose(bank(3 * gr, P, i * P), M.lv[:, hh, :], ident)
            T_S.mark(mm, f"m0{gr}{n}")

        def level_times_inv(n, e, gr, hs):
            P_S.after(pe, f"lv{e}{gr}{n}")
            V_S.after(pe, f"inv{e - 1}{gr}{n}")
            for i, hh in enumerate(hs):
                mm = pe.matmul(bank(3 * gr, P, i * P), M.lv[:, hh, :], M.inv[:, hh, :], start=True, stop=True)
            T_S.mark(mm, f"mt{e}{gr}{n}")

        def inv_step(n, e, gr, hs):
            S_S.after(pe, f"mt{e}{gr}{n}")
            inv_t = M.inv_t[n % 2]
            if e < 6:
                for i, hh in enumerate(hs):
                    pe.matmul(bank(3 * gr + 1, P, i * P), inv_t[:, hh, :], M.mt[:, hh, :], start=True, stop=True)
            for i, hh in enumerate(hs):
                mm = pe.matmul(bank(3 * gr + 2, P, i * P), M.mt[:, hh, :], inv_t[:, hh, :], start=True, stop=True)
            T_S.mark(mm, f"inv{e}{gr}{n}")

        def tokens(n, q_):
            t = slice(n * P, (n + 1) * P)
            if q_ == 0:
                if n:
                    V_S.after(pe, f"yn{n - 1}")
            else:
                S_S.after(pe, f"tok{q_ - 2}{n}" if q_ == 2 else f"yt{n - 1}") if q_ == 2 or n else None
            for c in C3:
                mm = pe.transpose(bank((7, 6, 7)[q_], P, c * P), (a_t, k_t, v_t)[q_][c][:, t], ident)
            T_S.mark(mm, f"tok{q_}{n}")

        def x0(n):
            S_S.after(pe, f"tok2{n}")
            if n:
                V_S.after(pe, f"st{n - 1}")
            t = slice(n * P, (n + 1) * P)
            for hh in H6:
                r, c = head_rows(hh), hh // 2
                mm = pe.matmul(by_parity(hh), M.m4[:, n % 2, hh, 2 * P:3 * P], M.tok[:, 2, hh * HD:(hh + 1) * HD],
                               start=True, stop=(n == 0))
                if n:
                    mm = pe.matmul(by_parity(hh), kk_t[c][r, t], M.z[r, c, :], start=False, stop=True)
            T_S.mark(mm, f"x0{n}")

        def u(n):
            S_S.after(pe, f"x0{n}")
            for hh in H6:
                mm = pe.matmul(bank(6, HD, hh * HD), M.inv_t[n % 2][:, hh, :], M.x0[:, hh * HD:(hh + 1) * HD],
                               start=True, stop=True)
            T_S.mark(mm, f"u{n}")

        def state(n):
            S_S.after(pe, f"u{n}")
            for hh in H6:
                r, c = head_rows(hh), hh // 2
                at = 7 * 512 + STATE_AT + c * HD
                o = M.ps[r, at:at + HD]
                pe.matmul(o, M.tok[:, 0, hh * HD:(hh + 1) * HD], M.u[:, hh * HD:(hh + 1) * HD],
                          start=True, stop=False)
                mm = pe.matmul(o, M.tok[:, 1, hh * HD:(hh + 1) * HD], M.tok[:, 2, hh * HD:(hh + 1) * HD],
                               start=False, stop=True)
            T_S.mark(mm, f"s{n}")

        def y(n):
            S_S.after(pe, f"u{n}")
            t = slice(n * P, (n + 1) * P)
            for hh in H6:
                r, c = head_rows(hh), hh // 2
                o = by_parity(hh)
                pe.matmul(o, M.m4[:, n % 2, hh, 3 * P:4 * P], M.tok[:, 2, hh * HD:(hh + 1) * HD],
                          start=True, stop=False)
                mm = pe.matmul(o, M.m4[:, n % 2, hh, P:2 * P], M.u[:, hh * HD:(hh + 1) * HD],
                               start=False, stop=(n == 0))
                if n:
                    mm = pe.matmul(o, r_t[c][r, t], M.z[r, c, :], start=False, stop=True)
            T_S.mark(mm, f"y{n}")

        def turned(n):
            V_S.after(pe, f"yn{n}")
            for c in C3:
                mm = pe.transpose(bank(6, P, c * P), M.y[:, c * P:(c + 1) * P], ident)
            T_S.mark(mm, f"yt{n}")

        V_S.after(pe, "ezs")
        for n in N4:
            for gr, hs in GROUPS:
                mats(n, gr, hs)
            if n:
                x0(n - 1)
            for gr, hs in GROUPS:
                first_level(n, gr, hs)
            if n:
                u(n - 1)
            for e in range(1, 7):
                for gr, hs in GROUPS:
                    level_times_inv(n, e, gr, hs)
                if n and e == 1:
                    state(n - 1)
                    y(n - 1)
                if e == 3:
                    if n:
                        turned(n - 1)
                    tokens(n, 0)
                if e == 5:
                    tokens(n, 1)
                    tokens(n, 2)
                for gr, hs in GROUPS:
                    inv_step(n, e, gr, hs)
        V_S.after(pe, "inv613")
        x0(3)
        u(3)
        y(3)
        turned(3)

    def rw_act(act):
        def x0(n):
            T_S.after(act, f"x0{n}")
            for p in (0, 1):
                ins = act.activation(of_parity(M.x0[:, :], p), heads(bank(6 + p, 192)), ACT.Copy)
            S_S.mark(ins, f"x0{n}")

        def u(n):
            T_S.after(act, f"u{n}")
            S_S.mark(act.activation(M.u[:, :], bank(6), ACT.Copy), f"u{n}")

        def deviation(n):
            V_S.after(act, f"var{n}")
            S_S.mark(act.activation(M.gn[:, 2, :], M.gn[:, 1, :], ACT.Sqrt, scale=1.0 / HD, bias=gn_eps_col), f"sd{n}")

        def turned(n):
            T_S.after(act, f"yt{n}")
            for c in C3:
                ins = act.activation(M.y1[:, c, :], bank(6, P, c * P), ACT.Identity,
                                     scale=M.col("rwkv_ln_w_2", c), bias=M.col("rwkv_ln_b_2", c))
            S_S.mark(ins, f"yt{n}")

        def high_part(n):
            V_S.after(act, f"y3{n}")
            S_S.mark(act.activation(M.x_hi[:, 3:6, n * P:(n + 1) * P], M.y1[:, :, :], ACT.Copy), f"hi{n}")

        def tokens(n, q_):
            T_S.after(act, f"tok{q_}{n}")
            S_S.mark(act.activation(M.tok[:, q_, :], bank((7, 6, 7)[q_]), ACT.Copy), f"tok{q_}{n}")

        for n in N4:
            if n:
                x0(n - 1)
                u(n - 1)
            for e in range(1, 7):
                for gr in (0, 1):
                    T_S.after(act, f"mt{e}{gr}{n}")
                    S_S.mark(act.activation(M.mt[:, 3 * gr:3 * gr + 3, :], heads(bank(3 * gr)), ACT.Copy),
                             f"mt{e}{gr}{n}")
                if n and e == 2:
                    deviation(n - 1)
                if n and e == 3:
                    turned(n - 1)
                if n and e == 4:
                    high_part(n - 1)
                for q_ in {3: (0,), 5: (1, 2)}.get(e, ()):
                    tokens(n, q_)
        for step in (x0, u, deviation, turned, high_part):
            step(3)

    def rw_dve(dve):
        eye3 = ident.unsqueeze(1).to_broadcast([P, 3, P])

        def masked(n, gr):
            hs = slice(3 * gr, 3 * gr + 3)
            T_S.after(dve, f"mat{gr}{n}")
            V_S.mark(dve.copy_predicated(M.m4[:, n % 2, hs, :],
                                         k_mask4.bitcast(U32).unsqueeze(1).to_broadcast([P, 3, 512]),
                                         heads(M.ps[:, 1536 * gr:1536 * (gr + 1)])), f"mask{gr}{n}")
            V_S.after(dve, f"mask{gr}{n}")
            V_S.mark(level(dve, n, 0, gr), f"lv0{gr}{n}")

        def inv_start(n, gr):
            hs = slice(3 * gr, 3 * gr + 3)
            V_S.after(dve, f"lv0{gr}{n}")
            dve.tensor_tensor(M.inv_t[n % 2][:, hs, :], M.lv[:, hs, :], eye3, ALU.add)
            T_S.after(dve, f"m0{gr}{n}")
            dve.tensor_tensor(M.inv[:, hs, :], heads(bank(3 * gr)), eye3, ALU.add)
            V_S.mark(dve.drain(), f"inv0{gr}{n}")

        def inv_sums(n, e, gr):
            hs = slice(3 * gr, 3 * gr + 3)
            inv, inv_t = M.inv[:, hs, :], M.inv_t[n % 2][:, hs, :]
            T_S.after(dve, f"inv{e}{gr}{n}")
            if e < 6:
                dve.tensor_tensor(inv, heads(bank(3 * gr + 1)), inv, ALU.add)
            dve.tensor_tensor(inv_t, heads(bank(3 * gr + 2)), inv_t, ALU.add)
            V_S.mark(dve.drain(), f"inv{e}{gr}{n}")

        y6, q6 = heads(M.y[:, :], 6), heads(M.ysq[:, :], 6)

        def over_head(i):
            return M.gn[:, i, :].unsqueeze(2).to_broadcast([P, 6, HD])

        def state_and_variance(n):
            T_S.after(dve, f"y{n}")
            if n < 3:
                ps_s = M.ps[:, 7 * 512 + STATE_AT:7 * 512 + STATE_AT + 192].rearrange("p (c x) -> p c x", c=3)
                if n:
                    dve.tensor_tensor(M.z[:, :, :], ps_s, M.z[:, :, :], ALU.add)
                    dve.drain()
                for c in C3:
                    src = M.z[:, c, :] if n else ps_s[:, c, :]
                    ins = dve.tensor_scalar(M.z[:, c, :], src, M.cend[:, 3, c, n:n + 1], None, ALU.mult)
                V_S.mark(ins, f"st{n}")
            y_ps = [heads(bank(6 + p, 192)) for p in (0, 1)]
            for p in (0, 1):
                dve.tensor_reduce(M.gn[:, 0, p:6:2], y_ps[p], AX.X, ALU.add)
            dve.drain()
            dve.tensor_scalar(M.gn[:, 0, :], M.gn[:, 0, :], -1.0 / HD, None, ALU.mult)
            dve.drain()
            for p in (0, 1):
                dve.tensor_tensor(of_parity(M.y[:, :], p), y_ps[p],
                                  M.gn[:, 0, p:6:2].unsqueeze(2).to_broadcast([P, 3, HD]), ALU.add)
            dve.drain()
            dve.tensor_tensor(q6, y6, y6, ALU.mult)
            dve.drain()
            V_S.mark(dve.tensor_reduce(M.gn[:, 1, :], q6, AX.X, ALU.add), f"var{n}")

        def normed(n):
            S_S.after(dve, f"sd{n}")
            dve.reciprocal(M.gn[:, 3, :], M.gn[:, 2, :])
            dve.drain()
            V_S.mark(dve.tensor_tensor(y6, y6, over_head(3), ALU.mult), f"yn{n}")

        def gated(n):
            S_S.after(dve, f"yt{n}")
            for c in C3:
                b = M.h[:, 2 * c + n // 2, SEQ + (n % 2) * P:SEQ + (n % 2 + 1) * P]
                dve.tensor_tensor(M.y1[:, c, :], M.y1[:, c, :], b, ALU.add)
            dve.drain()
            V_S.mark(dve.tensor_tensor(M.y1[:, :, :], M.y1[:, :, :], M.pj[:, 0:3, n * P:(n + 1) * P], ALU.mult), f"y3{n}")

        def low_part(n):
            S_S.after(dve, f"hi{n}")
            V_S.mark(dve.tensor_tensor(M.x_lo[:, 3:6, n * P:(n + 1) * P], M.y1[:, :, :],
                                       M.x_hi[:, 3:6, n * P:(n + 1) * P].bitcast(F32), ALU.subtract), f"lo{n}")

        of_last = {1: state_and_variance, 2: normed, 3: gated, 4: low_part}
        dve.wait_ge(zero_ready, done(3))
        for n in N4:
            for gr in (0, 1):
                masked(n, gr)
            for gr in (0, 1):
                inv_start(n, gr)
            for e in range(1, 7):
                for gr in (0, 1):
                    inv_sums(n, e, gr)
                if n and e in of_last:
                    of_last[e](n - 1)
        for step in (state_and_variance, normed, gated, low_part):
            step(3)

    def w_out_dve(dve):
        q0 = Q0["w_out"]
        for m in range(8):
            dve.wait_ge(tile_done, done(q0 + m + 1))
            o = M.h[:, m, 0:SEQ]
            dve.tensor_tensor(o, M.pair((q0 + m) % 4, 0, SEQ), o, ALU.add).then_inc(evac, 1)
            dve.drain().then_inc(h_ready, 1)
            early_dve(dve, "w_out", m)
        early_dve(dve, "w_out", 8)

    M.n_param_dma = count_param_dmas()
    block = ctx.enter_context(nc.Block())

    @block.sync
    def _(sp):
        prime(sp, [])
        start_sp(sp)
        for name in used_streams:
            if name == "pw1":
                pw1_sp(sp)
            else:
                load_stream(sp, name)
        finish_sp(sp)

    @block.gpsimd
    def _(pool):
        prime(pool, [P_S.sem, lo_ready, zero_ready])
        pool.memset(M.p_rows[:, PT - 1, :], 0.0)
        pool.memset(M.one[:, 0:1], EPS)
        pool.memset(M.one[:, 1:2], GN_EPS)
        pool.memset(M.one[:, 2:8], 0.0)
        pool.drain().then_inc(zero_ready, 1)
        if "pw1" in order:
            pool.wait_ge(start_c, done(3 + KD))
            pool.memset(M.vp[:, :, :], 0.0).then_inc(zero_ready, 1)
        for name in used_streams:
            if name == "w_out":
                V_S.after(pool, "abc2")
                pool.memset(M.m4[:, :, :, :], 0.0).then_inc(zero_ready, 1)
                low_stream(pool, name, 0, 2)
                rw_pool(pool)
                low_stream(pool, name, 2, 8)
                continue
            low_stream(pool, name)

    @block.scalar
    def _(act):
        prime(act, [mod_rows, hi_ready, start_c, sc_ready, sq_ready, rms_ready, y_ready, gate_ready, cv_ready,
                    mid_ready, silu_ready, ghi_ready, f_res, mem_ready, turn_c, att_p, att_c, att_e, otr_h, S_S.sem])
        ada_first_load(act)
        act.wait_ge(zero_ready, done(1))
        start_act(act)
        if q_end:
            high_first(act)
        for st in order:
            if st == "final":
                tables_act(act)
            if st == "mix":
                mem_act(act)
            if st in NN:
                norm_act(act, st)
            if st == "w_in":
                w_in_act(act)
            if st == "mixers":
                mix_prep_act(act)
                att_act(act, units2(), 64)
                mix_out_act(act)
                rw_pre_act(act)
                rw_act(act)
            if st == "w_out":
                plain_high(act, "w_out")
            if st == "pw1":
                pw1_act(act)
                act.wait_ge(mod_ready, done(2))
            if st == "pw2":
                pw2_act(act)
            if st == "qkv":
                qkv_act(act)
            if st == "attn":
                prep_act(act)
                attn_act(act)
            if st == "wo":
                plain_high(act, "wo")
            if st in ("ffn0", "ffn1", "ffn2"):
                b, w = int(st[3]), TOK if st == "ffn0" else SEQ
                for hf in (0, 1):
                    up_act(act, b, hf, w)
                    plain_high(act, f"down{b}{hf}")

    @block.tensor
    def _(pe):
        prime(pe, [mod_t, tile_done, ada_used, start_t, stat_ready, mu_ready, mem_t, out_t, rope_r, turn_t, att_s, att_t, att_o, otr_t, T_S.sem])
        start_pe(pe)
        for st in order:
            if st == "ln":
                mean_pe(pe)
            if st == "mix":
                mem_pe(pe)
            if st in NN:
                norm_pe(pe, st)
            if st == "n10":
                ada_pe(pe)
            if st == "w_in":
                w_in_pe(pe)
            if st == "mixers":
                mix_prep_pe(pe)
                S_S.after(pe, "bias")
                att_pe(pe, units2(), 64)
                mix_out_pe(pe)
                rw_pre_pe(pe)
                rw_pe(pe)
            if st == "w_out":
                V_S.after(pe, "lo3")
                stream_pe(pe, "w_out", lambda it, u: LAT)
            if st == "pw1":
                pw1_pe(pe)
            if st == "pw2":
                stream_pe(pe, "pw2", lambda it, u: BOTH, norm="ln")
            if st == "qkv":
                qkv_pe(pe)
            if st == "attn":
                prep_pe(pe)
                attn_pe(pe)
            if st == "wo":
                pe.wait_ge(xa_ready, done(8))
                stream_pe(pe, "wo", lambda it, u: LAT)
            if st in ("ffn0", "ffn1", "ffn2"):
                b, segs = int(st[3]), BOTH if st == "ffn0" else LAT
                for hf in (0, 1):
                    stream_pe(pe, f"up{b}{hf}", lambda it, u: segs,
                              norm=None if hf else ["n20", "n21", "ffn2_norm"][b])
                    stream_pe(pe, f"down{b}{hf}", lambda it, u: segs, from_g=HALF * (2 * b + hf + 1))
        finish_pe(pe)

    @block.vector
    def _(dve):
        prime(dve, [sq_used, evac, mod_ready, rstd_ready, t_ready, x_ready, h_ready, v_ready, tap_done, cv_cent,
                    taps_ready, prod_ready, g_ready, out_c, rope_c, att_m, att_r, xa_ready, V_S.sem])
        dve.wait_ge(start_c, done(3 + KD))
        dve.drain().then_inc(h_ready, 8)
        for st in order:
            if st == "ln":
                mean_dve(dve)
            if st in NN:
                norm_dve(dve, st)
            if st == "w_in":
                w_in_dve(dve)
            if st == "mixers":
                mix_prep_dve(dve)
                S_S.after(dve, "bias")
                att_dve(dve, units2(), 64)
                mix_out_dve(dve)
                rw_pre_dve(dve)
                rw_dve(dve)
            if st == "w_out":
                w_out_dve(dve)
            if st == "pw1":
                pw1_dve(dve)
                ada_rest_dve(dve)
            if st == "pw2":
                pw2_dve(dve)
            if st == "qkv":
                qkv_dve(dve)
            if st == "attn":
                attn_dve(dve)
            if st == "wo":
                wo_dve(dve)
            if st in ("ffn0", "ffn1", "ffn2"):
                b, w = int(st[3]), TOK if st == "ffn0" else SEQ
                for hf in (0, 1):
                    up_dve(dve, b, hf, w)
                    down_dve(dve, b, hf, w)
        finish_dve(dve)


_INS = ["x", "c", "ctx", "c_ctx", "ada_w", "ada_b", "norm1_g", "norm2_g", "final_g", "conv_w_pw1", "conv_b_pw1",
        "conv_w_dw", "conv_b_dw", "conv_ln_g", "conv_ln_b", "conv_w_pw2", "conv_b_pw2", "attn_w_qkv", "attn_w_o",
        "attn_sink", "ffn_w_up", "ffn_w_dw", "ffn_b_dw", "ffn_w_down", "mem_2", "rel_bias_2", "mix_norm_g_2",
        "w_in_2", "attn_q_norm_2", "attn_k_norm_2", "attn_sinks_2", "rwkv_mu_2", "rwkv_w0_2", "rwkv_w2_2",
        "rwkv_a0_2", "rwkv_a2_2", "rwkv_g2_2", "rwkv_k_k_2", "rwkv_k_a_2", "rwkv_r_k_2", "rwkv_ln_w_2",
        "rwkv_ln_b_2", "mem_norm_g_2", "w_mem_kv_2", "mem_q_norm_2", "mem_k_norm_2", "w_out_2", "ffn_norm_g_2",
        "w_up_2", "conv_w_2", "conv_b_2", "w_down_2"]
_OUT_SHAPE = (1, SEQ, D)


def kernel(**inputs):
    import numpy as _np
    import concourse.bacc as _bacc
    from concourse import mybir as _mybir
    from concourse.bass_utils import run_bass_kernel_spmd as _run

    nc = _bacc.Bacc("TRN2", target_bir_lowering=False, num_devices=1)
    arrays, aps = {}, {}
    given = {name: _np.ascontiguousarray(inputs[name]) for name in _INS}
    for name, a in list(given.items()) + list(constants().items()):
        arrays[f"in_{name}"] = a
        aps[name] = nc.dram_tensor(f"in_{name}", a.shape, _mybir.dt.from_np(a.dtype), kind="ExternalInput").ap()
    out = nc.dram_tensor("out_0", _OUT_SHAPE, F32, kind="ExternalOutput").ap()
    build(nc, aps, out)
    r = _run(nc, [arrays], core_ids=[0])
    return r.results[0]["out_0"]
```
